# Optimizing a Trainium2 kernel written in Bass

```python
import jax, jax.numpy as jnp
from jax import lax
import numpy as np

D_MODEL = 1024
BATCH = 1
SEQ = 1024
DEPTH = 2

GRID_W = 64
CTX_LEN = 256
HEAD_DIM = 64
N_FREQ = HEAD_DIM // 4
RET_HEADS = 4
SWA_Q_HEADS = 8
SWA_KV_HEADS = 2
GDN_HEADS = 4
RET_W = RET_HEADS * HEAD_DIM
SWA_W = SWA_Q_HEADS * HEAD_DIM
SWA_KV_W = SWA_KV_HEADS * HEAD_DIM
GDN_W = GDN_HEADS * HEAD_DIM
MIX_W = RET_W + SWA_W + GDN_W
IN_W = 4 * RET_W + SWA_W + 2 * SWA_KV_W + 4 * GDN_W + 4 * GDN_HEADS
WINDOW = 128
Q_BLOCK = 128
RET_CHUNK = 64
GDN_CHUNK = 64
CONV_W = 3
D_FF = ((8 * D_MODEL + 3 * 256 - 1) // (3 * 256)) * 256
ROPE_BASE = 10000.0
EPS = 1e-6
NEG_INF = -1e30
N_MOD = 6

kernel_name = 'hybrid_parallel_heads_dit_block'

def rmsnorm(x, w):
    xf = x.astype(jnp.float32)
    y = xf * lax.rsqrt(jnp.mean(xf * xf, axis=-1, keepdims=True) + EPS)
    return (y * w.astype(jnp.float32)).astype(x.dtype)

def head_rms(o):
    return o * lax.rsqrt(jnp.mean(o * o, axis=-1, keepdims=True) + EPS)

def l2norm(t):
    return t * lax.rsqrt(jnp.sum(t * t, axis=-1, keepdims=True) + EPS)

def flip(t):
    return jnp.flip(t, axis=2)

def heads(t, h):
    b, l, _ = t.shape
    return t.reshape(b, l, h, HEAD_DIM).transpose(0, 2, 1, 3)

def merge(t):
    b, h, l, d = t.shape
    return t.transpose(0, 2, 1, 3).reshape(b, l, h * d)

def axial_rope(rows):
    row = jnp.repeat(jnp.arange(rows), GRID_W).astype(jnp.float32)
    col = jnp.tile(jnp.arange(GRID_W), rows).astype(jnp.float32)
    freqs = ROPE_BASE ** (-jnp.arange(N_FREQ, dtype=jnp.float32) / N_FREQ)
    ang = jnp.stack([row[:, None] * freqs, col[:, None] * freqs], axis=1)
    return jnp.cos(ang), jnp.sin(ang)

def apply_rope(t, cos, sin):
    tr = t.reshape(*t.shape[:-1], 2, 2, N_FREQ).astype(jnp.float32)
    t1, t2 = tr[..., 0, :], tr[..., 1, :]
    out = jnp.stack([t1 * cos - t2 * sin, t1 * sin + t2 * cos], axis=-2)
    return out.reshape(t.shape).astype(t.dtype)

def split_proj(p):
    sizes = (RET_W, RET_W, RET_W, RET_W,
             SWA_W, SWA_KV_W, SWA_KV_W,
             GDN_W, GDN_W, GDN_W, GDN_W, 2 * GDN_HEADS, 2 * GDN_HEADS)
    out, start = [], 0
    for s in sizes:
        out.append(p[..., start:start + s])
        start += s
    return out

def short_conv(t, w):
    l = t.shape[1]
    pad = CONV_W // 2
    tp = jnp.pad(t, ((0, 0), (pad, pad), (0, 0)))
    return sum(tp[:, j:j + l] * w[j] for j in range(CONV_W))

def retention_chunked(q, k, v, log_gamma, s0):
    b, h, l, dk = q.shape
    dv = v.shape[-1]
    n = l // RET_CHUNK

    def chunks(t):
        return t.reshape(b, h, n, RET_CHUNK, t.shape[-1]).transpose(2, 0, 1, 3, 4)

    qn, kn, vn = chunks(q), chunks(k), chunks(v)
    idx = jnp.arange(RET_CHUNK, dtype=jnp.float32)
    lg = log_gamma.astype(jnp.float32)[:, None]
    diff = idx[:, None] - idx[None, :]
    dmask = jnp.where(diff >= 0, jnp.exp(lg[:, :, None] * jnp.maximum(diff, 0.0)), 0.0)
    q_dec = jnp.exp(lg * (idx + 1.0))[:, :, None]
    k_dec = jnp.exp(lg * (RET_CHUNK - 1.0 - idx))[:, :, None]
    c_dec = jnp.exp(log_gamma.astype(jnp.float32) * RET_CHUNK)[:, None, None]
    intra = jnp.einsum('nbhij,nbhje->nbhie',
                       jnp.einsum('nbhid,nbhjd->nbhij', qn, kn) * dmask, vn)

    def step(s, inp):
        qd, kd, vc = inp
        cross = jnp.einsum('bhid,bhde->bhie', qd, s)
        s = s * c_dec + jnp.einsum('bhjd,bhje->bhde', kd, vc)
        return s, cross

    s_fin, cross = lax.scan(step, s0, (qn * q_dec, kn * k_dec, vn))
    o = (intra + cross).transpose(1, 2, 0, 3, 4).reshape(b, h, l, dv)
    return o, s_fin

def gdn_chunked(q, k, v, g, beta, s0):
    b, h, l, dk = q.shape
    dv = v.shape[-1]
    n = l // GDN_CHUNK

    def chunks(t):
        return t.reshape(b, h, n, GDN_CHUNK, t.shape[-1]).transpose(2, 0, 1, 3, 4)

    qn = chunks(q) * dk ** -0.5
    kn, vn = chunks(k), chunks(v)
    gn = g.reshape(b, h, n, GDN_CHUNK).transpose(2, 0, 1, 3)
    bn = beta.reshape(b, h, n, GDN_CHUNK).transpose(2, 0, 1, 3)
    gc = jnp.cumsum(gn, axis=-1)
    idx = jnp.arange(GDN_CHUNK)
    tri = idx[:, None] >= idx[None, :]
    strict = idx[:, None] > idx[None, :]
    decay = jnp.exp(jnp.where(tri, gc[..., :, None] - gc[..., None, :], -jnp.inf))
    kk = jnp.einsum('nbhid,nbhjd->nbhij', kn, kn)
    m = jnp.where(strict, kk * bn[..., :, None] * decay, 0.0)
    t_mat = m + jnp.eye(GDN_CHUNK, dtype=jnp.float32)
    rhs = jnp.concatenate([vn * bn[..., None], kn * (bn * jnp.exp(gc))[..., None]], axis=-1)
    sol = lax.linalg.triangular_solve(t_mat, rhs, left_side=True, lower=True,
                                      unit_diagonal=True)
    u, w = sol[..., :dv], sol[..., dv:]
    attn = jnp.einsum('nbhid,nbhjd->nbhij', qn, kn) * decay
    q_dec = qn * jnp.exp(gc)[..., None]
    k_tail = kn * jnp.exp(gc[..., -1:] - gc)[..., None]
    g_tot = jnp.exp(gc[..., -1])[..., None, None]

    def step(s, inp):
        u_i, w_i, a_i, qd_i, kt_i, gt_i = inp
        v_new = u_i - jnp.einsum('bhid,bhde->bhie', w_i, s)
        o_i = jnp.einsum('bhid,bhde->bhie', qd_i, s) + jnp.einsum('bhij,bhje->bhie', a_i, v_new)
        s = s * gt_i + jnp.einsum('bhjd,bhje->bhde', kt_i, v_new)
        return s, o_i

    s_fin, o = lax.scan(step, s0, (u, w, attn, q_dec, k_tail, g_tot))
    o = o.transpose(1, 2, 0, 3, 4).reshape(b, h, l, dv)
    return o, s_fin

def swa_latent(q, k, v, k_ctx, v_ctx, sinks):
    b, hq, l, d = q.shape
    g = hq // SWA_KV_HEADS
    lc = k_ctx.shape[2]
    nblk = l // Q_BLOCK
    span = Q_BLOCK + 2 * WINDOW
    qg = q.reshape(b, SWA_KV_HEADS, g, l, d)
    kp = jnp.pad(k, ((0, 0), (0, 0), (WINDOW, WINDOW), (0, 0)))
    vp = jnp.pad(v, ((0, 0), (0, 0), (WINDOW, WINDOW), (0, 0)))
    scale = d ** -0.5
    sink = jnp.broadcast_to(sinks.astype(jnp.float32).reshape(1, SWA_KV_HEADS, g, 1, 1),
                            (b, SWA_KV_HEADS, g, Q_BLOCK, 1))

    def block(i):
        start = i * Q_BLOCK
        qb = lax.dynamic_slice_in_dim(qg, start, Q_BLOCK, axis=3)
        kb = lax.dynamic_slice_in_dim(kp, start, span, axis=2)
        vb = lax.dynamic_slice_in_dim(vp, start, span, axis=2)
        qpos = start + jnp.arange(Q_BLOCK)
        kpos = start - WINDOW + jnp.arange(span)
        valid = ((jnp.abs(qpos[:, None] - kpos[None, :]) <= WINDOW)
                 & (kpos >= 0)[None, :] & (kpos < l)[None, :])
        s_loc = jnp.einsum('bkgqd,bkjd->bkgqj', qb, kb).astype(jnp.float32) * scale
        s_loc = jnp.where(valid, s_loc, NEG_INF)
        s_ctx = jnp.einsum('bkgqd,bkjd->bkgqj', qb, k_ctx).astype(jnp.float32) * scale
        p = jax.nn.softmax(jnp.concatenate([s_loc, s_ctx, sink], axis=-1), axis=-1)
        p_loc = p[..., :span].astype(v.dtype)
        p_ctx = p[..., span:span + lc].astype(v.dtype)
        return (jnp.einsum('bkgqj,bkjd->bkgqd', p_loc, vb)
                + jnp.einsum('bkgqj,bkjd->bkgqd', p_ctx, v_ctx))

    out = lax.map(block, jnp.arange(nblk))
    return out.transpose(1, 2, 3, 0, 4, 5).reshape(b, hq, l, d)

def swa_context(q, k, v, sinks):
    b, hq, lc, d = q.shape
    g = hq // SWA_KV_HEADS
    qg = q.reshape(b, SWA_KV_HEADS, g, lc, d)
    s = jnp.einsum('bkgqd,bkjd->bkgqj', qg, k).astype(jnp.float32) * d ** -0.5
    sink = jnp.broadcast_to(sinks.astype(jnp.float32).reshape(1, SWA_KV_HEADS, g, 1, 1),
                            (b, SWA_KV_HEADS, g, lc, 1))
    p = jax.nn.softmax(jnp.concatenate([s, sink], axis=-1), axis=-1)[..., :lc].astype(v.dtype)
    return jnp.einsum('bkgqj,bkjd->bkgqd', p, v).reshape(b, hq, lc, d)

def retention_group(pc, pl, cos, sin, ret_rate, norm_w, need_ctx):
    log_gamma = jnp.log1p(-jnp.exp2(-ret_rate.astype(jnp.float32)))

    def prep(q, k, v, rope):
        q, k, v = (heads(t.astype(jnp.float32), RET_HEADS) for t in (q, k, v))
        if rope:
            q, k = apply_rope(q, cos, sin), apply_rope(k, cos, sin)
        return q, k * HEAD_DIM ** -0.5, v

    qc, kc, vc = prep(pc[0], pc[1], pc[2], False)
    ql, kl, vl = prep(pl[0], pl[1], pl[2], True)
    s0 = jnp.zeros((qc.shape[0], RET_HEADS, HEAD_DIM, HEAD_DIM), jnp.float32)
    oc_f, s_f = retention_chunked(qc, kc, vc, log_gamma[0], s0)
    oc_b, s_b = retention_chunked(flip(qc), flip(kc), flip(vc), log_gamma[1], s0)
    ol_f, _ = retention_chunked(ql, kl, vl, log_gamma[0], s_f)
    ol_b, _ = retention_chunked(flip(ql), flip(kl), flip(vl), log_gamma[1], s_b)

    def out(o, gate):
        y = merge(head_rms(o)) * norm_w.astype(jnp.float32) * jax.nn.silu(gate.astype(jnp.float32))
        return y.astype(gate.dtype)

    y_l = out(ol_f + flip(ol_b), pl[3])
    y_c = out(oc_f + flip(oc_b), pc[3]) if need_ctx else None
    return y_l, y_c

def swa_group(pc, pl, cos, sin, sinks, need_ctx):
    qc, kc, vc = heads(pc[0], SWA_Q_HEADS), heads(pc[1], SWA_KV_HEADS), heads(pc[2], SWA_KV_HEADS)
    ql = apply_rope(heads(pl[0], SWA_Q_HEADS), cos, sin)
    kl = apply_rope(heads(pl[1], SWA_KV_HEADS), cos, sin)
    vl = heads(pl[2], SWA_KV_HEADS)
    y_l = merge(swa_latent(ql, kl, vl, kc, vc, sinks))
    y_c = merge(swa_context(qc, kc, vc, sinks)) if need_ctx else None
    return y_l, y_c

def gdn_group(pc, pl, conv_w, a_log, dt_bias, norm_w, need_ctx):
    a_rate = jnp.exp(a_log.astype(jnp.float32))
    dtb = dt_bias.astype(jnp.float32)

    def prep(q, k, v, a, bg):
        b, l, _ = q.shape
        qkv = jax.nn.silu(short_conv(jnp.concatenate([q, k, v], axis=-1).astype(jnp.float32),
                                     conv_w.astype(jnp.float32)))
        q, k, v = (heads(qkv[..., i * GDN_W:(i + 1) * GDN_W], GDN_HEADS) for i in range(3))
        a = a.astype(jnp.float32).reshape(b, l, 2, GDN_HEADS)
        bg = bg.astype(jnp.float32).reshape(b, l, 2, GDN_HEADS)
        g = (-a_rate * jax.nn.softplus(a + dtb)).transpose(2, 0, 3, 1)
        beta = jax.nn.sigmoid(bg).transpose(2, 0, 3, 1)
        return l2norm(q), l2norm(k), v, g, beta

    qc, kc, vc, gcx, bc = prep(pc[0], pc[1], pc[2], pc[4], pc[5])
    ql, kl, vl, glt, bl = prep(pl[0], pl[1], pl[2], pl[4], pl[5])
    s0 = jnp.zeros((qc.shape[0], GDN_HEADS, HEAD_DIM, HEAD_DIM), jnp.float32)
    oc_f, s_f = gdn_chunked(qc, kc, vc, gcx[0], bc[0], s0)
    oc_b, s_b = gdn_chunked(flip(qc), flip(kc), flip(vc), flip(gcx[1]), flip(bc[1]), s0)
    ol_f, _ = gdn_chunked(ql, kl, vl, glt[0], bl[0], s_f)
    ol_b, _ = gdn_chunked(flip(ql), flip(kl), flip(vl), flip(glt[1]), flip(bl[1]), s_b)

    def out(o, z):
        y = merge(head_rms(o) * norm_w.astype(jnp.float32)) * jax.nn.silu(z.astype(jnp.float32))
        return y.astype(z.dtype)

    y_l = out(ol_f + flip(ol_b), pl[3])
    y_c = out(oc_f + flip(oc_b), pc[3]) if need_ctx else None
    return y_l, y_c

def mixer(hc, hl, cos, sin, w_in, ret_rate, ret_norm_w, sinks, conv_w, a_log, dt_bias,
          gdn_norm_w, w_out, need_ctx):
    pl = split_proj(hl @ w_in)
    pc = split_proj(hc @ w_in)
    r_l, r_c = retention_group(pc[0:4], pl[0:4], cos, sin, ret_rate, ret_norm_w, need_ctx)
    s_l, s_c = swa_group(pc[4:7], pl[4:7], cos, sin, sinks, need_ctx)
    g_l, g_c = gdn_group(pc[7:13], pl[7:13], conv_w, a_log, dt_bias, gdn_norm_w, need_ctx)
    y_l = jnp.concatenate([r_l, s_l, g_l], axis=-1) @ w_out
    y_c = jnp.concatenate([r_c, s_c, g_c], axis=-1) @ w_out if need_ctx else None
    return y_l, y_c

def swiglu(h, w1, w2):
    gu = h @ w1
    return (jax.nn.silu(gu[..., :D_FF]) * gu[..., D_FF:]) @ w2

def setup_inputs(seed: int = 0) -> dict:
    key = jax.random.key(seed)
    ks = jax.random.split(key, 20)

    def nrm(k, shape, scale):
        return jax.random.normal(k, shape, jnp.float32) * scale

    dt = jnp.exp(jax.random.uniform(ks[15], (DEPTH, 2, GDN_HEADS), jnp.float32,
                                    minval=np.log(1e-3), maxval=np.log(1e-1)))
    return {
        'x': nrm(ks[0], (BATCH, SEQ, D_MODEL), 1.0),
        'c': nrm(ks[1], (BATCH, D_MODEL), 1.0),
        'ctx': nrm(ks[2], (BATCH, CTX_LEN, D_MODEL), 1.0),
        'c_ctx': nrm(ks[3], (D_MODEL,), 1.0),
        'ada_w': nrm(ks[4], (DEPTH, D_MODEL, N_MOD * D_MODEL), 0.5 * D_MODEL ** -0.5),
        'ada_b': nrm(ks[5], (DEPTH, N_MOD * D_MODEL), 0.02),
        'norm_mix_w': 1.0 + nrm(ks[6], (DEPTH, D_MODEL), 0.02),
        'norm_ffn_w': 1.0 + nrm(ks[7], (DEPTH, D_MODEL), 0.02),
        'w_in': nrm(ks[8], (DEPTH, D_MODEL, IN_W), D_MODEL ** -0.5),
        'ret_rate': 5.0 + jnp.arange(RET_HEADS, dtype=jnp.float32) + nrm(ks[9], (DEPTH, 2, RET_HEADS), 0.1),
        'ret_norm_w': 1.0 + nrm(ks[10], (DEPTH, RET_W), 0.02),
        'swa_sinks': nrm(ks[11], (DEPTH, SWA_Q_HEADS), 1.0),
        'gdn_conv_w': nrm(ks[12], (DEPTH, CONV_W, 3 * GDN_W), CONV_W ** -0.5),
        'gdn_a_log': jnp.log(jax.random.uniform(ks[13], (DEPTH, 2, GDN_HEADS), jnp.float32,
                                                minval=1.0, maxval=16.0)),
        'gdn_dt_bias': dt + jnp.log(-jnp.expm1(-dt)),
        'gdn_norm_w': 1.0 + nrm(ks[14], (DEPTH, HEAD_DIM), 0.02),
        'w_out': nrm(ks[16], (DEPTH, MIX_W, D_MODEL), MIX_W ** -0.5),
        'w_ffn_in': nrm(ks[17], (DEPTH, D_MODEL, 2 * D_FF), D_MODEL ** -0.5),
        'w_ffn_out': nrm(ks[18], (DEPTH, D_FF, D_MODEL), D_FF ** -0.5),
        'final_norm_w': 1.0 + nrm(ks[19], (D_MODEL,), 0.02),
    }

def reference(x, c, ctx, c_ctx, ada_w, ada_b, norm_mix_w, norm_ffn_w, w_in, ret_rate,
              ret_norm_w, swa_sinks, gdn_conv_w, gdn_a_log, gdn_dt_bias, gdn_norm_w, w_out,
              w_ffn_in, w_ffn_out, final_norm_w):
    l = x.shape[1]
    rows = l // GRID_W
    cos, sin = axial_rope(rows)
    c_s = jax.nn.silu(c)
    cc_s = jax.nn.silu(c_ctx)
    xc = ctx
    for layer in range(DEPTH):
        need_ctx = layer < DEPTH - 1
        mod = (c_s @ ada_w[layer] + ada_b[layer])[:, None, :]
        sh1, sc1, g1, sh2, sc2, g2 = jnp.split(mod, N_MOD, axis=-1)
        modc = cc_s @ ada_w[layer] + ada_b[layer]
        shc1, scc1, gc1, shc2, scc2, gc2 = jnp.split(modc, N_MOD, axis=-1)
        hl = rmsnorm(x, norm_mix_w[layer]) * (1.0 + sc1) + sh1
        hc = rmsnorm(xc, norm_mix_w[layer]) * (1.0 + scc1) + shc1
        y_l, y_c = mixer(hc, hl, cos, sin, w_in[layer], ret_rate[layer], ret_norm_w[layer],
                         swa_sinks[layer], gdn_conv_w[layer], gdn_a_log[layer],
                         gdn_dt_bias[layer], gdn_norm_w[layer], w_out[layer], need_ctx)
        x = x + g1 * y_l
        x = x + g2 * swiglu(rmsnorm(x, norm_ffn_w[layer]) * (1.0 + sc2) + sh2,
                            w_ffn_in[layer], w_ffn_out[layer])
        if need_ctx:
            xc = xc + gc1 * y_c
            xc = xc + gc2 * swiglu(rmsnorm(xc, norm_ffn_w[layer]) * (1.0 + scc2) + shc2,
                                   w_ffn_in[layer], w_ffn_out[layer])
    return rmsnorm(x, final_norm_w)


_drawn_inputs = setup_inputs


def setup_inputs(seed=0):
    import zlib

    import numpy as np

    out = dict(_drawn_inputs(seed))
    spreads = {}
    factors = {'norm_mix_w': 7.427,
     'norm_ffn_w': 6.519,
     'ret_norm_w': 8.0,
     'swa_sinks': 8.0,
     'gdn_norm_w': 8.0,
     'final_norm_w': 2.833}
    for name, (base, spread) in spreads.items():
        noise = np.random.default_rng([zlib.crc32(name.encode()), seed]).standard_normal(out[name].shape)
        drawn = base * np.exp(spread * noise) if base else spread * noise
        out[name] = __import__('jax').numpy.asarray(drawn.astype(out[name].dtype))
    for name, factor in factors.items():
        out[name] = (out[name] * factor).astype(out[name].dtype)
    return out
```

```python
from contextlib import ExitStack

import numpy as np

import concourse.bass as bass
from concourse import mybir

ALU = mybir.AluOpType
ACT = mybir.ActivationFunctionType
AX = mybir.AxisListType
F32 = mybir.dt.float32
F32R = mybir.dt.float32r

P = 128
DM = 1024
KC = DM // P
CTX, LAT = 256, 1024
TOK = CTX + LAT
TILES = TOK // P
DEPTH = 2
HD = 64
RH, SH, GH = 4, 8, 4
IN_W = 2832
GROUPS, GW = 6, IN_W // 6
DFF = 2816
FC = DFF // P
NMOD = 6
EPS = 1e-6
NEG = -1e30

R_Q, R_K, R_V, R_G = 0, 256, 512, 768
S_Q, S_K, S_V = 1024, 1536, 1664
G_Q, G_K, G_V, G_Z, G_A, G_B = 1792, 2048, 2304, 2560, 2816, 2824
R0 = P
ROWS = R0 + TOK + 3 + P


def row_of(t):
    return R0 + 1 + t * P + (t >= 2)



def token_slices(lo):
    full = [(0, 256), (256, 512), (768, 512)]
    return full if lo == 0 else full[1:]


class Stage:

    def __init__(self, nc, name):
        self.nc, self.name, self.sems = nc, name, []

    def __enter__(self):
        self.mem = ExitStack()
        return self

    def sb(self, name, shape, dt=F32):
        return self.mem.enter_context(self.nc.sbuf_tensor(f"{self.name}_{name}", shape, dt))

    def ps(self, name, shape, dt=F32):
        return self.mem.enter_context(self.nc.psum_tensor(f"{self.name}_{name}", shape, dt))

    def sem(self, name):
        s = self.mem.enter_context(self.nc.semaphore(f"{self.name}_{name}"))
        self.sems.append(s)
        return s

    def __exit__(self, *a):
        if a[0] is None:
            self.nc.clear_and_free_semaphores(self.sems)
            self.nc.all_engine_barrier()
        self.mem.close()


def modulation(nc, layer, cs, ada_w, ada_b, norm_mix, norm_ffn, ident, mod, amix, affn):
    NG = NMOD * DM // 512
    with Stage(nc, f"ada{layer}") as st:
        c_in = st.sb("c_in", [P, KC, 2])
        c_s = st.sb("c_s", [P, KC, 2])
        w = [st.sb(f"w{u}", [P, KC, 512]) for u in range(2)]
        rows = st.sb("rows", [2, NMOD * DM])
        bias = st.sb("bias", [2, NMOD * DM])
        nw = st.sb("nw", [P, 2, KC])
        acc = [st.ps(f"acc{u}", [2, 512]) for u in range(2)]
        cols = st.ps("cols", [P, NMOD * KC * 2])
        small_in, w_in0, w_in1 = st.sem("small_in"), st.sem("w_in0"), st.sem("w_in1")
        silu_done, turned = st.sem("silu_done"), st.sem("turned")
        acc_done = [st.sem(f"acc_done{u}") for u in range(2)]
        row_done = [st.sem(f"row_done{u}") for u in range(2)]
        mod_done, plus_one, scale_done = st.sem("mod_done"), st.sem("plus_one"), st.sem("scale_done")
        w_in = [w_in0, w_in1]
        with nc.Block() as block:
            @block.sync
            def _(sp):
                sp.dma_start(c_in[:], cs).then_inc(small_in, 16)
                sp.dma_start(bias[:], ada_b[layer]).then_inc(small_in, 16)
                sp.dma_start(nw[:, 0, :], norm_mix[layer]).then_inc(small_in, 16)
                sp.dma_start(nw[:, 1, :], norm_ffn[layer]).then_inc(small_in, 16)
                with sp.Fori(0, NG // 2) as g:
                    for u in range(2):
                        sp.wait_ge(acc_done[u], g)
                        src = ada_w[layer].rearrange("(k p) n -> p k n", p=P)
                        sp.dma_start(w[u][:], src[:, :, bass.ds(g * 1024 + u * 512, 512)]).then_inc(w_in[u], 16)

            @block.scalar
            def _(act):
                act.wait_ge(small_in, 64)
                act.activation(c_s[:], c_in[:], ACT.Silu).then_inc(silu_done, 1)

            @block.tensor
            def _(pe):
                pe.wait_ge(silu_done, 1)
                with pe.Fori(0, NG // 2) as g:
                    for u in range(2):
                        pe.wait_ge(w_in[u], g * 16 + 16)
                        pe.wait_ge(row_done[u], g)
                        for k in range(KC):
                            mm = pe.matmul(acc[u][:], c_s[:, k, :], w[u][:, k, :], start=(k == 0), stop=(k == KC - 1))
                        mm.then_inc(acc_done[u], 1)
                for u in range(2):
                    pe.wait_ge(row_done[u], NG // 2)
                for m in range(NMOD * KC):
                    mm = pe.transpose(cols[:, 2 * m:2 * m + 2], rows[:, m * P:(m + 1) * P], ident[0:2, 0:2])
                mm.then_inc(turned, 1)

            @block.vector
            def _(dve):
                dve.wait_ge(small_in, 64)
                with dve.Fori(0, NG // 2) as g:
                    for u in range(2):
                        dve.wait_ge(acc_done[u], g + 1)
                        at = bass.ds(g * 1024 + u * 512, 512)
                        dve.tensor_tensor(rows[:, at], acc[u][:], bias[:, at], ALU.add).then_inc(row_done[u], 1)
                dve.wait_ge(turned, 1)
                dve.tensor_copy(mod[:].rearrange("p m v -> p (m v)"), cols[:]).then_inc(mod_done, 1)
                dve.wait_ge(mod_done, 1)
                for which, out in ((0, amix), (1, affn)):
                    sc = mod[:, (3 * which + 1) * KC:(3 * which + 2) * KC, :]
                    dve.tensor_scalar(out[:], sc, 1.0, None, ALU.add).then_inc(plus_one, 1)
                    dve.wait_ge(plus_one, which + 1)
                    dve.tensor_tensor(out[:], out[:], nw[:, which, :].unsqueeze(2).broadcast_to([P, KC, 2]), ALU.mult).then_inc(scale_done, 1)
                dve.wait_ge(scale_done, 2)


def normed(nc, st, x, scale, mod, shift0, lo, hi_t, lo_t, ones, eps):
    slices = token_slices(lo)
    sq = [st.sb(f"sq{u}", [P, 512]) for u in range(2)]
    root = st.sb("root", [P, 512])
    inv = [st.sb(f"inv{u}", [P, 512]) for u in range(2)]
    scaled = [st.sb(f"scaled{u}", [P, 512]) for u in range(2)]
    full = [st.sb(f"full{u}", [P, 512]) for u in range(2)]
    ms = st.ps("ms", [P, 512])
    squared, summed, rooted, inverted = st.sem("squared"), st.sem("summed"), st.sem("rooted"), st.sem("inverted")
    scaled_s, shifted, rounded, h_ready = st.sem("scaled"), st.sem("shifted"), st.sem("rounded"), st.sem("h_ready")

    def act_norm(act):
        for s, (t0, n) in enumerate(slices):
            v = 1 if t0 < CTX else 0
            for k in range(KC):
                i = s * KC + k
                if i >= 2:
                    act.wait_ge(summed, i - 1)
                act.activation(sq[i % 2][:, 0:n], x[:, k, t0:t0 + n], ACT.Square).then_inc(squared, 1)
            act.wait_ge(summed, (s + 1) * KC)
            if s >= 1:
                act.wait_ge(inverted, s)
            act.activation(root[:, 0:n], ms[:, 0:n], ACT.Sqrt, bias=eps[:]).then_inc(rooted, 1)
            for k in range(KC):
                i = s * KC + k
                act.wait_ge(scaled_s, i + 1)
                if i >= 2:
                    act.wait_ge(h_ready, i - 1)
                act.activation(full[i % 2][:, 0:n], scaled[i % 2][:, 0:n], ACT.Identity,
                               bias=mod[:, shift0 + k, v:v + 1], scale=scale[:, k, v:v + 1]).then_inc(shifted, 1)
                act.wait_ge(shifted, i + 1)
                act.activation(hi_t[:, k, t0:t0 + n], full[i % 2][:, 0:n], ACT.Copy).then_inc(rounded, 1)

    def pe_norm(pe):
        for s, (t0, n) in enumerate(slices):
            if s >= 1:
                pe.wait_ge(rooted, s)
            for k in range(KC):
                pe.wait_ge(squared, s * KC + k + 1)
                pe.matmul(ms[:, 0:n], ones[:], sq[(s * KC + k) % 2][:, 0:n], start=(k == 0), stop=(k == KC - 1)).then_inc(summed, 1)

    def dve_norm(dve):
        for s, (t0, n) in enumerate(slices):
            dve.wait_ge(rooted, s + 1)
            dve.reciprocal(inv[s % 2][:, 0:n], root[:, 0:n]).then_inc(inverted, 1)
            dve.wait_ge(inverted, s + 1)

            def scale_one(k):
                i = s * KC + k
                if i >= 2:
                    dve.wait_ge(shifted, i - 1)
                dve.tensor_tensor(scaled[i % 2][:, 0:n], x[:, k, t0:t0 + n], inv[s % 2][:, 0:n], ALU.mult).then_inc(scaled_s, 1)

            scale_one(0)
            for k in range(KC):
                i = s * KC + k
                if k + 1 < KC:
                    scale_one(k + 1)
                dve.wait_ge(rounded, i + 1)
                dve.tensor_tensor(lo_t[:, k, t0:t0 + n], full[i % 2][:, 0:n], hi_t[:, k, t0:t0 + n].bitcast(F32),
                                  ALU.subtract).then_inc(h_ready, 1)

    return act_norm, pe_norm, dve_norm, h_ready, len(slices) * KC


def project(nc, layer, x, w_in, proj, mod, amix, ones, eps):
    with Stage(nc, f"prj{layer}") as st:
        h_hi = st.sb("h_hi", [P, KC, TOK], F32R)
        h_lo = st.sb("h_lo", [P, KC, TOK], F32R)
        act_norm, pe_norm, dve_norm, h_ready, parts = normed(nc, st, x, amix, mod, 0, 0, h_hi, h_lo, ones, eps)
        raw = st.sb("raw", [P, KC, GW])
        w_hi = st.sb("w_hi", [P, KC, GW], F32R)
        w_lo = st.sb("w_lo", [P, KC, GW], F32R)
        out = st.sb("out", [P, 5, GW])
        acc = [st.ps(f"acc{b}", [P, 512]) for b in range(5)]
        w_landed = [st.sem(f"w_landed{k}") for k in range(KC)]
        w_rounded, w_split, w_used = st.sem("w_rounded"), st.sem("w_split"), st.sem("w_used")
        summed = st.sem("psum_done")
        copied = [st.sem(f"copied{b}") for b in range(5)]
        stored = [st.sem(f"stored{b}") for b in range(5)]
        src = w_in[layer].rearrange("(k p) n -> p k n", p=P)
        with nc.Block() as block:
            @block.sync
            def _(sp):
                with sp.Fori(0, GROUPS) as g:
                    for k in range(KC):
                        sp.wait_ge(w_split, g * KC)
                        sp.dma_start(raw[:, k, :], src[:, k, bass.ds(g * GW, GW)]).then_inc(w_landed[k], 16)

            def split_hi(act, g):
                for k in range(KC):
                    act.wait_ge(w_landed[k], g * 16 + 16)
                    if k < KC - 1:
                        act.wait_ge(w_used, g * (KC - 1) + k + 1)
                    else:
                        act.wait_ge(summed, g * TILES)
                    act.activation(w_hi[:, k, :], raw[:, k, :], ACT.Copy).then_inc(w_rounded, 1)

            def split_lo(dve, g):
                for k in range(KC):
                    dve.wait_ge(w_rounded, g * KC + k + 1)
                    dve.tensor_tensor(w_lo[:, k, :], raw[:, k, :], w_hi[:, k, :].bitcast(F32), ALU.subtract).then_inc(w_split, 1)

            @block.scalar
            def _(act):
                act_norm(act)
                with act.Fori(0, GROUPS) as g:
                    split_hi(act, g)
                    for t in range(0, TILES, 2):
                        act.wait_ge(summed, g * TILES + t + 1)
                        act.wait_ge(stored[t % 5], (g * 2 + t // 5) * 16)
                        act.activation(out[:, t % 5, :], acc[t % 5][:, 0:GW], ACT.Copy).then_inc(copied[t % 5], 1)

            @block.vector
            def _(dve):
                dve_norm(dve)
                with dve.Fori(0, GROUPS) as g:
                    split_lo(dve, g)
                    for t in range(1, TILES, 2):
                        dve.wait_ge(summed, g * TILES + t + 1)
                        dve.wait_ge(stored[t % 5], (g * 2 + t // 5) * 16)
                        dve.tensor_copy(out[:, t % 5, :], acc[t % 5][:, 0:GW]).then_inc(copied[t % 5], 1)

            @block.tensor
            def _(pe):
                pe_norm(pe)
                pe.wait_ge(h_ready, parts)
                pe.sem_inc(w_used, KC - 1)
                with pe.Fori(0, GROUPS) as g:
                    for t in range(TILES):
                        tok = slice(t * P, (t + 1) * P)
                        pe.wait_ge(copied[t % 5], g * 2 + t // 5)
                        for k in range(KC):
                            if t == 0:
                                pe.wait_ge(w_split, g * KC + k + 1)
                            for a, b, s in ((h_hi, w_hi, 0), (h_lo, w_hi, 1), (h_hi, w_lo, 2)):
                                mm = pe.matmul(acc[t % 5][:, 0:GW], a[:, k, tok], b[:, k, :],
                                               start=(k == 0 and s == 0), stop=(k == KC - 1 and s == 2))
                            if t == TILES - 1 and k < KC - 1:
                                mm.then_inc(w_used, 1)
                        mm.then_inc(summed, 1)

            @block.gpsimd
            def _(pool):
                with pool.Fori(0, GROUPS) as g:
                    for t in range(TILES):
                        pool.wait_ge(copied[t % 5], g * 2 + t // 5 + 1)
                        row = row_of(t)
                        pool.dma_start(proj[row:row + P, bass.ds(g * GW, GW)], out[:, t % 5, :]).then_inc(stored[t % 5], 16)
                for b in range(5):
                    pool.wait_ge(stored[b], GROUPS * 2 * 16)


class WeightUnits:

    def __init__(self, st, units):
        self.units = units
        self.raw = [st.sb(f"raw{u}", [P, DM]) for u in range(2)]
        self.hi = [st.sb(f"w_hi{u}", [P, DM], F32R) for u in range(2)]
        self.lo = [st.sb(f"w_lo{u}", [P, DM], F32R) for u in range(2)]
        self.landed = [st.sem(f"w_landed{u}") for u in range(2)]
        self.rounded = [st.sem(f"w_rounded{u}") for u in range(2)]
        self.ready = [st.sem(f"w_ready{u}") for u in range(2)]
        self.used = [st.sem(f"w_used{u}") for u in range(2)]

    def load_all(self, sp, turns):
        with sp.Fori(0, turns) as n:
            for u in range(2):
                sp.wait_ge(self.ready[u], n)
                sp.dma_start(self.raw[u][:], self.units[bass.ds(n * 2 + u, 1)].rearrange("a p n -> (a p) n")).then_inc(self.landed[u], 16)

    def round(self, act, u, n):
        act.wait_ge(self.landed[u], n * 16 + 16)
        act.wait_ge(self.used[u], n)
        act.activation(self.hi[u][:], self.raw[u][:], ACT.Copy).then_inc(self.rounded[u], 1)

    def rest(self, dve, u, n):
        dve.wait_ge(self.rounded[u], n + 1)
        dve.tensor_tensor(self.lo[u][:], self.raw[u][:], self.hi[u][:].bitcast(F32), ALU.subtract).then_inc(self.ready[u], 1)


def three_passes(pe, out, w_hi, w_lo, b_hi, b_lo, first, last):
    pe.matmul(out, w_hi, b_hi, start=first, stop=False)
    pe.matmul(out, w_hi, b_lo, start=False, stop=False)
    return pe.matmul(out, w_lo, b_hi, start=False, stop=last)


def ffn(nc, layer, x, lo, units, mod, affn, ones, eps):
    J = 4
    NFULL, REST = FC // J, FC % J
    TURNS = 6
    SETS = 8
    LAST, LSET = NFULL * TURNS, NFULL * SETS
    slices = token_slices(lo)
    with Stage(nc, f"ffn{layer}") as st:
        h_hi = st.sb("h_hi", [P, KC, TOK], F32R)
        h_lo = st.sb("h_lo", [P, KC, TOK], F32R)
        with Stage(nc, f"ffn{layer}n") as sn:
            act_norm, pe_norm, dve_norm, h_ready, parts = normed(nc, sn, x, affn, mod, 3 * KC, lo, h_hi, h_lo, ones, eps)
            with nc.Block() as block:
                block.scalar(act_norm)
                block.tensor(pe_norm)
                block.vector(dve_norm)
        a_hi = st.sb("a_hi", [P, J, TOK], F32R)
        a_lo = st.sb("a_lo", [P, J, TOK], F32R)
        sil = st.sb("sil", [P, TOK])
        prod = st.sb("prod", [P, TOK])
        bank = [[st.ps(f"bank{i}{s}", [P, 512]) for s in range(len(slices))] for i in range(2)]
        w = WeightUnits(st, units)
        full = [[st.sem(f"full{i}{s}") for s in range(len(slices))] for i in range(2)]
        free = [[st.sem(f"free{i}{s}") for s in range(len(slices))] for i in range(2)]
        a_rounded, a_ready = st.sem("a_rounded"), st.sem("a_ready")
        NS = len(slices)

        def pe_up(pe, n, b):
            for u in range(2):
                pe.wait_ge(w.ready[u], n + 1)
                for s, (t0, ln) in enumerate(slices):
                    pe.wait_ge(free[u][s], b)
                    for k in range(KC):
                        f = slice(k * P, (k + 1) * P)
                        mm = three_passes(pe, bank[u][s][:, 0:ln], w.hi[u][:, f], w.lo[u][:, f],
                                          h_hi[:, k, t0:t0 + ln], h_lo[:, k, t0:t0 + ln], k == 0, k == KC - 1)
                    mm.then_inc(full[u][s], 1)
                pe.wait_ge(full[u][NS - 1], b + 1)
                pe.sem_inc(w.used[u], 1)

        def act_up(act, j, c, n, b, before):
            for s, (t0, ln) in enumerate(slices):
                act.wait_ge(full[0][s], b + 1)
                act.wait_ge(free[1][s], b)
                act.activation(sil[:, t0:t0 + ln], bank[0][s][:, 0:ln], ACT.Silu).then_inc(free[0][s], 1)
            w.round(act, 0, n + 1)
            act.wait_ge(w.used[1], before)
            for s, (t0, ln) in enumerate(slices):
                act.wait_ge(free[1][s], b + 1)
                act.activation(a_hi[:, j, t0:t0 + ln], prod[:, t0:t0 + ln], ACT.Copy).then_inc(a_rounded, 1)
            w.round(act, 1, n + 1)

        def dve_up(dve, j, c, n, b):
            w.rest(dve, 0, n + 1)

            def rest(s):
                t0, ln = slices[s]
                dve.wait_ge(a_rounded, c * NS + s + 1)
                dve.tensor_tensor(a_lo[:, j, t0:t0 + ln], prod[:, t0:t0 + ln], a_hi[:, j, t0:t0 + ln].bitcast(F32),
                                  ALU.subtract).then_inc(a_ready, 1)

            for s, (t0, ln) in enumerate(slices):
                dve.wait_ge(a_ready, c * NS)
                dve.wait_ge(full[1][s], b + 1)
                dve.wait_ge(free[0][s], b + 1)
                dve.tensor_tensor(prod[:, t0:t0 + ln], sil[:, t0:t0 + ln], bank[1][s][:, 0:ln], ALU.mult).then_inc(free[1][s], 1)
                if s >= 1:
                    rest(s - 1)
            rest(NS - 1)
            w.rest(dve, 1, n + 1)

        def pe_down(pe, n, b, js, each):
            for u in range(2):
                pe.wait_ge(w.ready[u], n + 1)
                wide = each * P
                for e in range(each):
                    i, use = e % 2, b + u * (each // 2) + e // 2
                    for s, (t0, ln) in enumerate(slices):
                        pe.wait_ge(free[i][s], use)
                        for j in range(js):
                            f = slice(j * wide + e * P, j * wide + (e + 1) * P)
                            mm = three_passes(pe, bank[i][s][:, 0:ln], w.hi[u][:, f], w.lo[u][:, f],
                                              a_hi[:, j, t0:t0 + ln], a_lo[:, j, t0:t0 + ln], j == 0, j == js - 1)
                        mm.then_inc(full[i][s], 1)
                pe.wait_ge(full[1][NS - 1], b + (u + 1) * (each // 2))
                pe.sem_inc(w.used[u], 1)

        def dve_down(dve, n, b, m0, each, more):
            for u in range(2):
                for e in range(each):
                    i, use = e % 2, b + u * (each // 2) + e // 2
                    m = m0 + (u * each + e)
                    for s, (t0, ln) in enumerate(slices):
                        v = 1 if t0 < CTX else 0
                        dve.wait_ge(full[i][s], use + 1)
                        xs = x[:, bass.ds(m, 1), t0:t0 + ln].rearrange("p a n -> p (a n)")
                        dve.scalar_tensor_tensor(xs, bank[i][s][:, 0:ln], mod[:, bass.ds(m + 5 * KC, 1), v], xs,
                                                 ALU.mult, ALU.add).then_inc(free[i][s], 1)
                if more:
                    w.rest(dve, u, n + 1)

        def act_down(act, n, more):
            if more:
                for u in range(2):
                    w.round(act, u, n + 1)

        with nc.Block() as block:
            @block.sync
            def _(sp):
                w.load_all(sp, LAST + REST + 1)

            @block.scalar
            def _(act):
                for u in range(2):
                    w.round(act, u, 0)
                with act.Fori(0, NFULL) as g:
                    with act.Fori(0, J) as j:
                        act_up(act, bass.ds(j, 1), g * J + j, g * TURNS + j, g * SETS + j, g * TURNS)
                    with act.Fori(0, 2) as q:
                        act_down(act, g * TURNS + J + q, True)
                for j in range(REST):
                    act_up(act, bass.ds(j, 1), NFULL * J + j, LAST + j, LSET + j, LAST)

            @block.vector
            def _(dve):
                for u in range(2):
                    w.rest(dve, u, 0)
                with dve.Fori(0, NFULL) as g:
                    with dve.Fori(0, J) as j:
                        dve_up(dve, bass.ds(j, 1), g * J + j, g * TURNS + j, g * SETS + j)
                    with dve.Fori(0, 2) as q:
                        dve_down(dve, g * TURNS + J + q, g * SETS + J + q * 2, q * 4, 2, True)
                for j in range(REST):
                    dve_up(dve, bass.ds(j, 1), NFULL * J + j, LAST + j, LSET + j)
                dve_down(dve, LAST + REST, LSET + REST, 0, 4, False)

            @block.tensor
            def _(pe):
                with pe.Fori(0, NFULL) as g:
                    with pe.Fori(0, J) as j:
                        pe_up(pe, g * TURNS + j, g * SETS + j)
                    with pe.Fori(0, 2) as q:
                        pe.wait_ge(a_ready, (g + 1) * (J * NS))
                        pe_down(pe, g * TURNS + J + q, g * SETS + J + q * 2, J, 2)
                for j in range(REST):
                    pe_up(pe, LAST + j, LSET + j)
                pe.wait_ge(a_ready, FC * NS)
                pe_down(pe, LAST + REST, LSET + REST, REST, 4)


T_RK, T_KT, T_NK, T_LT, T_AT, T_GV = 0, 512, 1024, 1536, 2048, 2560
T_W = 2816
F_RQ, F_RQF, F_RQB, F_RK, F_GQF, F_GQB = 0, 2, 4, 6, 8, 10
F_N = 12
C_ID, C_LE, C_GE, C_GT, C_LT, C_C0, C_C1, C_DIST = range(8)


def constants():
    l, i = np.arange(P)[:, None], np.arange(P)[None, :]
    same = (l // 64) == (i // 64)
    mats = [l == i, same & (l <= i), same & (l >= i), same & (l > i), same & (l < i),
            (l < 64) & (i >= 0), (l >= 64) & (i >= 0)]
    mats = [m.astype(np.float32) for m in mats] + [(i - l).astype(np.float32)]
    mats = np.stack(mats, 1)
    lc, ic = (np.arange(P) % 64)[:, None], np.arange(64)[None, :]
    tri = np.stack([lc <= ic, lc >= ic], 1).astype(np.float32)
    ksteps = np.stack([P - 1.0 - np.arange(P), np.arange(P) + 0.0], 1).astype(np.float32)
    qsteps = np.broadcast_to(np.stack([np.arange(P) + 1.0, P - np.arange(P) + 0.0]), (P, 2, P)).astype(np.float32)
    rope = np.zeros((TILES, P, 2, 64), np.float32)
    rope[:2, :, 0] = 1.0
    pos = np.arange(LAT)
    freqs = np.float32(10000.0) ** (-np.arange(16, dtype=np.float32) / np.float32(16))
    for axis, at in enumerate((pos // 64, pos % 64)):
        ang = (at.astype(np.float32)[:, None] * freqs).reshape(8, P, 16)
        c, s = np.cos(ang), np.sin(ang)
        rope[2:, :, 0, 32 * axis:32 * axis + 32] = np.concatenate([c, c], -1)
        rope[2:, :, 1, 32 * axis:32 * axis + 32] = np.concatenate([-s, s], -1)
    q, k = np.arange(P)[:, None], np.arange(3 * P)[None, :] - P
    win = np.zeros((TILES, P, 3 * P), np.float32)
    win[:2] = NEG
    for t in range(2, TILES):
        at = (t - 2) * P + k
        win[t] = np.where((np.abs(q - k) <= 128) & (at >= 0) & (at < LAT), 0.0, NEG)
    return mats, tri, ksteps, qsteps, rope, win


def signals(st, names):
    return {n: st.sem(n) for n in names.split()}


def settle(eng, passed):
    eng.sem_inc(passed, 1)


def prepare(nc, layer, proj, rope, conv_w, small, mats, tri, ksteps, qsteps, pack, feat, diag, tot, swq, swk):
    with Stage(nc, f"pre{layer}") as st:
        pr = st.sb("pr", [P, IN_W])
        before, after = st.sb("before", [P, 768]), st.sb("after", [P, 768])
        rp = st.sb("rp", [P, 2, 64])
        cw = st.sb("cw", [P, 3, 768])
        sm = st.sb("sm", [P, 3, 8])
        al, dtb, rate = sm[:, 0, :], sm[:, 1, :], sm[:, 2, :]
        lg = st.sb("lg", [P, 8])
        kd = st.sb("kd", [P, 2, RH])
        qd = st.sb("qd", [P, 2, 2, P])
        hot, swp = st.sb("hot", [P, 1152]), st.sb("swp", [P, 1152])
        hp = st.sb("hp", [P, 512])
        c0, c1, c2 = st.sb("c0", [P, 768]), st.sb("c1", [P, 768]), st.sb("c2", [P, 768])
        cv = st.sb("cv", [P, 768])
        sq = st.sb("sq", [P, 512])
        ss, rt, rn = st.sb("ss", [P, 8]), st.sb("rt", [P, 8]), st.sb("rn", [P, 8])
        xa, xn, xe, xl, g = (st.sb(n, [P, 8]) for n in ("xa", "xn", "xe", "xl", "g"))
        bm, be, b1, beta = (st.sb(n, [P, 8]) for n in ("bm", "be", "b1", "beta"))
        es = st.sb("es", [P, 32])
        nt, kt = st.sb("nt", [P, 8]), st.sb("kt", [P, 8])
        gu, mb, e1, de = (st.sb(n, [P, 2, 4, 64]) for n in ("gu", "mb", "e1", "de"))
        kh, qh = st.sb("kh", [P, 256]), st.sb("qh", [P, 256])
        qg = st.sb("qg", [P, 2, 4, 64])
        khT, qhT = st.sb("khT", [P, 2, P]), st.sb("qhT", [P, 2, P])
        pk = st.sb("pk", [P, T_W])
        ft = st.sb("ft", [P, F_N, P])
        sqT, skT = st.sb("sqT", [P, 4, P]), st.sb("skT", [P, P])
        one, eps = st.sb("one", [P, 1]), st.sb("eps", [P, 1])
        b_r, b_q, b_k, b_g, b_d, b_s, b_D, b_h = [st.ps(f"b_{n}", [P, 512]) for n in "rqkgdsDh"]
        s = signals(st, """set_in in_main in_side const expa lnready lgn expo decays alneg
            xa xn xe xl sp g bm be b1 beta gu sums es nt kt dsum e1 mb de c0 c1 c2 ca cb cv sq ss rt rn
            kh qh qg rot swapped rotated rk gv turned_r turned_q turned_k turned_g turned_d
            ftr ftf ftb ftd sqT skT khT qhT prod_e prod_o lt at nk ktp
            pe_passed sp_passed o_pack o_feat o_tot o_diag o_swq o_swk""")
        mat = lambda m: mats[:, m, :]
        B4 = [P, 2, 4, 64]

        def heads(ap, n):
            return ap.rearrange("p (h e) -> p h e", h=n)

        def per_head(ap8):
            return heads(ap8, 2).unsqueeze(3).broadcast_to(B4)

        def over_dirs(ap256):
            return heads(ap256, 4).unsqueeze(1).broadcast_to(B4)

        def packed(col):
            return pk[:, col:col + 512].rearrange("p (a h n) -> p a h n", a=2, h=4)

        with nc.Block() as block:
            @block.sync
            def _(sp):
                sp.dma_start(cw[:], conv_w[layer]).then_inc(s["set_in"], 16)
                sp.dma_start(sm[:], small[layer]).then_inc(s["set_in"], 16)

                def loads(t, row):
                    sp.wait_ge(s["swapped"], t * 8)
                    settle(sp, s["sp_passed"])
                    for q in (s["c0"], s["c2"], s["c1"], s["rot"], s["xa"], s["bm"]):
                        sp.wait_ge(q, t)
                    settle(sp, s["sp_passed"])
                    sp.dma_start(pr[:], proj[bass.ds(row, P), :]).then_inc(s["in_main"], 16)
                    sp.dma_start(rp[:], rope[bass.ds(t, 1)].rearrange("a p c n -> (a p) c n")).then_inc(s["in_main"], 16)
                    sp.dma_start(before[:], proj[bass.ds(row - 1, P), G_Q:G_Q + 768]).then_inc(s["in_side"], 16)
                    sp.dma_start(after[:], proj[bass.ds(row + 1, P), G_Q:G_Q + 768]).then_inc(s["in_side"], 16)

                def stores(t):
                    def got(*q):
                        for x in q:
                            sp.wait_ge(x, t + 1)
                        settle(sp, s["sp_passed"])

                    got(s["es"])
                    sp.dma_start(tot[bass.ds(t, 1)].rearrange("a p n -> (a p) n"), es[:, 16:32]).then_inc(s["o_tot"], 16)
                    got(s["sqT"], s["skT"])
                    sp.dma_start(swq[bass.ds(t, 1)].rearrange("a p c n -> (a p) c n"), sqT[:]).then_inc(s["o_swq"], 16)
                    sp.dma_start(swk[:, bass.ds(t * P + P, P)], skT[:]).then_inc(s["o_swk"], 16)
                    got(s["rk"], s["gv"], s["nk"], s["ktp"], s["lt"], s["at"])
                    sp.dma_start(pack[bass.ds(t, 1)].rearrange("a p n -> (a p) n"), pk[:]).then_inc(s["o_pack"], 16)
                    lt = pk[:, T_LT:T_LT + 512].rearrange("p (h i) -> p h i", h=8)
                    for b in range(4):
                        for d in range(2):
                            sp.dma_start(diag[d, bass.ds(t * 4 + b, 1)].rearrange("a h j i -> (a j) h i"),
                                         lt[32 * b:32 * b + 32, 4 * d:4 * d + 4, 32 * (b % 2):32 * (b % 2) + 32]).then_inc(s["o_diag"], 16)
                    sp.wait_ge(s["ftr"], t * 2 + 2)
                    settle(sp, s["sp_passed"])
                    got(s["ftf"], s["ftb"], s["ftd"])
                    sp.dma_start(feat[bass.ds(t, 1)].rearrange("a p f n -> (a p) f n"), ft[:]).then_inc(s["o_feat"], 16)

                sp.dma_start(pr[:], proj[row_of(0):row_of(0) + P, :]).then_inc(s["in_main"], 16)
                sp.dma_start(rp[:], rope[0]).then_inc(s["in_main"], 16)
                sp.dma_start(before[:], proj[row_of(0) - 1:row_of(0) - 1 + P, G_Q:G_Q + 768]).then_inc(s["in_side"], 16)
                sp.dma_start(after[:], proj[row_of(0) + 1:row_of(0) + 1 + P, G_Q:G_Q + 768]).then_inc(s["in_side"], 16)
                with sp.Fori(0, 1) as t:
                    loads(t + 1, t * P + row_of(1))
                    stores(t)
                with sp.Fori(1, TILES - 1) as t:
                    loads(t + 1, t * P + (row_of(2) - P))
                    stores(t)
                with sp.Fori(TILES - 1, TILES) as t:
                    stores(t)
                for q, n in ((s["o_tot"], 1), (s["o_swq"], 1), (s["o_swk"], 1), (s["o_pack"], 1), (s["o_feat"], 1), (s["o_diag"], 8)):
                    sp.wait_ge(q, TILES * 16 * n)

            @block.scalar
            def _(act):
                act.wait_ge(s["set_in"], 32)
                act.wait_ge(s["const"], 2)
                act.activation(al, al, ACT.Exp).then_inc(s["expa"], 1)
                act.activation(lg[:], rate, ACT.Exp, scale=-float(np.log(2.0))).then_inc(s["lnready"], 1)
                act.wait_ge(s["lnready"], 1)
                act.activation(lg[:], lg[:], ACT.Ln, scale=-1.0, bias=one[:]).then_inc(s["lgn"], 1)
                act.wait_ge(s["expo"], 9)
                act.activation(kd[:], kd[:], ACT.Exp).then_inc(s["decays"], 1)
                act.activation(qd[:], qd[:], ACT.Exp).then_inc(s["decays"], 1)
                with act.Fori(0, TILES) as t:
                    def got(*q):
                        for x in q:
                            act.wait_ge(x, t + 1)

                    def spent(*q):
                        for x in q:
                            act.wait_ge(x, t)

                    got(s["xn"]); spent(s["xl"])
                    act.activation(xe[:], xn[:], ACT.Exp).then_inc(s["xe"], 1)
                    got(s["bm"]); spent(s["b1"])
                    act.activation(be[:], bm[:], ACT.Exp, scale=-1.0).then_inc(s["be"], 1)
                    got(s["xe"]); spent(s["sp"])
                    act.activation(xl[:], xe[:], ACT.Ln, bias=one[:]).then_inc(s["xl"], 1)
                    got(s["sums"]); spent(s["nt"], s["kt"], s["qg"]); act.wait_ge(s["o_tot"], t * 16)
                    act.activation(es[:], b_s[:, 0:32], ACT.Exp).then_inc(s["es"], 1)
                    got(s["dsum"]); spent(s["de"])
                    act.activation(e1[:].rearrange("p a h n -> p (a h n)"), b_D[:], ACT.Exp).then_inc(s["e1"], 1)
                    got(s["cb"]); spent(s["sq"], s["kh"], s["qh"], s["gv"])
                    act.activation(cv[:], c1[:], ACT.Silu).then_inc(s["cv"], 1)
                    got(s["ss"]); spent(s["rn"])
                    act.activation(rt[:], ss[:], ACT.Sqrt, bias=eps[:]).then_inc(s["rt"], 1)
                    got(s["turned_q"]); act.wait_ge(s["o_swq"], t * 16)
                    act.activation(sqT[:].rearrange("p a n -> p (a n)"), b_q[:], ACT.Copy, scale=0.125).then_inc(s["sqT"], 1)
                    got(s["turned_k"]); act.wait_ge(s["o_swk"], t * 16)
                    act.activation(skT[:], b_k[:, 0:P], ACT.Copy).then_inc(s["skT"], 1)
                    got(s["turned_r"]); act.wait_ge(s["o_feat"], t * 16)
                    act.activation(ft[:, F_RQ:F_RQ + 2, :].rearrange("p a n -> p (a n)"), b_r[:, 0:256], ACT.Copy).then_inc(s["ftr"], 1)
                    act.activation(ft[:, F_RK:F_RK + 2, :].rearrange("p a n -> p (a n)"), b_r[:, 256:512], ACT.Copy).then_inc(s["ftr"], 1)
                    got(s["turned_g"]); spent(s["prod_e"], s["prod_o"])
                    act.activation(khT[:].rearrange("p a n -> p (a n)"), b_g[:, 0:256], ACT.Copy).then_inc(s["khT"], 1)
                    act.activation(qhT[:].rearrange("p a n -> p (a n)"), b_g[:, 256:512], ACT.Copy).then_inc(s["qhT"], 1)
                    got(s["turned_d"])
                    act.activation(ft[:, F_GQF:F_GQF + 4, :].rearrange("p a n -> p (a n)"), b_d[:], ACT.Copy).then_inc(s["ftd"], 1)

            @block.gpsimd
            def _(pool):
                pool.memset(one[:], 1.0).then_inc(s["const"], 1)
                pool.memset(eps[:], EPS).then_inc(s["const"], 1)
                pool.wait_ge(s["set_in"], 32)
                with pool.Fori(0, TILES) as t:
                    def got(*q):
                        for x in q:
                            pool.wait_ge(x, t + 1)

                    def spent(*q):
                        for x in q:
                            pool.wait_ge(x, t)

                    pool.wait_ge(s["in_side"], t * 32 + 32); spent(s["ca"])
                    pool.tensor_tensor(c0[:], before[:], cw[:, 0, :], ALU.mult).then_inc(s["c0"], 1)
                    spent(s["cb"])
                    pool.tensor_tensor(c2[:], after[:], cw[:, 2, :], ALU.mult).then_inc(s["c2"], 1)
                    pool.wait_ge(s["in_main"], t * 32 + 32); spent(s["rotated"])
                    for base, n, at in ((R_Q, 8, 0), (S_Q, 10, 512)):
                        src = pr[:, base:base + n * 64].rearrange("p (h a u f) -> p h a u f", h=n, a=2, u=2)
                        dst = swp[:, at:at + n * 64].rearrange("p (h a u f) -> p h a u f", h=n, a=2, u=2)
                        for half in range(2):
                            for axis in range(2):
                                sn = rp[:, 1, 32 * axis + 16 * half:32 * axis + 16 * half + 16].unsqueeze(1).broadcast_to([P, n, 16])
                                pool.tensor_tensor(dst[:, :, axis, half, :], src[:, :, axis, 1 - half, :], sn, ALU.mult).then_inc(s["swapped"], 1)
                    got(s["cv"]); spent(s["ss"])
                    pool.tensor_tensor(sq[:], cv[:, 0:512], cv[:, 0:512], ALU.mult).then_inc(s["sq"], 1)
                    got(s["beta"]); spent(s["de"])
                    pool.tensor_tensor(mb[:], tri[:].unsqueeze(2).broadcast_to(B4), per_head(beta[:]), ALU.mult).then_inc(s["mb"], 1)
                    got(s["kh"], s["nt"], s["kt"]); pool.wait_ge(s["o_pack"], t * 16)
                    pool.tensor_tensor(packed(T_NK), over_dirs(kh[:]), per_head(nt[:]), ALU.mult).then_inc(s["nk"], 1)
                    pool.tensor_tensor(packed(T_KT), over_dirs(kh[:]), per_head(kt[:]), ALU.mult).then_inc(s["ktp"], 1)

            @block.vector
            def _(dve):
                dve.wait_ge(s["expa"], 1)
                dve.tensor_scalar(al, al, -1.0, None, ALU.mult).then_inc(s["alneg"], 1)
                dve.wait_ge(s["lgn"], 1)
                dve.tensor_tensor(kd[:], heads(lg[:], 2), ksteps[:].unsqueeze(2).broadcast_to([P, 2, RH]), ALU.mult).then_inc(s["expo"], 1)
                for h in range(RH):
                    half = slice(64 * (h % 2), 64 * (h % 2) + 64)
                    for d in range(2):
                        dve.tensor_scalar(qd[half, d, h // 2, :], qsteps[half, d, :], lg[half, 4 * d + h:4 * d + h + 1], None,
                                          ALU.mult).then_inc(s["expo"], 1)
                dve.wait_ge(s["decays"], 2)
                dve.wait_ge(s["alneg"], 1)
                with dve.Fori(0, TILES) as t:
                    def got(*q):
                        for x in q:
                            dve.wait_ge(x, t + 1)

                    def spent(*q):
                        for x in q:
                            dve.wait_ge(x, t)

                    dve.wait_ge(s["in_main"], t * 32 + 32)
                    spent(s["sp"])
                    dve.tensor_tensor(xa[:], pr[:, G_A:G_A + 8], dtb, ALU.add).then_inc(s["xa"], 1)
                    spent(s["be"])
                    dve.tensor_scalar(bm[:], pr[:, G_B:G_B + 8], -80.0, None, ALU.max).then_inc(s["bm"], 1)
                    got(s["xa"]); spent(s["xe"])
                    dve.scalar_tensor_tensor(xn[:], xa[:], -1.0, xa[:], ALU.mult, ALU.min).then_inc(s["xn"], 1)
                    got(s["be"]); spent(s["beta"])
                    dve.tensor_scalar(b1[:], be[:], 1.0, None, ALU.add).then_inc(s["b1"], 1)
                    got(s["b1"]); spent(s["mb"], s["kt"])
                    dve.reciprocal(beta[:], b1[:]).then_inc(s["beta"], 1)
                    got(s["xl"])
                    dve.scalar_tensor_tensor(xl[:], xa[:], 0.0, xl[:], ALU.max, ALU.add).then_inc(s["sp"], 1)
                    got(s["sp"]); spent(s["gu"], s["sums"])
                    dve.tensor_tensor(g[:], xl[:], al, ALU.mult).then_inc(s["g"], 1)
                    got(s["g"]); spent(s["dsum"])
                    dve.tensor_tensor(gu[:], tri[:].unsqueeze(2).broadcast_to(B4), per_head(g[:]), ALU.mult).then_inc(s["gu"], 1)
                    dve.wait_ge(s["turned_r"], t); dve.wait_ge(s["turned_q"], t); dve.wait_ge(s["turned_k"], t)
                    spent(s["rk"])
                    cos = lambda n: rp[:, 0, :].unsqueeze(1).broadcast_to([P, n, 64])
                    dve.tensor_tensor(heads(hot[:, 0:512], 8), heads(pr[:, R_Q:R_Q + 512], 8), cos(8), ALU.mult)
                    dve.tensor_tensor(heads(hot[:, 512:1152], 10), heads(pr[:, S_Q:S_Q + 640], 10), cos(10), ALU.mult).then_inc(s["rot"], 1)
                    got(s["rot"]); dve.wait_ge(s["swapped"], t * 8 + 8)
                    dve.tensor_tensor(hot[:, 0:512], hot[:, 0:512], swp[:, 0:512], ALU.add)
                    dve.tensor_tensor(hot[:, 1024:1152], hot[:, 1024:1152], swp[:, 1024:1152], ALU.add)
                    side = lambda ap: ap[:, 512:1024].rearrange("p (u c n) -> p u c n", u=2, c=4)
                    dve.tensor_tensor(hp[:].rearrange("p (c u n) -> p u c n", c=4, u=2), side(hot), side(swp), ALU.add).then_inc(s["rotated"], 1)
                    spent(s["cv"])
                    dve.tensor_tensor(c1[:], pr[:, G_Q:G_Q + 768], cw[:, 1, :], ALU.mult).then_inc(s["c1"], 1)
                    got(s["c1"], s["c0"])
                    dve.tensor_tensor(c1[:], c1[:], c0[:], ALU.add).then_inc(s["ca"], 1)
                    got(s["ca"], s["c2"])
                    dve.tensor_tensor(c1[:], c1[:], c2[:], ALU.add).then_inc(s["cb"], 1)
                    got(s["rotated"]); dve.wait_ge(s["o_pack"], t * 16); dve.wait_ge(s["o_diag"], t * 128)
                    dve.tensor_tensor(packed(T_RK), over_dirs(hot[:, 256:512]), kd[:].unsqueeze(3).broadcast_to(B4), ALU.mult).then_inc(s["rk"], 1)
                    got(s["sq"]); spent(s["rt"])
                    dve.tensor_reduce(ss[:], heads(sq[:], 8), AX.X, ALU.add).then_inc(s["ss"], 1)
                    got(s["rt"]); spent(s["kh"], s["qh"])
                    dve.reciprocal(rn[:], rt[:]).then_inc(s["rn"], 1)
                    got(s["rn"]); spent(s["turned_g"], s["nk"], s["ktp"])
                    dve.tensor_tensor(heads(kh[:], 4), heads(cv[:, 256:512], 4), rn[:, 4:8].unsqueeze(2).broadcast_to([P, 4, 64]), ALU.mult).then_inc(s["kh"], 1)
                    spent(s["qg"])
                    dve.scalar_tensor_tensor(heads(qh[:], 4), heads(cv[:, 0:256], 4), 0.125, rn[:, 0:4].unsqueeze(2).broadcast_to([P, 4, 64]),
                                             ALU.mult, ALU.mult).then_inc(s["qh"], 1)
                    dve.tensor_copy(pk[:, T_GV:T_GV + 256], cv[:, 512:768]).then_inc(s["gv"], 1)
                    got(s["es"]); spent(s["nk"])
                    dve.tensor_scalar(nt[:], es[:, 0:8], -1.0, None, ALU.mult).then_inc(s["nt"], 1)
                    spent(s["ktp"])
                    dve.tensor_tensor(kt[:], es[:, 8:16], beta[:], ALU.mult).then_inc(s["kt"], 1)
                    got(s["qh"]); spent(s["turned_d"])
                    dve.tensor_tensor(qg[:], over_dirs(qh[:]), per_head(es[:, 0:8]), ALU.mult).then_inc(s["qg"], 1)
                    dve.wait_ge(s["ftr"], t * 2 + 2); dve.wait_ge(s["o_feat"], t * 16)
                    for d, col, q in ((0, F_RQF, s["ftf"]), (1, F_RQB, s["ftb"])):
                        dve.tensor_tensor(ft[:, col:col + 2, :], b_r[:, 0:256].rearrange("p (a n) -> p a n", a=2), qd[:, d, :, :], ALU.mult).then_inc(q, 1)
                    got(s["e1"], s["mb"]); spent(s["lt"], s["at"])
                    dve.tensor_tensor(de[:], e1[:], mb[:], ALU.mult).then_inc(s["de"], 1)
                    got(s["de"], s["prod_e"], s["prod_o"])
                    for col, q, o in ((T_LT, s["lt"], 0), (T_AT, s["at"], 128)):
                        for d in range(2):
                            for odd, bank in ((0, b_h), (1, b_k)):
                                src = bank[:, 256 * odd + o:256 * odd + o + 128].rearrange("p (h n) -> p h n", h=2)
                                last = dve.tensor_tensor(packed(col)[:, d, odd::2, :], src, de[:, d, odd::2, :], ALU.mult)
                        last.then_inc(q, 1)

            @block.tensor
            def _(pe):
                with pe.Fori(0, TILES) as t:
                    def got(*q):
                        for x in q:
                            pe.wait_ge(x, t + 1)

                    def spent(*q):
                        for x in q:
                            pe.wait_ge(x, t)

                    got(s["g"]); spent(s["es"])
                    for m, c0_, c1_, gcol in ((C_LE, 0, 4, 0), (C_GE, 4, 8, 4), (C_GT, 8, 12, 0), (C_LT, 12, 16, 4),
                                              (C_C0, 16, 24, 0), (C_C1, 24, 32, 0)):
                        mm = pe.matmul(b_s[:, c0_:c1_], mat(m), g[:, gcol:gcol + c1_ - c0_], start=True, stop=True)
                    mm.then_inc(s["sums"], 1)
                    got(s["gu"]); spent(s["e1"])
                    pe.matmul(b_D[:, 0:256], mat(C_GT), gu[:, 0, :, :].rearrange("p h n -> p (h n)"), start=True, stop=True)
                    mm = pe.matmul(b_D[:, 256:512], mat(C_LT), gu[:, 1, :, :].rearrange("p h n -> p (h n)"), start=True, stop=True)
                    mm.then_inc(s["dsum"], 1)
                    got(s["rotated"]); spent(s["ftf"], s["ftb"]); pe.wait_ge(s["ftr"], t * 2)
                    for c in range(4):
                        mm = pe.transpose(b_r[:, c * P:(c + 1) * P], hot[:, c * P:(c + 1) * P], mat(C_ID))
                    mm.then_inc(s["turned_r"], 1)
                    spent(s["sqT"])
                    for c in range(4):
                        mm = pe.transpose(b_q[:, c * P:(c + 1) * P], hp[:, c * P:(c + 1) * P], mat(C_ID))
                    mm.then_inc(s["turned_q"], 1)
                    spent(s["lt"], s["at"])
                    pe.transpose(b_k[:, 0:P], hot[:, 1024:1152], mat(C_ID)).then_inc(s["turned_k"], 1)
                    got(s["kh"], s["qh"]); spent(s["khT"], s["qhT"])
                    for c in range(4):
                        src = (kh, qh)[c // 2]
                        mm = pe.transpose(b_g[:, c * P:(c + 1) * P], src[:, (c % 2) * P:(c % 2 + 1) * P], mat(C_ID))
                    mm.then_inc(s["turned_g"], 1)
                    got(s["qg"]); spent(s["ftd"])
                    for c in range(4):
                        mm = pe.transpose(b_d[:, c * P:(c + 1) * P], qg[:, c // 2, 2 * (c % 2):2 * (c % 2) + 2, :], mat(C_ID))
                    mm.then_inc(s["turned_d"], 1)
                    got(s["khT"], s["qhT"], s["skT"])
                    settle(pe, s["pe_passed"])
                    for odd, bank, q in ((0, b_h, s["prod_e"]), (1, b_k, s["prod_o"])):
                        for pair in range(2):
                            for c in range(2):
                                d, j = slice(64 * odd, 64 * odd + 64), slice(64 * c, 64 * c + 64)
                                for o, rhs in ((0, khT), (128, qhT)):
                                    at = 256 * odd + o + 64 * pair
                                    mm = pe.matmul(bank[j, at:at + 64], khT[d, pair, j], rhs[d, pair, j], start=True, stop=True)
                        mm.then_inc(q, 1)


def solve(nc, layer, diag, inv):
    NB = 2 * TILES * GH
    with Stage(nc, f"slv{layer}") as st:
        n_in = [st.sb(f"n{d}", [NB, 2, 32, 32]) for d in range(2)]
        neg = [st.sb(f"neg{d}", [NB, 2, 32, 32]) for d in range(2)]
        xt = [st.sb(f"xt{d}", [NB, 2, 32, 32]) for d in range(2)]
        xx = [st.sb(f"xx{d}", [NB, 2, 32, 32]) for d in range(2)]
        prod = [st.sb(f"prod{d}", [NB, 2, 32, 32]) for d in range(2)]
        landed = [st.sem(f"landed{d}") for d in range(2)]
        zeroed, unit, negated, turned = [[st.sem(f"{n}{d}") for d in range(2)] for n in ("zeroed", "unit", "negated", "turned")]
        multiplied, summed = [[st.sem(f"{n}{d}") for d in range(2)] for n in ("multiplied", "summed")]
        stored = st.sem("stored")
        half = 2 * TILES
        with nc.Block() as block:
            @block.sync
            def _(sp):
                for d in range(2):
                    for slot in range(2):
                        sp.dma_start(n_in[d][:, slot].rearrange("p j i -> p (j i)"),
                                     diag[d, slot * half:(slot + 1) * half].rearrange("a h j i -> (a h) (j i)")).then_inc(landed[d], 16)
                for d in range(2):
                    for which, buf, ready, n in ((0, xt, summed, 31), (1, xx, turned, 1)):
                        sp.wait_ge(ready[d], n)
                        for slot in range(2):
                            sp.dma_start(inv[which, d, slot * half:(slot + 1) * half].rearrange("a h j i -> (a h) (j i)"),
                                         buf[d][:, slot].rearrange("p j i -> p (j i)")).then_inc(stored, 16)
                sp.wait_ge(stored, 8 * 16)

            @block.scalar
            def _(act):
                for d in range(2):
                    act.wait_ge(landed[d], 32)
                    act.activation(neg[d][:], n_in[d][:], ACT.Copy, scale=-1.0).then_inc(negated[d], 1)
                for d in range(2):
                    act.wait_ge(summed[d], 31)
                    act.activation(xx[d][:], xt[d][:].rearrange("p s c j -> p s j c"), ACT.Copy).then_inc(turned[d], 1)

            @block.gpsimd
            def _(pool):
                for d in range(2):
                    pool.memset(xt[d][:], 0.0).then_inc(zeroed[d], 1)
                    pool.wait_ge(zeroed[d], 1)
                    flat = xt[d][:].rearrange("p s c j -> p s (c j)")
                    pool.memset(flat[:, :, 0:1024:33], 1.0).then_inc(unit[d], 1)

            @block.vector
            def _(dve):
                for d in range(2):
                    dve.wait_ge(unit[d], 1)
                    dve.wait_ge(negated[d], 1)
                for step in range(1, 32):
                    for d in range(2):
                        r = step if d == 0 else 31 - step
                        before = slice(0, r) if d == 0 else slice(r + 1, 32)
                        if step > 1:
                            dve.wait_ge(summed[d], step - 1)
                        n_row = neg[d][:, :, before, r].unsqueeze(2).broadcast_to([NB, 2, step, step])
                        dve.tensor_tensor(prod[d][:, :, 0:step, 0:step], xt[d][:, :, before, before], n_row, ALU.mult).then_inc(multiplied[d], 1)
                    for d in range(2):
                        r = step if d == 0 else 31 - step
                        before = slice(0, r) if d == 0 else slice(r + 1, 32)
                        dve.wait_ge(multiplied[d], step)
                        dve.tensor_reduce(xt[d][:, :, before, r], prod[d][:, :, 0:step, 0:step], AX.X, ALU.add).then_inc(summed[d], 1)


def join(nc, layer, pack, inv, wts, us):
    with Stage(nc, f"jn{layer}") as st:
        off = [st.sb(f"off{u}", [P, 8, P]) for u in range(2)]
        xdt = [st.sb(f"xdt{u}", [P, 8, P]) for u in range(2)]
        xd = [st.sb(f"xd{u}", [P, 8, P]) for u in range(2)]
        vn = [st.sb(f"vn{u}", [P, 768]) for u in range(2)]
        y = [st.sb(f"y{d}", [P, 4, P]) for d in range(2)]
        xt = [st.sb(f"xt{d}", [P, 4, P]) for d in range(2)]
        u_o = [st.sb(f"u{d}", [P, 2, 2, HD]) for d in range(2)]
        w_o = [st.sb(f"w{d}", [P, 2, P]) for d in range(2)]
        b_y, b_g, b_u, b_w = [[st.ps(f"b_{n}{d}", [P, 512]) for d in range(2)] for n in "yguw"]
        zeroed = st.sem("zeroed")
        landed = [st.sem(f"landed{u}") for u in range(2)]
        y_sum, y_out, g_sum, x_done, u_sum, w_sum, u_out, w_out, stored = [[st.sem(f"{n}{d}") for d in range(2)] for n in (
            "y_sum", "y_out", "g_sum", "x_done", "u_sum", "w_sum", "u_out", "w_out", "stored")]
        sp_passed, pool_passed = st.sem("sp_passed"), st.sem("pool_passed")
        with nc.Block() as block:
            @block.sync
            def _(sp):
                sp.wait_ge(zeroed, 6)

                def load(u, t):
                    for b in range(4):
                        rows = slice(32 * b, 32 * b + 32)
                        for which, buf in ((0, xdt), (1, xd)):
                            for d in range(2):
                                sp.dma_start(buf[u][rows, 4 * d:4 * d + 4, rows],
                                             inv[which, d, bass.ds(t * 4 + b, 1)].rearrange("a h c j -> (a c) h j")).then_inc(landed[u], 16)
                        d, ib = (0, b + 1) if b % 2 == 0 else (1, b - 1)
                        src = pack[bass.ds(t, 1)].rearrange("a p n -> (a p) n")[rows, T_LT + 256 * d:T_LT + 256 * d + 256]
                        src = src.rearrange("p (h i) -> p h i", h=4)[:, :, 32 * (ib % 2):32 * (ib % 2) + 32]
                        sp.dma_start(off[u][rows, 4 * d:4 * d + 4, 32 * ib:32 * ib + 32], src).then_inc(landed[u], 16)
                    src = pack[bass.ds(t, 1)].rearrange("a p n -> (a p) n")
                    sp.dma_start(vn[u][:, 0:512], src[:, T_NK:T_NK + 512]).then_inc(landed[u], 16)
                    sp.dma_start(vn[u][:, 512:768], src[:, T_GV:T_GV + 256]).then_inc(landed[u], 16)

                for u in range(2):
                    load(u, u)
                with sp.Fori(0, TILES // 2 - 1) as n:
                    for u in range(2):
                        for q in (u_sum, w_sum):
                            for d in range(2):
                                sp.wait_ge(q[d], n * 2 + u + 1)
                                settle(sp, sp_passed)
                        load(u, n * 2 + u + 2)

            NL = 16 * (16 + 4 + 2)

            @block.tensor
            def _(pe):
                with pe.Fori(0, TILES // 2) as n:
                    for u in range(2):
                        t = n * 2 + u
                        pe.wait_ge(landed[u], n * NL + NL)
                        for d in range(2):
                            pe.wait_ge(y_out[d], t)
                            for h in range(4):
                                mm = pe.matmul(b_y[d][:, h * P:(h + 1) * P], off[u][:, 4 * d + h, :], xd[u][:, 4 * d + h, :], start=True, stop=True)
                            mm.then_inc(y_sum[d], 1)
                        for d in range(2):
                            pe.wait_ge(y_out[d], t + 1)
                            pe.wait_ge(x_done[d], t)
                            for h in range(4):
                                mm = pe.matmul(b_g[d][:, h * P:(h + 1) * P], y[d][:, h, :], xdt[u][:, 4 * d + h, :], start=True, stop=True)
                            mm.then_inc(g_sum[d], 1)
                        for d in range(2):
                            pe.wait_ge(x_done[d], t + 1)
                            pe.wait_ge(w_out[d], t)
                            for h in range(4):
                                e = slice(64 * (h % 2), 64 * (h % 2) + 64)
                                k = 256 * d + 64 * h
                                mm = pe.matmul(b_w[d][e, (h // 2) * P:(h // 2 + 1) * P], vn[u][:, k:k + 64], xt[d][:, h, :], start=True, stop=True)
                            mm.then_inc(w_sum[d], 1)
                            pe.wait_ge(u_out[d], t * 2)
                            for h in range(4):
                                pair = slice(512 + 128 * (h // 2), 512 + 128 * (h // 2) + 128)
                                mm = pe.matmul(b_u[d][:, h * P:(h + 1) * P], xt[d][:, h, :], vn[u][:, pair], start=True, stop=True)
                            mm.then_inc(u_sum[d], 1)

            @block.scalar
            def _(act):
                with act.Fori(0, TILES // 2) as n:
                    for u in range(2):
                        t = n * 2 + u
                        for d in range(2):
                            act.wait_ge(y_sum[d], t + 1)
                            act.wait_ge(g_sum[d], t)
                            act.activation(y[d][:].rearrange("p h n -> p (h n)"), b_y[d][:], ACT.Copy).then_inc(y_out[d], 1)
                        for d in range(2):
                            act.wait_ge(w_sum[d], t + 1)
                            act.wait_ge(stored[d], t * 32)
                            act.activation(w_o[d][:].rearrange("p a n -> p (a n)"), b_w[d][:, 0:256], ACT.Copy).then_inc(w_out[d], 1)

            @block.vector
            def _(dve):
                with dve.Fori(0, TILES // 2) as n:
                    for u in range(2):
                        t = n * 2 + u
                        for d in range(2):
                            dve.wait_ge(g_sum[d], t + 1)
                            dve.wait_ge(u_sum[d], t)
                            dve.tensor_tensor(xt[d][:].rearrange("p h n -> p (h n)"), xdt[u][:, 4 * d:4 * d + 4, :].rearrange("p h n -> p (h n)"),
                                              b_g[d][:], ALU.subtract).then_inc(x_done[d], 1)
                        for d in range(2):
                            dve.wait_ge(u_sum[d], t + 1)
                            dve.wait_ge(stored[d], t * 32)
                            for p in range(2):
                                src = b_u[d][:].rearrange("p (a n) -> p a n", a=2)[:, :, 192 * p:192 * p + 64]
                                dve.tensor_copy(u_o[d][:, :, p, :], src).then_inc(u_out[d], 1)

            @block.gpsimd
            def _(pool):
                for u in range(2):
                    for buf in (off, xdt, xd):
                        pool.memset(buf[u][:], 0.0).then_inc(zeroed, 1)
                with pool.Fori(0, TILES) as t:
                    for d in range(2):
                        pool.wait_ge(w_out[d], t + 1)
                        settle(pool, pool_passed)
                        dst = wts[bass.ds(t, 1)].rearrange("a p d c n -> (a p) d c n")
                        pool.dma_start(dst[:, d], w_o[d][:]).then_inc(stored[d], 16)
                        pool.wait_ge(u_out[d], t * 2 + 2)
                        settle(pool, pool_passed)
                        pool.dma_start(us[bass.ds(t, 1)].rearrange("a p n -> (a p) n")[:, 256 * d:256 * d + 256],
                                       u_o[d][:].rearrange("p a q e -> p (a q e)")).then_inc(stored[d], 16)
                for d in range(2):
                    pool.wait_ge(stored[d], TILES * 32)


def scan(nc, layer, proj, pack, feat, tot, wts, us, small, mats, o_ret, o_gdn):
    with Stage(nc, f"scn{layer}") as st:
        dual = lambda n, shape: [st.sb(f"{n}{u}", shape) for u in range(2)]
        gt = st.sb("gt", [P, TILES, 2, 2, 2, 2])
        gth = st.sb("gth", [P, TILES, 2, 2, 2])
        w_t = dual("w_t", [P, 2, 2, P])
        gqd = dual("gqd", [P, 2, 2, P])
        u_i = [dual(f"u_i{c}", [P, 256]) for c in range(2)]
        ktz = [dual(f"ktz{c}", [P, 2, 256]) for c in range(2)]
        atz = [dual(f"atz{c}", [P, 4, P]) for c in range(2)]
        rqz = dual("rqz", [P, 2, 2, P])
        rk, rv = dual("rk", [P, 2, P]), dual("rv", [P, 2, 256])
        rqd, rkd = dual("rqd", [P, 2, 2, P]), dual("rkd", [P, 2, 256])
        S, Sg = st.sb("S", [P, 2, 2, P]), st.sb("Sg", [P, 2, 2, P])
        R, Rg = st.sb("R", [P, 2, 2, P]), st.sb("Rg", [P, 2, 2, P])
        z = st.sb("z", [P, 256])
        mask, scores = st.sb("mask", [P, 4, P]), st.sb("scores", [P, 4, P])
        sm, lg, cd, cdh = st.sb("sm", [P, 3, 8]), st.sb("lg", [P, 8]), st.sb("cd", [P, 2, 2, 2]), st.sb("cdh", [P, 2, 2])
        far, keep, eg, kept = (st.sb(n, [P, 2, P]) for n in ("far", "keep", "eg", "kept"))
        one = st.sb("one", [P, 1])
        b_z, b_o, b_S, b_k, b_r, b_R = [st.ps(f"b_{n}", [P, 512]) for n in ("z", "o", "S", "k", "r", "R")]
        s = signals(st, """set_in const zeroed rate_e lgs cds cdhs gths fars keeps egs masked1 mask_done
            in0 in1 z_sum z_done dS_sum Sg_done S_done o_sum o_out k_sum scored r_sum r_out dR_sum Rg_done R_done
            sp_passed dve_passed pool_passed act_passed""")
        in_s = (s["in0"], s["in1"])
        NL = 16 * 25
        half = lambda a: slice(64 * a, 64 * a + 64)
        dist = mats[:, C_DIST, :]

        def tile_pairs(eng, body):
            with eng.Fori(0, 1) as n:
                for u in range(2):
                    body(n, u, n * 2 + u, n * 0 + (1 - u))
            with eng.Fori(1, TILES // 2) as n:
                for u in range(2):
                    body(n, u, n * 2 + u, n * -2 + (TILES + 1 - u))

        with nc.Block() as block:
            @block.sync
            def _(sp):
                sp.dma_start(gt[:].rearrange("p t c d a q -> p t (c d a q)"), tot.rearrange("t p n -> p t n")).then_inc(s["set_in"], 16)
                sp.dma_start(sm[:], small[layer]).then_inc(s["set_in"], 16)
                sp.wait_ge(s["zeroed"], 12)

                def tile(ap, t):
                    return ap[bass.ds(t, 1)].rearrange("a p n -> (a p) n")

                def rows_of(t, first):
                    return t * P + (row_of(0) if first else row_of(2) - 2 * P)

                def load(u, tf, tb, first):
                    q = in_s[u]
                    both = ((0, tf), (1, tb))
                    for d, t in both:
                        sp.dma_start(w_t[u][:, d], wts[bass.ds(t, 1)].rearrange("a p d c n -> (a p) d c n")[:, d]).then_inc(q, 16)
                        for c in range(2):
                            r = half(c if d == 0 else 1 - c)
                            sp.dma_start(u_i[c][u][r, :], tile(us, t)[r, 256 * d:256 * d + 256]).then_inc(q, 16)
                            sp.dma_start(ktz[c][u][r, d, :], tile(pack, t)[r, T_KT + 256 * d:T_KT + 256 * d + 256]).then_inc(q, 16)
                            src = tile(pack, t)[r, T_AT + 256 * d:T_AT + 256 * d + 256].rearrange("p (h i) -> p h i", h=4)
                            sp.dma_start(atz[c][u][r, :, half(d)], src).then_inc(q, 16)
                        ft = feat[bass.ds(t, 1)].rearrange("a p f n -> (a p) f n")
                        sp.dma_start(gqd[u][:, d], ft[:, F_GQF + 2 * d:F_GQF + 2 * d + 2, :]).then_inc(q, 16)
                        sp.dma_start(rqd[u][:, d], ft[:, F_RQF + 2 * d:F_RQF + 2 * d + 2, :]).then_inc(q, 16)
                        sp.dma_start(rkd[u][:, d, :], tile(pack, t)[:, T_RK + 256 * d:T_RK + 256 * d + 256]).then_inc(q, 16)
                        sp.dma_start(rv[u][:, d, :], proj[bass.ds(rows_of(t, first), P), R_V:R_V + 256]).then_inc(q, 16)
                    ft = feat[bass.ds(tf, 1)].rearrange("a p f n -> (a p) f n")
                    for p in range(2):
                        sp.dma_start(rqz[u][half(p), :, p, :], ft[half(p), F_RQ:F_RQ + 2, :]).then_inc(q, 16)
                    sp.dma_start(rk[u][:], ft[:, F_RK:F_RK + 2, :]).then_inc(q, 16)

                def again(t):
                    for q, k in ((s["o_sum"], 2), (s["r_sum"], 1), (s["dR_sum"], 1), (s["dS_sum"], 2), (s["z_done"], 2)):
                        sp.wait_ge(q, (t - 1) * k)
                        settle(sp, s["sp_passed"])

                with sp.Fori(0, 1) as n:
                    for u in range(2):
                        load(u, n + u, n + (1 - u), True)
                with sp.Fori(1, TILES // 2) as n:
                    for u in range(2):
                        again(n * 2 + u)
                        load(u, n * 2 + u, n * -2 + (TILES + 1 - u), False)

            @block.gpsimd
            def _(pool):
                for u in range(2):
                    for buf in (ktz[0], ktz[1], atz[0], atz[1], rqz):
                        pool.memset(buf[u][:], 0.0).then_inc(s["zeroed"], 1)
                pool.memset(S[:], 0.0).then_inc(s["zeroed"], 1)
                pool.memset(R[:], 0.0).then_inc(s["zeroed"], 1)
                pool.memset(one[:], 1.0).then_inc(s["const"], 1)
                pool.wait_ge(s["gths"], 2); pool.wait_ge(s["cdhs"], 2); pool.wait_ge(s["zeroed"], 12)

                def body(n, u, t, tb):
                    for c in range(2):
                        pool.wait_ge(s["S_done"], t * 4 + 2 * c)
                        for d, tt, cc in ((0, t, c), (1, tb, 1 - c)):
                            g = gth[:, bass.ds(tt, 1), cc, d, :].rearrange("p a n -> p (a n)").unsqueeze(2).broadcast_to([P, 2, P])
                            pool.tensor_tensor(Sg[:, d], S[:, d], g, ALU.mult).then_inc(s["Sg_done"], 1)
                        if c == 0:
                            pool.wait_ge(s["R_done"], t * 2)
                            pool.tensor_tensor(Rg[:], R[:], cdh[:].unsqueeze(3).broadcast_to([P, 2, 2, P]), ALU.mult).then_inc(s["Rg_done"], 1)

                tile_pairs(pool, body)

            @block.scalar
            def _(act):
                act.wait_ge(s["set_in"], 32)
                act.wait_ge(s["const"], 1)
                act.activation(lg[:], sm[:, 2, :], ACT.Exp, scale=-float(np.log(2.0))).then_inc(s["rate_e"], 1)
                act.wait_ge(s["rate_e"], 1)
                act.activation(lg[:], lg[:], ACT.Ln, scale=-1.0, bias=one[:]).then_inc(s["lgs"], 1)
                act.wait_ge(s["lgs"], 1)
                act.activation(cd[:].rearrange("p d a q -> p (d a q)"), lg[:], ACT.Exp, scale=float(P)).then_inc(s["cds"], 1)
                act.wait_ge(s["fars"], 2)
                for h in range(4):
                    if h:
                        act.wait_ge(s["masked1"], h)
                    for d in range(2):
                        act.activation(eg[:, d, :], far[:, d, :], ACT.Exp, scale=lg[:, 4 * d + h:4 * d + h + 1]).then_inc(s["egs"], 1)

                def body(n, u, t, tb):
                    for c in range(2):
                        act.wait_ge(s["o_sum"], t * 2 + c + 1)
                        for d, tt, cc in ((0, t, c), (1, tb, 1 - c)):
                            act.activation(o_gdn[:, d, :, bass.ds(tt * P + 64 * cc, 64)],
                                           b_o[:, 0:256].rearrange("p (a n) -> p a n", a=2)[:, :, half(d)], ACT.Copy).then_inc(s["o_out"], 1)
                        if c == 0:
                            act.wait_ge(s["r_sum"], t + 1)
                            for d, tt in ((0, t), (1, tb)):
                                act.activation(o_ret[:, d, :, bass.ds(tt * P, P)],
                                               b_r[:, 256 * d:256 * d + 256].rearrange("p (a n) -> p a n", a=2), ACT.Copy,
                                               scale=0.125).then_inc(s["r_out"], 1)

                tile_pairs(act, body)

            @block.vector
            def _(dve):
                dve.wait_ge(s["set_in"], 32)
                for p in range(2):
                    dve.tensor_copy(gth[half(p)], gt[half(p), :, :, :, :, p]).then_inc(s["gths"], 1)
                dve.wait_ge(s["cds"], 1)
                for p in range(2):
                    dve.tensor_copy(cdh[half(p)], cd[half(p), :, :, p]).then_inc(s["cdhs"], 1)
                dve.tensor_scalar(far[:, 0, :], dist, 0.0, None, ALU.max).then_inc(s["fars"], 1)
                dve.tensor_scalar(far[:, 1, :], dist, -1.0, 0.0, ALU.mult, ALU.max).then_inc(s["fars"], 1)
                dve.tensor_scalar(keep[:, 0, :], dist, 0.0, None, ALU.is_ge).then_inc(s["keeps"], 1)
                dve.tensor_scalar(keep[:, 1, :], dist, 0.0, None, ALU.is_le).then_inc(s["keeps"], 1)
                dve.wait_ge(s["keeps"], 2)
                for h in range(4):
                    dve.wait_ge(s["egs"], 2 * h + 2)
                    if h:
                        dve.wait_ge(s["mask_done"], h)
                    dve.tensor_tensor(kept[:], eg[:], keep[:], ALU.mult).then_inc(s["masked1"], 1)
                    dve.wait_ge(s["masked1"], h + 1)
                    dve.tensor_tensor(mask[:, h, :], kept[:, 0, :], kept[:, 1, :], ALU.add).then_inc(s["mask_done"], 1)
                dve.wait_ge(s["mask_done"], 4)

                def body(n, u, t, tb):
                    for c in range(2):
                        dve.wait_ge(s["z_sum"], t * 2 + c + 1)
                        dve.wait_ge(in_s[u], n * NL + NL)
                        dve.wait_ge(s["o_sum"], t * 2 + c)
                        dve.tensor_tensor(z[:], b_z[:, 0:256], u_i[c][u][:], ALU.add).then_inc(s["z_done"], 1)
                        if c == 0:
                            dve.wait_ge(s["k_sum"], t + 1)
                            dve.wait_ge(s["r_sum"], t)
                            dve.tensor_tensor(scores[:], b_k[:].rearrange("p (h n) -> p h n", h=4), mask[:], ALU.mult).then_inc(s["scored"], 1)
                        dve.wait_ge(s["dS_sum"], t * 2 + c + 1)
                        dve.wait_ge(s["Sg_done"], t * 4 + 2 * c + 2)
                        for p in range(2):
                            at = lambda b: b[:].rearrange("p (d a n) -> p d a n", d=2, a=2)[half(p), :, :, half(p)]
                            dve.tensor_tensor(S[half(p), :, :, half(p)], Sg[half(p), :, :, half(p)], at(b_S), ALU.add).then_inc(s["S_done"], 1)
                        if c == 1:
                            dve.wait_ge(s["dR_sum"], t + 1)
                            dve.wait_ge(s["Rg_done"], t + 1)
                            for p in range(2):
                                at = lambda b: b[:].rearrange("p (d a n) -> p d a n", d=2, a=2)[half(p), :, :, half(p)]
                                dve.tensor_tensor(R[half(p), :, :, half(p)], Rg[half(p), :, :, half(p)], at(b_R), ALU.add).then_inc(s["R_done"], 1)

                tile_pairs(dve, body)

            @block.tensor
            def _(pe):
                pe.wait_ge(s["zeroed"], 12)

                def body(n, u, t, tb):
                    pe.wait_ge(in_s[u], n * NL + NL)
                    for c in range(2):
                        cc = (c, 1 - c)
                        pe.wait_ge(s["S_done"], t * 4 + 2 * c)
                        pe.wait_ge(s["z_done"], t * 2 + c)
                        for d in range(2):
                            for a in range(2):
                                mm = pe.matmul(b_z[half(cc[d]), a * P:(a + 1) * P], w_t[u][:, d, a, half(cc[d])], S[:, d, a, :], start=True, stop=True)
                        mm.then_inc(s["z_sum"], 1)
                        pe.wait_ge(s["o_out"], t * 4 + 2 * c)
                        for d in range(2):
                            for a in range(2):
                                for p in range(2):
                                    pe.matmul(b_o[half(p), a * P + 64 * d:a * P + 64 * d + 64], S[:, d, a, half(p)],
                                              gqd[u][:, d, a, half(cc[d])], start=(d == 0 and a == 0), stop=False)
                        if c == 0:
                            pe.wait_ge(s["scored"], t)
                            for a in range(2):
                                mm = pe.matmul(b_k[:, 256 * a:256 * a + 256], rk[u][:, a, :], rqz[u][:, a].rearrange("p q n -> p (q n)"), start=True, stop=True)
                            mm.then_inc(s["k_sum"], 1)
                        else:
                            pe.wait_ge(s["R_done"], t * 2)
                            for d in range(2):
                                for a in range(2):
                                    at = 256 * d + 128 * a
                                    mm = pe.matmul(b_R[:, at:at + P], rkd[u][:, d, a * P:(a + 1) * P], rv[u][:, d, a * P:(a + 1) * P], start=True, stop=True)
                            mm.then_inc(s["dR_sum"], 1)
                        pe.wait_ge(s["z_done"], t * 2 + c + 1)
                        for d in range(2):
                            for a in range(2):
                                at = 256 * d + 128 * a
                                mm = pe.matmul(b_S[:, at:at + P], ktz[c][u][:, d, a * P:(a + 1) * P], z[:, a * P:(a + 1) * P], start=True, stop=True)
                        mm.then_inc(s["dS_sum"], 1)
                        for a in range(2):
                            for p in range(2):
                                h = 2 * a + p
                                mm = pe.matmul(b_o[half(p), a * P:(a + 1) * P], z[:, h * 64:h * 64 + 64], atz[c][u][:, h, :], start=False, stop=(a == 1))
                        mm.then_inc(s["o_sum"], 1)
                        if c == 0:
                            pe.wait_ge(s["r_out"], t * 2)
                            pe.wait_ge(s["R_done"], t * 2)
                            for d in range(2):
                                for a in range(2):
                                    at = 256 * d + 128 * a
                                    pe.matmul(b_r[:, at:at + P], R[:, d, a, :], rqd[u][:, d, a, :], start=(d == 0 and a == 0), stop=False)
                            pe.wait_ge(s["scored"], t + 1)
                            for a in range(2):
                                for p in range(2):
                                    h = 2 * a + p
                                    mm = pe.matmul(b_r[half(p), a * P:(a + 1) * P], rv[u][:, 0, h * 64:h * 64 + 64], scores[:, h, :], start=False, stop=(a == 1))
                            mm.then_inc(s["r_sum"], 1)

                tile_pairs(pe, body)


def window(nc, layer, t0, proj, swq, swk, win, sinks, mats, y_hi, y_lo):
    NT = TILES - t0
    K = 3 * P + CTX
    with Stage(nc, f"win{layer}") as st:
        keys = st.sb("keys", [P, TOK + 2 * P])
        vc = st.sb("vc", [P, 2, P])
        sink = st.sb("sink", [P, SH])
        qz = [st.sb(f"qz{u}", [P, 2, 4, P]) for u in range(2)]
        mask = [st.sb(f"mask{u}", [P, 3 * P]) for u in range(2)]
        vw = [st.sb(f"vw{u}", [P, 3, P]) for u in range(2)]
        prob = [st.sb(f"prob{i}", [P, K]) for i in range(2)]
        probT = [st.sb(f"probT{i}", [P, 5, P]) for i in range(2)]
        mx = [st.sb(f"mx{i}", [P, 2]) for i in range(2)]
        low = [st.sb(f"low{i}", [P, 1]) for i in range(2)]
        nmax = [st.sb(f"nmax{i}", [P, 1]) for i in range(2)]
        part = [st.sb(f"part{i}", [P, 3]) for i in range(2)]
        den, rden = [st.sb(f"den{i}", [P, 1]) for i in range(2)], [st.sb(f"rden{i}", [P, 1]) for i in range(2)]
        yt = st.sb("yt", [P, SH * HD])
        b_l, b_c, b_o = [[st.ps(f"b_{n}{i}", [P, 512]) for i in range(2)] for n in "lco"]
        b_t0, b_t1 = st.ps("b_t0", [P, 512]), st.ps("b_t1", [P, 512])
        s = signals(st, "set_in zeroed t0_out t1_out y_turned y_rounded y_split pe_passed dve_passed sp_passed")
        landed, s_sum, masked, cmax, lowered, m_done, e_loc, e_ctx, e_sink, t_sum, o_sum, summed, inverted, y_done = [
            [st.sem(f"{n}{i}") for i in range(2)] for n in
            "landed s_sum masked cmax lowered m_done e_loc e_ctx e_sink t_sum o_sum summed inverted y_done".split()]

        with nc.Block() as block:
            @block.sync
            def _(sp):
                sp.dma_start(keys[:], swk).then_inc(s["set_in"], 16)
                sp.dma_start(vc[:], proj[R0 + 1:R0 + 1 + CTX, S_V:S_V + P].rearrange("(b p) n -> p b n", p=P)).then_inc(s["set_in"], 16)
                sp.dma_start(sink[:], sinks[layer]).then_inc(s["set_in"], 16)
                sp.wait_ge(s["zeroed"], 2)

                def load(u, t, row):
                    for p in range(2):
                        r = slice(64 * p, 64 * p + 64)
                        sp.dma_start(qz[u][r, p], swq[bass.ds(t, 1)].rearrange("a p c n -> (a p) c n")[r]).then_inc(landed[u], 16)
                    sp.dma_start(mask[u][:], win[bass.ds(t, 1)].rearrange("a p n -> (a p) n")).then_inc(landed[u], 16)
                    sp.dma_start(vw[u][:], proj[bass.ds(row - P, 3 * P), S_V:S_V + P].rearrange("(b p) n -> p b n", p=P)).then_inc(landed[u], 16)

                for u in range(2):
                    with sp.Fori(t0 + u, t0 + u + 1) as t:
                        load(u, t, t * P + (row_of(t0) - t0 * P))
                with sp.Fori(1, NT // 2) as n:
                    for u in range(2):
                        for q in o_sum:
                            sp.wait_ge(q, (n * 2 + u - 1) * 4)
                            settle(sp, s["sp_passed"])
                        load(u, n * 2 + (u + t0), n * (2 * P) + ((u + t0) * P + row_of(2) - 2 * P))

            @block.gpsimd
            def _(pool):
                for u in range(2):
                    pool.memset(qz[u][:], 0.0).then_inc(s["zeroed"], 1)

            def scores(pe, h, u, T):
                i, use = h % 2, T * 4 + h // 2
                pe.wait_ge(masked[i], use)
                pe.wait_ge(e_ctx[i], use)
                q = qz[u][:, h // 4, h % 4, :]
                pe.matmul(b_l[i][:, 0:3 * P], q, keys[:, bass.ds(T * P + t0 * P, 3 * P)], start=True, stop=True)
                pe.matmul(b_c[i][:, 0:CTX], q, keys[:, P:P + CTX], start=True, stop=True).then_inc(s_sum[i], 1)

            @block.tensor
            def _(pe):
                pe.wait_ge(s["set_in"], 48)
                with pe.Fori(0, NT // 2) as n:
                    for u in range(2):
                        T = n * 2 + u
                        pe.wait_ge(landed[u], n * 64 + 64)
                        scores(pe, 0, u, T)
                        for h in range(SH):
                            i, use = h % 2, T * 4 + h // 2
                            if h + 1 < SH:
                                scores(pe, h + 1, u, T)
                            pe.wait_ge(e_loc[i], use + 1)
                            pe.wait_ge(e_ctx[i], use + 1)
                            pe.wait_ge(s["t0_out"], T * 8 + h)
                            pe.wait_ge(s["t1_out"], T * 8 + h)
                            if h == 0:
                                pe.wait_ge(s["y_split"], T)
                            for b in range(5):
                                bank = b_t0[:, b * P:(b + 1) * P] if b < 3 else b_t1[:, (b - 3) * P:(b - 2) * P]
                                mm = pe.transpose(bank, prob[i][:, b * P:(b + 1) * P], mats[:, C_ID, :])
                            mm.then_inc(t_sum[i], 1)
                            pe.wait_ge(s["t0_out"], T * 8 + h + 1)
                            pe.wait_ge(s["t1_out"], T * 8 + h + 1)
                            pe.wait_ge(y_done[i], use)
                            for b in range(5):
                                v = vw[u][:, b, :] if b < 3 else vc[:, b - 3, :]
                                mm = pe.matmul(b_o[i][:, 0:P], probT[i][:, b, :], v, start=(b == 0), stop=(b == 4))
                            mm.then_inc(o_sum[i], 1)
                        for i in range(2):
                            pe.wait_ge(y_done[i], T * 4 + 4)
                        for c in range(4):
                            mm = pe.transpose(b_t0[:, c * P:(c + 1) * P], yt[:, c * P:(c + 1) * P], mats[:, C_ID, :])
                        mm.then_inc(s["y_turned"], 1)

            def maximum(dve, h, u, T):
                i, use = h % 2, T * 4 + h // 2
                if h == 0:
                    dve.wait_ge(landed[u], (T - u) * 32 + 64)
                dve.wait_ge(s_sum[i], use + 1)
                dve.wait_ge(t_sum[i], use)
                dve.wait_ge(lowered[i], use)
                settle(dve, s["dve_passed"])
                dve.tensor_tensor_reduce(prob[i][:, 0:3 * P], b_l[i][:, 0:3 * P], mask[u][:], 1.0, NEG, ALU.add, ALU.max,
                                         mx[i][:, 0:1]).then_inc(masked[i], 1)
                dve.tensor_reduce(mx[i][:, 1:2], b_c[i][:, 0:CTX], AX.X, ALU.max).then_inc(cmax[i], 1)
                dve.wait_ge(masked[i], use + 1)
                dve.wait_ge(cmax[i], use + 1)
                dve.wait_ge(m_done[i], use)
                dve.tensor_tensor(low[i][:], mx[i][:, 0:1], mx[i][:, 1:2], ALU.max).then_inc(lowered[i], 1)
                dve.wait_ge(lowered[i], use + 1)
                dve.wait_ge(e_sink[i], use)
                dve.tensor_scalar(nmax[i][:], low[i][:], sink[:, h:h + 1], -1.0, ALU.max, ALU.mult).then_inc(m_done[i], 1)

            def weigh(dve, h, T):
                i, use = h % 2, T * 4 + h // 2
                dve.wait_ge(o_sum[i], use + 1)
                dve.wait_ge(inverted[i], use + 1)
                if h == 0:
                    dve.wait_ge(s["y_turned"], T)
                e = slice(64 * (h // 4), 64 * (h // 4) + 64)
                dve.tensor_scalar(yt[:, h * 64:h * 64 + 64], b_o[i][:, e], rden[i][:], None, ALU.mult).then_inc(y_done[i], 1)

            @block.vector
            def _(dve):
                dve.wait_ge(s["set_in"], 48)
                with dve.Fori(0, NT // 2) as n:
                    for u in range(2):
                        T = n * 2 + u
                        tok = bass.ds(T * P + t0 * P, P)
                        maximum(dve, 0, u, T)
                        for h in range(SH):
                            i, use = h % 2, T * 4 + h // 2
                            if h + 1 < SH:
                                maximum(dve, h + 1, u, T)
                            dve.wait_ge(t_sum[i], use + 1)
                            dve.wait_ge(o_sum[i], use)
                            dve.tensor_copy(probT[i][:, 3:5, :].rearrange("p a n -> p (a n)"), b_t1[:, 0:2 * P]).then_inc(s["t1_out"], 1)
                            dve.wait_ge(e_sink[i], use + 1)
                            dve.wait_ge(inverted[i], use)
                            dve.scalar_tensor_tensor(den[i][:], part[i][:, 0:1], part[i][:, 1:2], part[i][:, 2:3], ALU.add, ALU.add).then_inc(summed[i], 1)
                            dve.wait_ge(summed[i], use + 1)
                            dve.wait_ge(y_done[i], use)
                            dve.reciprocal(rden[i][:], den[i][:]).then_inc(inverted[i], 1)
                            if h:
                                weigh(dve, h - 1, T)
                        weigh(dve, SH - 1, T)
                        dve.wait_ge(s["y_rounded"], T + 1)
                        dve.tensor_tensor(y_lo[:, 2:6, tok], b_t0[:].rearrange("p (c n) -> p c n", c=4), y_hi[:, 2:6, tok].bitcast(F32),
                                          ALU.subtract).then_inc(s["y_split"], 1)

            def exponentials(act, h, T):
                i, use = h % 2, T * 4 + h // 2
                act.wait_ge(m_done[i], use + 1)
                act.wait_ge(summed[i], use)
                act.activation(prob[i][:, 0:3 * P], prob[i][:, 0:3 * P], ACT.Exp, bias=nmax[i][:], accum_out=part[i][:, 0:1]).then_inc(e_loc[i], 1)
                act.activation(prob[i][:, 3 * P:K], b_c[i][:, 0:CTX], ACT.Exp, bias=nmax[i][:], accum_out=part[i][:, 1:2]).then_inc(e_ctx[i], 1)
                act.activation(part[i][:, 2:3], sink[:, h:h + 1], ACT.Exp, bias=nmax[i][:]).then_inc(e_sink[i], 1)

            @block.scalar
            def _(act):
                with act.Fori(0, NT // 2) as n:
                    for u in range(2):
                        T = n * 2 + u
                        tok = bass.ds(T * P + t0 * P, P)
                        exponentials(act, 0, T)
                        for h in range(SH):
                            i, use = h % 2, T * 4 + h // 2
                            if h + 1 < SH:
                                exponentials(act, h + 1, T)
                            act.wait_ge(t_sum[i], use + 1)
                            act.wait_ge(o_sum[i], use)
                            act.activation(probT[i][:, 0:3, :].rearrange("p a n -> p (a n)"), b_t0[:, 0:3 * P], ACT.Copy).then_inc(s["t0_out"], 1)
                        act.wait_ge(s["y_turned"], T + 1)
                        act.activation(y_hi[:, 2:6, tok], b_t0[:].rearrange("p (c n) -> p c n", c=4), ACT.Copy).then_inc(s["y_rounded"], 1)


def gated(nc, layer, t0, proj, norm_w, mats, o_ret, o_gdn, y_hi, y_lo, eps):
    NG = (TILES - t0) // 2
    W = 2 * P
    with Stage(nc, f"gate{layer}") as st:
        gin = [st.sb(f"gin{u}", [P, 2, 512]) for u in range(2)]
        nw = st.sb("nw", [P, 4])
        mean = st.sb("mean", [P, P])
        os_, sq, sg, root, inv, y1, yf = (st.sb(n, [P, 4, W]) for n in ("os", "sq", "sg", "root", "inv", "y1", "yf"))
        b_g, b_m = [[st.ps(f"b_{n}{i}", [P, 512]) for i in range(2)] for n in "gm"]
        s = signals(st, "set_in mean0 mean1 in0 in1 added squared turned silued summed rooted inverted normed gated rounded split sp_passed")
        ins = (s["in0"], s["in1"])
        with nc.Block() as block:
            @block.sync
            def _(sp):
                sp.dma_start(nw[:], norm_w[layer]).then_inc(s["set_in"], 16)

                for g in range(NG):
                    if g >= 2:
                        sp.wait_ge(s["turned"], g - 1)
                    row = row_of(t0 + 2 * g)
                    for half, col in ((0, R_G), (1, G_Z)):
                        sp.dma_start(gin[g % 2][:, :, 256 * half:256 * half + 256],
                                     proj[row:row + W, col:col + 256].rearrange("(b p) n -> p b n", p=P)).then_inc(ins[g % 2], 16)

            @block.gpsimd
            def _(pool):
                pool.memset(mean[:], 0.0).then_inc(s["mean0"], 1)
                pool.wait_ge(s["mean0"], 1)
                for p in range(2):
                    r = slice(64 * p, 64 * p + 64)
                    pool.memset(mean[r, r], 1.0 / HD).then_inc(s["mean1"], 1)
                pool.wait_ge(s["mean1"], 2)
                with pool.Fori(0, NG) as g:
                    tok = bass.ds(g * W + t0 * P, W)
                    pool.wait_ge(s["normed"], g)
                    pool.wait_ge(s["squared"], g)
                    pool.tensor_tensor(os_[:, 0:2, :], o_ret[:, 0, :, tok], o_ret[:, 1, :, tok], ALU.add).then_inc(s["added"], 1)
                    pool.tensor_tensor(os_[:, 2:4, :], o_gdn[:, 0, :, tok], o_gdn[:, 1, :, tok], ALU.add).then_inc(s["added"], 1)

            @block.tensor
            def _(pe):
                pe.wait_ge(s["mean1"], 2)
                for g in range(NG):
                    pe.wait_ge(ins[g % 2], (g // 2 + 1) * 32)
                    if g:
                        pe.wait_ge(s["silued"], 2 * g)
                    for c in range(4):
                        for b in range(2):
                            at = (c % 2) * W + b * P
                            mm = pe.transpose(b_g[c // 2][:, at:at + P], gin[g % 2][:, b, c * P:(c + 1) * P], mats[:, C_ID, :])
                    mm.then_inc(s["turned"], 1)
                    pe.wait_ge(s["squared"], g + 1)
                    if g:
                        pe.wait_ge(s["rooted"], 2 * g)
                    for i in range(2):
                        mm = pe.matmul(b_m[i][:], mean[:], sq[:, 2 * i:2 * i + 2, :].rearrange("p c n -> p (c n)"), start=True, stop=True)
                    mm.then_inc(s["summed"], 1)

            flat = lambda b, i: b[:, 2 * i:2 * i + 2, :].rearrange("p c n -> p (c n)")

            @block.scalar
            def _(act):
                with act.Fori(0, NG) as g:
                    tok = bass.ds(g * W + t0 * P, W)
                    act.wait_ge(s["added"], g * 2 + 2)
                    act.wait_ge(s["summed"], g)
                    act.activation(sq[:], os_[:], ACT.Square).then_inc(s["squared"], 1)
                    act.wait_ge(s["summed"], g + 1)
                    act.wait_ge(s["inverted"], g)
                    for i in range(2):
                        act.activation(flat(root, i), b_m[i][:], ACT.Sqrt, bias=eps[:]).then_inc(s["rooted"], 1)
                    act.wait_ge(s["turned"], g + 1)
                    act.wait_ge(s["gated"], g * 4)
                    for i in range(2):
                        act.activation(flat(sg, i), b_g[i][:], ACT.Silu).then_inc(s["silued"], 1)
                    act.wait_ge(s["gated"], g * 4 + 4)
                    for i, c in ((0, 0), (1, 6)):
                        act.activation(y_hi[:, c:c + 2, tok], yf[:, 2 * i:2 * i + 2, :], ACT.Copy).then_inc(s["rounded"], 1)

            @block.vector
            def _(dve):
                dve.wait_ge(s["set_in"], 16)
                with dve.Fori(0, NG) as g:
                    tok = bass.ds(g * W + t0 * P, W)
                    dve.wait_ge(s["rooted"], g * 2 + 2)
                    dve.wait_ge(s["normed"], g)
                    dve.reciprocal(inv[:], root[:]).then_inc(s["inverted"], 1)
                    dve.wait_ge(s["inverted"], g + 1)
                    dve.wait_ge(s["gated"], g * 4)
                    dve.tensor_tensor(y1[:], os_[:], inv[:], ALU.mult).then_inc(s["normed"], 1)
                    dve.wait_ge(s["normed"], g + 1)
                    dve.wait_ge(s["silued"], g * 2 + 2)
                    dve.wait_ge(s["split"], g * 2)
                    for c in range(4):
                        dve.scalar_tensor_tensor(yf[:, c, :], y1[:, c, :], nw[:, c:c + 1], sg[:, c, :], ALU.mult, ALU.mult).then_inc(s["gated"], 1)
                    dve.wait_ge(s["rounded"], g * 2 + 2)
                    for i, c in ((0, 0), (1, 6)):
                        dve.tensor_tensor(y_lo[:, c:c + 2, tok], yf[:, 2 * i:2 * i + 2, :], y_hi[:, c:c + 2, tok].bitcast(F32),
                                          ALU.subtract).then_inc(s["split"], 1)


def mixed(nc, layer, lo, x, units, mod, y_hi, y_lo):
    slices = token_slices(lo)
    NS, TURNS = len(slices), KC // 2
    with Stage(nc, f"mix{layer}") as st:
        w = WeightUnits(st, units)
        bank = [[st.ps(f"bank{u}{s}", [P, 512]) for s in range(NS)] for u in range(2)]
        full = [[st.sem(f"full{u}{s}") for s in range(NS)] for u in range(2)]
        free = [[st.sem(f"free{u}{s}") for s in range(NS)] for u in range(2)]
        with nc.Block() as block:
            @block.sync
            def _(sp):
                w.load_all(sp, TURNS)

            @block.scalar
            def _(act):
                with act.Fori(0, TURNS) as n:
                    for u in range(2):
                        w.round(act, u, n)

            @block.tensor
            def _(pe):
                with pe.Fori(0, TURNS) as n:
                    for u in range(2):
                        pe.wait_ge(w.ready[u], n + 1)
                        for s, (t0, ln) in enumerate(slices):
                            pe.wait_ge(free[u][s], n)
                            for k in range(KC):
                                f = slice(k * P, (k + 1) * P)
                                mm = three_passes(pe, bank[u][s][:, 0:ln], w.hi[u][:, f], w.lo[u][:, f],
                                                  y_hi[:, k, t0:t0 + ln], y_lo[:, k, t0:t0 + ln], k == 0, k == KC - 1)
                            mm.then_inc(full[u][s], 1)
                        pe.wait_ge(full[u][NS - 1], n + 1)
                        pe.sem_inc(w.used[u], 1)

            @block.vector
            def _(dve):
                def add(n, u):
                    for s, (t0, ln) in enumerate(slices):
                        v = 1 if t0 < CTX else 0
                        dve.wait_ge(full[u][s], n + 1)
                        xs = x[:, bass.ds(n * 2 + u, 1), t0:t0 + ln].rearrange("p a n -> p (a n)")
                        dve.scalar_tensor_tensor(xs, bank[u][s][:, 0:ln], mod[:, bass.ds(n * 2 + (u + 2 * KC), 1), v], xs,
                                                 ALU.mult, ALU.add).then_inc(free[u][s], 1)

                for u in range(2):
                    w.rest(dve, u, 0)
                with dve.Fori(0, TURNS - 1) as n:
                    for u in range(2):
                        add(n, u)
                        w.rest(dve, u, n + 1)
                with dve.Fori(TURNS - 1, TURNS) as n:
                    for u in range(2):
                        add(n, u)


def final(nc, x, norm_w, out, ones, eps):
    with Stage(nc, "fin") as st:
        nw = st.sb("nw", [P, KC])
        sq = [st.sb(f"sq{i}", [P, 512]) for i in range(2)]
        root, inv = st.sb("root", [P, 512]), st.sb("inv", [P, 512])
        y = st.sb("y", [P, KC, LAT])
        ms = [st.ps(f"ms{s}", [P, 512]) for s in range(2)]
        s = signals(st, "set_in squared summed rooted inverted done stored")
        with nc.Block() as block:
            @block.sync
            def _(sp):
                sp.dma_start(nw[:], norm_w).then_inc(s["set_in"], 16)
                for i in range(2 * KC):
                    sp.wait_ge(s["done"], i + 1)
                    at = slice((i // KC) * 512, (i // KC) * 512 + 512)
                    sp.dma_start(out[:, i % KC, at], y[:, i % KC, at]).then_inc(s["stored"], 16)
                sp.wait_ge(s["stored"], 2 * KC * 16)

            @block.scalar
            def _(act):
                for sl in range(2):
                    t = CTX + 512 * sl
                    for k in range(KC):
                        i = sl * KC + k
                        if i >= 2:
                            act.wait_ge(s["summed"], i - 1)
                        act.activation(sq[i % 2][:], x[:, k, t:t + 512], ACT.Square).then_inc(s["squared"], 1)
                    act.wait_ge(s["summed"], (sl + 1) * KC)
                    if sl:
                        act.wait_ge(s["inverted"], 1)
                    act.activation(root[:], ms[sl][:], ACT.Sqrt, bias=eps[:]).then_inc(s["rooted"], 1)

            @block.tensor
            def _(pe):
                for i in range(2 * KC):
                    pe.wait_ge(s["squared"], i + 1)
                    pe.matmul(ms[i // KC][:], ones[:], sq[i % 2][:], start=(i % KC == 0), stop=(i % KC == KC - 1)).then_inc(s["summed"], 1)

            @block.vector
            def _(dve):
                dve.wait_ge(s["set_in"], 16)
                for sl in range(2):
                    t = CTX + 512 * sl
                    dve.wait_ge(s["rooted"], sl + 1)
                    if sl:
                        dve.wait_ge(s["done"], KC)
                    dve.reciprocal(inv[:], root[:]).then_inc(s["inverted"], 1)
                    dve.wait_ge(s["inverted"], sl + 1)
                    for k in range(KC):
                        dve.scalar_tensor_tensor(y[:, k, sl * 512:sl * 512 + 512], x[:, k, t:t + 512], nw[:, k:k + 1], inv[:],
                                                 ALU.mult, ALU.mult).then_inc(s["done"], 1)


def begin(nc, loads, zeros, fills):
    with Stage(nc, "begin") as st:
        zero = st.sb("zero", [P, G_Z - S_V])
        loaded, zeroed, filled, stored = (st.sem(n) for n in ("loaded", "zeroed", "filled", "stored"))
        with nc.Block() as block:
            @block.sync
            def _(sp):
                for dst, src in loads:
                    sp.dma_start(dst, src).then_inc(loaded, 16)
                sp.wait_ge(zeroed, 1)
                for dst in zeros:
                    sp.dma_start(dst, zero[0:dst.shape[0], 0:dst.shape[1]]).then_inc(stored, 16)
                sp.wait_ge(stored, 16 * len(zeros))
                sp.wait_ge(loaded, 16 * len(loads))

            @block.vector
            def _(dve):
                dve.memset(zero[:], 0.0).then_inc(zeroed, 1)
                for dst, value in fills:
                    dve.memset(dst, value).then_inc(filled, 1)
                dve.wait_ge(filled, len(fills))


def program(nc, x_in, cs, ada_w, ada_b, norm_mix, norm_ffn, w_in, small, sinks, conv_w, mix_norm, w_out, w_ffn,
            final_norm, mats_in, tri_in, ksteps_in, qsteps_in, rope, win, out):
    scratch = lambda name, shape: nc.dram_tensor(name, shape, F32, kind="Internal").ap()
    proj = scratch("proj", (ROWS, IN_W))
    pack = scratch("pack", (TILES, P, T_W))
    feat = scratch("feat", (TILES, P, F_N, P))
    diag = scratch("diag", (2, 4 * TILES, GH, 32, 32))
    inv = scratch("inv", (2, 2, 4 * TILES, GH, 32, 32))
    tot = scratch("tot", (TILES, P, 16))
    swq = scratch("swq", (TILES, P, 4, P))
    swk = scratch("swk", (P, TOK + 2 * P))
    wts = scratch("wts", (TILES, P, 2, 2, P))
    us = scratch("us", (TILES, P, 512))
    with ExitStack() as mem:
        def sb(name, shape):
            return mem.enter_context(nc.sbuf_tensor(name, shape, F32))

        x = sb("x", [P, KC, TOK])
        mats, tri, ksteps, qsteps = sb("mats", [P, 8, P]), sb("tri", [P, 2, HD]), sb("ksteps", [P, 2]), sb("qsteps", [P, 2, P])
        ones, eps = sb("ones", [P, P]), sb("eps", [P, 1])
        mod, amix, affn = sb("mod", [P, NMOD * KC, 2]), sb("amix", [P, KC, 2]), sb("affn", [P, KC, 2])
        pads = [(0, P), (P, P + 1), (R0 + 1 + CTX, R0 + 2 + CTX), (ROWS - P - 1, ROWS - 1), (ROWS - 1, ROWS)]
        begin(nc, [(x[:], x_in), (mats[:], mats_in), (tri[:], tri_in), (ksteps[:], ksteps_in), (qsteps[:], qsteps_in)],
              [proj[a:b, S_V:G_Z] for a, b in pads] + [swk[:, 0:P], swk[:, TOK + P:TOK + 2 * P]],
              [(ones[:], 1.0 / DM), (eps[:], EPS)])
        for layer in range(DEPTH):
            lo = 0 if layer < DEPTH - 1 else CTX
            t0 = lo // P
            modulation(nc, layer, cs, ada_w, ada_b, norm_mix, norm_ffn, mats[:, C_ID, :], mod, amix, affn)
            project(nc, layer, x, w_in, proj, mod, amix, ones, eps)
            prepare(nc, layer, proj, rope, conv_w, small, mats, tri, ksteps, qsteps, pack, feat, diag, tot, swq, swk)
            solve(nc, layer, diag, inv)
            join(nc, layer, pack, inv, wts, us)
            with Stage(nc, f"o{layer}") as so:
                o_ret, o_gdn = so.sb("o_ret", [P, 2, 2, TOK]), so.sb("o_gdn", [P, 2, 2, TOK])
                scan(nc, layer, proj, pack, feat, tot, wts, us, small, mats, o_ret, o_gdn)
                y_hi, y_lo = so.sb("y_hi", [P, KC, TOK], F32R), so.sb("y_lo", [P, KC, TOK], F32R)
                gated(nc, layer, t0, proj, mix_norm, mats, o_ret, o_gdn, y_hi, y_lo, eps)
                window(nc, layer, t0, proj, swq, swk, win, sinks, mats, y_hi, y_lo)
                mixed(nc, layer, lo, x, w_out[layer], mod, y_hi, y_lo)
            ffn(nc, layer, x, lo, w_ffn[layer], mod, affn, ones, eps)
        final(nc, x, final_norm, out, ones, eps)


def ffn_units(w1, w2):
    units = []
    for j0 in range(0, FC, 4):
        js = min(4, FC - j0)
        for j in range(j0, j0 + js):
            for half in range(2):
                c = w1[:, half * DFF + j * P:half * DFF + (j + 1) * P]
                units.append(c.reshape(KC, P, P).transpose(1, 0, 2).reshape(P, DM))
        wide = DM // js
        rows = w2[j0 * P:(j0 + js) * P].reshape(js, P, DM)
        for m in range(0, DM, wide):
            units.append(rows[:, :, m:m + wide].transpose(1, 0, 2).reshape(P, DM))
    return np.stack(units)


def kernel(**inputs):
    import concourse.bacc as bacc
    from concourse.bass_utils import run_bass_kernel_spmd

    a = {k: np.asarray(v) for k, v in inputs.items()}
    feature = lambda v: np.ascontiguousarray(v.reshape(-1, P).T)
    spread = lambda v: np.broadcast_to(v.reshape(1, -1), (P, v.size))
    mats, tri, ksteps, qsteps, rope, win = constants()
    tokens = np.concatenate([a["ctx"][0], a["x"][0]], 0)
    arrays = {
        "x_in": tokens.T.reshape(KC, P, TOK).transpose(1, 0, 2),
        "cs": np.stack([feature(a["c"][0]), feature(a["c_ctx"])], -1),
        "ada_w": a["ada_w"],
        "ada_b": np.broadcast_to(a["ada_b"][:, None], (DEPTH, 2, NMOD * DM)),
        "norm_mix": np.stack([feature(v) for v in a["norm_mix_w"]]),
        "norm_ffn": np.stack([feature(v) for v in a["norm_ffn_w"]]),
        "w_in": a["w_in"],
        "small": np.stack([np.stack([spread(a[n][l]) for n in ("gdn_a_log", "gdn_dt_bias", "ret_rate")], 1) for l in range(DEPTH)]),
        "sinks": np.stack([spread(v) for v in a["swa_sinks"]]),
        "conv_w": np.broadcast_to(a["gdn_conv_w"][:, None], (DEPTH, P, 3, 768)),
        "mix_norm": np.stack([np.concatenate([feature(a["ret_norm_w"][l]), feature(np.tile(a["gdn_norm_w"][l], 4))], 1) for l in range(DEPTH)]),
        "w_out": a["w_out"].reshape(DEPTH, KC, P, KC, P).transpose(0, 3, 2, 1, 4).reshape(DEPTH, KC, P, DM),
        "w_ffn": np.stack([ffn_units(a["w_ffn_in"][l], a["w_ffn_out"][l]) for l in range(DEPTH)]),
        "final_norm": feature(a["final_norm_w"]),
        "mats_in": mats, "tri_in": tri, "ksteps_in": ksteps, "qsteps_in": qsteps, "rope": rope, "win": win,
    }
    arrays = {k: np.ascontiguousarray(v) for k, v in arrays.items()}
    nc = bacc.Bacc("TRN2", target_bir_lowering=False, num_devices=1)
    args = [nc.dram_tensor(k, v.shape, mybir.dt.from_np(v.dtype), kind="ExternalInput").ap() for k, v in arrays.items()]
    args.append(nc.dram_tensor("out", (P, KC, LAT), F32, kind="ExternalOutput").ap())
    program(nc, *args)
    r = run_bass_kernel_spmd(nc, [arrays], core_ids=[0])
    out = r.results[0]["out"]
    return np.ascontiguousarray(out.transpose(1, 0, 2).reshape(DM, LAT).T)[None]
```

```python
from contextlib import ExitStack

import numpy as np

import concourse.bass as bass
from concourse import mybir

ALU = mybir.AluOpType
ACT = mybir.ActivationFunctionType
AX = mybir.AxisListType
F32 = mybir.dt.float32
F32R = mybir.dt.float32r

P = 128
DM = 1024
KC = DM // P
CTX, LAT = 256, 1024
TOK = CTX + LAT
TILES = TOK // P
DEPTH = 2
HD = 64
RH, SH, GH = 4, 8, 4
IN_W = 2832
GROUPS, GW = 6, IN_W // 6
DFF = 2816
FC = DFF // P
NMOD = 6
EPS = 1e-6
NEG = -1e30

R_Q, R_K, R_V, R_G = 0, 256, 512, 768
S_Q, S_K, S_V = 1024, 1536, 1664
G_Q, G_K, G_V, G_Z, G_A, G_B = 1792, 2048, 2304, 2560, 2816, 2824
R0 = P
ROWS = R0 + TOK + 3 + P


def row_of(t):
    return R0 + 1 + t * P + (t >= 2)



def token_slices(lo):
    full = [(0, 256), (256, 512), (768, 512)]
    return full if lo == 0 else full[1:]


class Stage:

    def __init__(self, nc, name):
        self.nc, self.name, self.sems = nc, name, []

    def __enter__(self):
        self.mem = ExitStack()
        return self

    def sb(self, name, shape, dt=F32):
        return self.mem.enter_context(self.nc.sbuf_tensor(f"{self.name}_{name}", shape, dt))

    def ps(self, name, shape, dt=F32):
        return self.mem.enter_context(self.nc.psum_tensor(f"{self.name}_{name}", shape, dt))

    def sem(self, name):
        s = self.mem.enter_context(self.nc.semaphore(f"{self.name}_{name}"))
        self.sems.append(s)
        return s

    def __exit__(self, *a):
        if a[0] is None:
            self.nc.clear_and_free_semaphores(self.sems)
            self.nc.all_engine_barrier()
        self.mem.close()


def modulation(nc, layer, cs, ada_w, ada_b, norm_mix, norm_ffn, ident, mod, amix, affn):
    with Stage(nc, f"ada{layer}") as st:
        sync, scalar, tensor, gpsimd = modulating(nc, st, layer, cs, ada_w, ada_b, norm_mix, norm_ffn, ident, mod, amix, affn)
        with nc.Block() as block:
            block.sync(sync)
            block.scalar(scalar)
            block.tensor(tensor)
            block.gpsimd(gpsimd)


def modulating(nc, st, layer, cs, ada_w, ada_b, norm_mix, norm_ffn, ident, mod, amix, affn):
    NG = NMOD * DM // 512
    c_in = st.sb("m_c_in", [P, KC, 2])
    c_s = st.sb("m_c_s", [P, KC, 2])
    w = [st.sb(f"m_w{u}", [P, KC, 512]) for u in range(2)]
    rows = st.sb("m_rows", [2, NMOD * DM])
    bias = st.sb("m_bias", [P, NMOD * KC])
    product = st.sb("m_product", [P, NMOD * KC, 2])
    nw = st.sb("m_nw", [P, 2, KC])
    acc = [st.ps(f"m_acc{u}", [2, 512]) for u in range(2)]
    cols = st.ps("m_cols", [P, NMOD * KC * 2])
    small_in, w_in0, w_in1 = st.sem("m_small_in"), st.sem("m_w_in0"), st.sem("m_w_in1")
    silu_done, turned, cols_out = st.sem("m_silu_done"), st.sem("m_turned"), st.sem("m_cols_out")
    acc_done = [st.sem(f"m_acc_done{u}") for u in range(2)]
    row_done = [st.sem(f"m_row_done{u}") for u in range(2)]
    mod_done, plus_one, scale_done = st.sem("m_mod_done"), st.sem("m_plus_one"), st.sem("m_scale_done")
    w_in = [w_in0, w_in1]

    def sync(sp):
        sp.dma_start(c_in[:], cs).then_inc(small_in, 16)
        sp.dma_start(bias[:], ada_b[layer]).then_inc(small_in, 16)
        sp.dma_start(nw[:, 0, :], norm_mix[layer]).then_inc(small_in, 16)
        sp.dma_start(nw[:, 1, :], norm_ffn[layer]).then_inc(small_in, 16)
        with sp.Fori(0, NG // 2) as g:
            for u in range(2):
                sp.wait_ge(acc_done[u], g)
                src = ada_w[layer].rearrange("(k p) n -> p k n", p=P)
                sp.dma_start(w[u][:], src[:, :, bass.ds(g * 1024 + u * 512, 512)]).then_inc(w_in[u], 16)

    def scalar(act):
        act.wait_ge(small_in, 64)
        act.activation(c_s[:], c_in[:], ACT.Silu).then_inc(silu_done, 1)
        with act.Fori(0, NG // 2) as g:
            for u in range(2):
                act.wait_ge(acc_done[u], g + 1)
                act.activation(rows[:, bass.ds(g * 1024 + u * 512, 512)], acc[u][:], ACT.Copy).then_inc(row_done[u], 1)
        act.wait_ge(turned, 1)
        act.activation(product[:].rearrange("p m v -> p (m v)"), cols[:], ACT.Copy).then_inc(cols_out, 1)

    def tensor(pe):
        pe.wait_ge(silu_done, 1)
        with pe.Fori(0, NG // 2) as g:
            for u in range(2):
                pe.wait_ge(w_in[u], g * 16 + 16)
                pe.wait_ge(row_done[u], g)
                for k in range(KC):
                    mm = pe.matmul(acc[u][:], c_s[:, k, :], w[u][:, k, :], start=(k == 0), stop=(k == KC - 1))
                mm.then_inc(acc_done[u], 1)
        for u in range(2):
            pe.wait_ge(row_done[u], NG // 2)
        for m in range(NMOD * KC):
            mm = pe.transpose(cols[:, 2 * m:2 * m + 2], rows[:, m * P:(m + 1) * P], ident[0:2, 0:2])
        mm.then_inc(turned, 1)

    def gpsimd(pool):
        pool.wait_ge(small_in, 64)
        pool.wait_ge(cols_out, 1)
        pool.tensor_tensor(mod[:], product[:], bias[:].unsqueeze(2).broadcast_to([P, NMOD * KC, 2]),
                           ALU.add).then_inc(mod_done, 1)
        pool.wait_ge(mod_done, 1)
        for which, out in ((0, amix), (1, affn)):
            sc = mod[:, (3 * which + 1) * KC:(3 * which + 2) * KC, :]
            pool.tensor_scalar(out[:], sc, 1.0, None, ALU.add).then_inc(plus_one, 1)
            pool.wait_ge(plus_one, which + 1)
            pool.tensor_tensor(out[:], out[:], nw[:, which, :].unsqueeze(2).broadcast_to([P, KC, 2]), ALU.mult).then_inc(scale_done, 1)
        pool.wait_ge(scale_done, 2)

    return sync, scalar, tensor, gpsimd


def normed(nc, st, x, scale, mod, shift0, lo, hi_t, lo_t, ones, eps):
    slices = token_slices(lo)
    sq = [st.sb(f"sq{u}", [P, 512]) for u in range(2)]
    inv = [st.sb(f"inv{s}", [P, n]) for s, (t0, n) in enumerate(slices)]
    scaled = [st.sb(f"scaled{u}", [P, 512]) for u in range(2)]
    ms = [st.ps(f"ms{s}", [P, 512]) for s in range(len(slices))]
    squared, summed, rooted, inverted = st.sem("squared"), st.sem("summed"), st.sem("rooted"), st.sem("inverted")
    scaled_s, rounded, h_ready = st.sem("scaled"), st.sem("rounded"), st.sem("h_ready")

    def act_norm(act, between=None):
        for s, (t0, n) in enumerate(slices):
            for k in range(KC):
                i = s * KC + k
                if i >= 2:
                    act.wait_ge(summed, i - 1)
                act.activation(sq[i % 2][:, 0:n], x[:, k, t0:t0 + n], ACT.Square).then_inc(squared, 1)
        for s, (t0, n) in enumerate(slices):
            act.wait_ge(summed, (s + 1) * KC)
            act.activation(inv[s][:], ms[s][:, 0:n], ACT.Sqrt, bias=eps[:]).then_inc(rooted, 1)
        if between:
            between(act)
        for s, (t0, n) in enumerate(slices):
            v = 1 if t0 < CTX else 0
            for k in range(KC):
                act.wait_ge(scaled_s, s * KC + k + 1)
                act.activation(hi_t[:, k, t0:t0 + n], scaled[(s * KC + k) % 2][:, 0:n], ACT.Identity,
                               bias=mod[:, shift0 + k, v:v + 1]).then_inc(rounded, 1)

    def pe_norm(pe):
        for s, (t0, n) in enumerate(slices):
            for k in range(KC):
                pe.wait_ge(squared, s * KC + k + 1)
                pe.matmul(ms[s][:, 0:n], ones[:], sq[(s * KC + k) % 2][:, 0:n], start=(k == 0), stop=(k == KC - 1)).then_inc(summed, 1)

    def dve_norm(dve):
        def scale_one(i):
            s, k = i // KC, i % KC
            t0, n = slices[s]
            v = 1 if t0 < CTX else 0
            if k == 0:
                dve.wait_ge(rooted, s + 1)
                dve.reciprocal(inv[s][:], inv[s][:]).then_inc(inverted, 1)
                dve.wait_ge(inverted, s + 1)
            if i >= 2:
                dve.wait_ge(h_ready, i - 1)
            dve.scalar_tensor_tensor(scaled[i % 2][:, 0:n], x[:, k, t0:t0 + n], scale[:, k, v:v + 1], inv[s][:],
                                     ALU.mult, ALU.mult).then_inc(scaled_s, 1)

        parts = len(slices) * KC
        scale_one(0)
        for i in range(parts):
            s, k = i // KC, i % KC
            t0, n = slices[s]
            v = 1 if t0 < CTX else 0
            if i + 1 < parts:
                scale_one(i + 1)
            dve.wait_ge(rounded, i + 1)
            dve.scalar_tensor_tensor(lo_t[:, k, t0:t0 + n], scaled[i % 2][:, 0:n], mod[:, shift0 + k, v:v + 1],
                                     hi_t[:, k, t0:t0 + n].bitcast(F32), ALU.add, ALU.subtract).then_inc(h_ready, 1)

    return act_norm, pe_norm, dve_norm, h_ready


def project(nc, layer, x, w_in, proj, mod, amix, ones, eps):
    with Stage(nc, f"prj{layer}") as st:
        h_hi = st.sb("h_hi", [P, KC, TOK], F32R)
        h_lo = st.sb("h_lo", [P, KC, TOK], F32R)
        act_norm, pe_norm, dve_norm, h_ready = normed(nc, st, x, amix, mod, 0, 0, h_hi, h_lo, ones, eps)
        raw = st.sb("raw", [P, KC, GW])
        w_hi = st.sb("w_hi", [P, KC, GW], F32R)
        w_lo = st.sb("w_lo", [P, KC, GW], F32R)
        out = st.sb("out", [P, 5, GW])
        acc = [st.ps(f"acc{b}", [P, 512]) for b in range(5)]
        w_landed = [st.sem(f"w_landed{k}") for k in range(KC)]
        w_rounded, w_split, w_used = st.sem("w_rounded"), st.sem("w_split"), st.sem("w_used")
        summed = st.sem("psum_done")
        copied = [st.sem(f"copied{b}") for b in range(5)]
        stored = [st.sem(f"stored{b}") for b in range(5)]
        src = w_in[layer].rearrange("(k p) n -> p k n", p=P)
        with nc.Block() as block:
            @block.sync
            def _(sp):
                with sp.Fori(0, GROUPS) as g:
                    for k in range(KC):
                        sp.wait_ge(w_split, g * KC)
                        sp.dma_start(raw[:, k, :], src[:, k, bass.ds(g * GW, GW)]).then_inc(w_landed[k], 16)

            def split_hi(act, g):
                for k in range(KC):
                    act.wait_ge(w_landed[k], g * 16 + 16)
                    if k < KC - 1:
                        act.wait_ge(w_used, g * (KC - 1) + k + 1)
                    else:
                        act.wait_ge(summed, g * TILES)
                    act.activation(w_hi[:, k, :], raw[:, k, :], ACT.Copy).then_inc(w_rounded, 1)

            def split_lo(dve, g):
                for k in range(KC):
                    dve.wait_ge(w_rounded, g * KC + k + 1)
                    dve.tensor_tensor(w_lo[:, k, :], raw[:, k, :], w_hi[:, k, :].bitcast(F32), ALU.subtract).then_inc(w_split, 1)

            @block.scalar
            def _(act):
                act_norm(act, between=lambda act: split_hi(act, 0))

                def copy(g, t):
                    act.wait_ge(summed, g * TILES + t + 1)
                    act.wait_ge(stored[t % 5], (g * 2 + t // 5) * 16)
                    act.activation(out[:, t % 5, :], acc[t % 5][:, 0:GW], ACT.Copy).then_inc(copied[t % 5], 1)

                with act.Fori(0, GROUPS - 1) as g:
                    for t in range(0, TILES, 2):
                        copy(g, t)
                    split_hi(act, g + 1)
                for t in range(0, TILES, 2):
                    copy(GROUPS - 1, t)

            @block.vector
            def _(dve):
                split_lo(dve, 0)
                dve_norm(dve)

                def copy(g, t):
                    dve.wait_ge(summed, g * TILES + t + 1)
                    dve.wait_ge(stored[t % 5], (g * 2 + t // 5) * 16)
                    dve.tensor_copy(out[:, t % 5, :], acc[t % 5][:, 0:GW]).then_inc(copied[t % 5], 1)

                with dve.Fori(0, GROUPS - 1) as g:
                    for t in range(1, TILES - 1, 2):
                        copy(g, t)
                    split_lo(dve, g + 1)
                    copy(g, TILES - 1)
                for t in range(1, TILES, 2):
                    copy(GROUPS - 1, t)

            @block.tensor
            def _(pe):
                pe.sem_inc(w_used, KC - 1)
                pe_norm(pe)
                with pe.Fori(0, GROUPS) as g:
                    for t in range(TILES):
                        tok = slice(t * P, (t + 1) * P)
                        pe.wait_ge(h_ready, (1 + sum(t * P >= t0 + n for t0, n in token_slices(0))) * KC)
                        pe.wait_ge(copied[t % 5], g * 2 + t // 5)
                        for k in range(KC):
                            if t == 0:
                                pe.wait_ge(w_split, g * KC + k + 1)
                            for a, b, s in ((h_hi, w_hi, 0), (h_lo, w_hi, 1), (h_hi, w_lo, 2)):
                                mm = pe.matmul(acc[t % 5][:, 0:GW], a[:, k, tok], b[:, k, :],
                                               start=(k == 0 and s == 0), stop=(k == KC - 1 and s == 2))
                            if t == TILES - 1 and k < KC - 1:
                                mm.then_inc(w_used, 1)
                        mm.then_inc(summed, 1)

            @block.gpsimd
            def _(pool):
                with pool.Fori(0, GROUPS) as g:
                    for t in range(TILES):
                        pool.wait_ge(copied[t % 5], g * 2 + t // 5 + 1)
                        row = row_of(t)
                        pool.dma_start(proj[row:row + P, bass.ds(g * GW, GW)], out[:, t % 5, :]).then_inc(stored[t % 5], 16)
                for b in range(5):
                    pool.wait_ge(stored[b], GROUPS * 2 * 16)


class WeightUnits:

    def __init__(self, st, units):
        self.units = units
        self.raw = [st.sb(f"raw{u}", [P, DM]) for u in range(2)]
        self.hi = [st.sb(f"w_hi{u}", [P, DM], F32R) for u in range(2)]
        self.lo = [st.sb(f"w_lo{u}", [P, DM], F32R) for u in range(2)]
        self.landed = [st.sem(f"w_landed{u}") for u in range(2)]
        self.rounded = [st.sem(f"w_rounded{u}") for u in range(2)]
        self.ready = [st.sem(f"w_ready{u}") for u in range(2)]
        self.used = [st.sem(f"w_used{u}") for u in range(2)]

    def load_all(self, sp, turns):
        with sp.Fori(0, turns) as n:
            for u in range(2):
                sp.wait_ge(self.ready[u], n)
                sp.dma_start(self.raw[u][:], self.units[bass.ds(n * 2 + u, 1)].rearrange("a p n -> (a p) n")).then_inc(self.landed[u], 16)

    def round(self, act, u, n):
        act.wait_ge(self.landed[u], n * 16 + 16)
        act.wait_ge(self.used[u], n)
        act.activation(self.hi[u][:], self.raw[u][:], ACT.Copy).then_inc(self.rounded[u], 1)

    def rest(self, dve, u, n):
        dve.wait_ge(self.rounded[u], n + 1)
        dve.tensor_tensor(self.lo[u][:], self.raw[u][:], self.hi[u][:].bitcast(F32), ALU.subtract).then_inc(self.ready[u], 1)


def three_passes(pe, out, w_hi, w_lo, b_hi, b_lo, first, last):
    pe.matmul(out, w_hi, b_hi, start=first, stop=False)
    pe.matmul(out, w_hi, b_lo, start=False, stop=False)
    return pe.matmul(out, w_lo, b_hi, start=False, stop=last)


def ffn(nc, layer, x, lo, units, mod, affn, ones, eps):
    J = 4
    NFULL, REST = FC // J, FC % J
    TURNS = 6
    SETS = 8
    LAST, LSET = NFULL * TURNS, NFULL * SETS
    slices = token_slices(lo)
    with Stage(nc, f"ffn{layer}") as st:
        h_hi = st.sb("h_hi", [P, KC, TOK], F32R)
        h_lo = st.sb("h_lo", [P, KC, TOK], F32R)
        with Stage(nc, f"ffn{layer}n") as sn:
            act_norm, pe_norm, dve_norm, h_ready = normed(nc, sn, x, affn, mod, 3 * KC, lo, h_hi, h_lo, ones, eps)
            with nc.Block() as block:
                block.scalar(act_norm)
                block.tensor(pe_norm)
                block.vector(dve_norm)
        a_hi = st.sb("a_hi", [P, J, TOK], F32R)
        a_lo = st.sb("a_lo", [P, J, TOK], F32R)
        sil = st.sb("sil", [P, TOK])
        prod = st.sb("prod", [P, TOK])
        bank = [[st.ps(f"bank{i}{s}", [P, 512]) for s in range(len(slices))] for i in range(2)]
        w = WeightUnits(st, units)
        full = [[st.sem(f"full{i}{s}") for s in range(len(slices))] for i in range(2)]
        free = [[st.sem(f"free{i}{s}") for s in range(len(slices))] for i in range(2)]
        a_rounded, a_ready = st.sem("a_rounded"), st.sem("a_ready")
        NS = len(slices)

        def pe_up(pe, n, b):
            for u in range(2):
                pe.wait_ge(w.ready[u], n + 1)
                for s, (t0, ln) in enumerate(slices):
                    pe.wait_ge(free[u][s], b)
                    for k in range(KC):
                        f = slice(k * P, (k + 1) * P)
                        mm = three_passes(pe, bank[u][s][:, 0:ln], w.hi[u][:, f], w.lo[u][:, f],
                                          h_hi[:, k, t0:t0 + ln], h_lo[:, k, t0:t0 + ln], k == 0, k == KC - 1)
                    mm.then_inc(full[u][s], 1)
                pe.wait_ge(full[u][NS - 1], b + 1)
                pe.sem_inc(w.used[u], 1)

        def act_up(act, j, c, n, b, before):
            for s, (t0, ln) in enumerate(slices):
                act.wait_ge(full[0][s], b + 1)
                act.wait_ge(free[1][s], b)
                act.activation(sil[:, t0:t0 + ln], bank[0][s][:, 0:ln], ACT.Silu).then_inc(free[0][s], 1)
            w.round(act, 0, n + 1)
            act.wait_ge(w.used[1], before)
            for s, (t0, ln) in enumerate(slices):
                act.wait_ge(free[1][s], b + 1)
                act.activation(a_hi[:, j, t0:t0 + ln], prod[:, t0:t0 + ln], ACT.Copy).then_inc(a_rounded, 1)
            w.round(act, 1, n + 1)

        def dve_up(dve, j, c, n, b):
            w.rest(dve, 0, n + 1)

            def rest(s):
                t0, ln = slices[s]
                dve.wait_ge(a_rounded, c * NS + s + 1)
                dve.tensor_tensor(a_lo[:, j, t0:t0 + ln], prod[:, t0:t0 + ln], a_hi[:, j, t0:t0 + ln].bitcast(F32),
                                  ALU.subtract).then_inc(a_ready, 1)

            for s, (t0, ln) in enumerate(slices):
                dve.wait_ge(a_ready, c * NS)
                dve.wait_ge(full[1][s], b + 1)
                dve.wait_ge(free[0][s], b + 1)
                dve.tensor_tensor(prod[:, t0:t0 + ln], sil[:, t0:t0 + ln], bank[1][s][:, 0:ln], ALU.mult).then_inc(free[1][s], 1)
                if s >= 1:
                    rest(s - 1)
            rest(NS - 1)
            w.rest(dve, 1, n + 1)

        def pe_down(pe, n, b, js, each):
            for u in range(2):
                pe.wait_ge(w.ready[u], n + 1)
                wide = each * P
                for e in range(each):
                    i, use = e % 2, b + u * (each // 2) + e // 2
                    for s, (t0, ln) in enumerate(slices):
                        pe.wait_ge(free[i][s], use)
                        for j in range(js):
                            f = slice(j * wide + e * P, j * wide + (e + 1) * P)
                            mm = three_passes(pe, bank[i][s][:, 0:ln], w.hi[u][:, f], w.lo[u][:, f],
                                              a_hi[:, j, t0:t0 + ln], a_lo[:, j, t0:t0 + ln], j == 0, j == js - 1)
                        mm.then_inc(full[i][s], 1)
                pe.wait_ge(full[1][NS - 1], b + (u + 1) * (each // 2))
                pe.sem_inc(w.used[u], 1)

        def dve_down(dve, n, b, m0, each, more):
            for u in range(2):
                for e in range(each):
                    i, use = e % 2, b + u * (each // 2) + e // 2
                    m = m0 + (u * each + e)
                    for s, (t0, ln) in enumerate(slices):
                        v = 1 if t0 < CTX else 0
                        dve.wait_ge(full[i][s], use + 1)
                        xs = x[:, bass.ds(m, 1), t0:t0 + ln].rearrange("p a n -> p (a n)")
                        dve.scalar_tensor_tensor(xs, bank[i][s][:, 0:ln], mod[:, bass.ds(m + 5 * KC, 1), v], xs,
                                                 ALU.mult, ALU.add).then_inc(free[i][s], 1)
                if more:
                    w.rest(dve, u, n + 1)

        def act_down(act, n, more):
            if more:
                for u in range(2):
                    w.round(act, u, n + 1)

        with nc.Block() as block:
            @block.sync
            def _(sp):
                w.load_all(sp, LAST + REST + 1)

            @block.scalar
            def _(act):
                for u in range(2):
                    w.round(act, u, 0)
                with act.Fori(0, NFULL) as g:
                    with act.Fori(0, J) as j:
                        act_up(act, bass.ds(j, 1), g * J + j, g * TURNS + j, g * SETS + j, g * TURNS)
                    with act.Fori(0, 2) as q:
                        act_down(act, g * TURNS + J + q, True)
                for j in range(REST):
                    act_up(act, bass.ds(j, 1), NFULL * J + j, LAST + j, LSET + j, LAST)

            @block.vector
            def _(dve):
                for u in range(2):
                    w.rest(dve, u, 0)
                with dve.Fori(0, NFULL) as g:
                    with dve.Fori(0, J) as j:
                        dve_up(dve, bass.ds(j, 1), g * J + j, g * TURNS + j, g * SETS + j)
                    with dve.Fori(0, 2) as q:
                        dve_down(dve, g * TURNS + J + q, g * SETS + J + q * 2, q * 4, 2, True)
                for j in range(REST):
                    dve_up(dve, bass.ds(j, 1), NFULL * J + j, LAST + j, LSET + j)
                dve_down(dve, LAST + REST, LSET + REST, 0, 4, False)

            @block.tensor
            def _(pe):
                with pe.Fori(0, NFULL) as g:
                    with pe.Fori(0, J) as j:
                        pe_up(pe, g * TURNS + j, g * SETS + j)
                    with pe.Fori(0, 2) as q:
                        pe.wait_ge(a_ready, (g + 1) * (J * NS))
                        pe_down(pe, g * TURNS + J + q, g * SETS + J + q * 2, J, 2)
                for j in range(REST):
                    pe_up(pe, LAST + j, LSET + j)
                pe.wait_ge(a_ready, FC * NS)
                pe_down(pe, LAST + REST, LSET + REST, REST, 4)


T_RK, T_RV, T_NK, T_LT, T_GV = 0, 256, 768, 1280, 1792
T_D, T_KT, T_AT = 2048, 0, 256
T_W = 3072
F_RQ, F_RK = 0, 2
F_D, F_DN, F_RQD, F_GQD, F_GW = 4, 6, 0, 2, 4
F_N = F_D + 2 * F_DN
C_ID, C_LE, C_GE, C_GT, C_LT, C_C0, C_C1, C_DIST = range(8)


def constants():
    l, i = np.arange(P)[:, None], np.arange(P)[None, :]
    same = (l // 64) == (i // 64)
    mats = [l == i, same & (l <= i), same & (l >= i), same & (l > i), same & (l < i),
            (l < 64) & (i >= 0), (l >= 64) & (i >= 0)]
    mats = [m.astype(np.float32) for m in mats] + [(i - l).astype(np.float32)]
    mats = np.stack(mats, 1)
    lc, ic = (np.arange(P) % 64)[:, None], np.arange(64)[None, :]
    tri = np.stack([lc <= ic, lc >= ic], 1).astype(np.float32)
    ksteps = np.stack([P - 1.0 - np.arange(P), np.arange(P) + 0.0], 1).astype(np.float32)
    qsteps = np.broadcast_to(np.stack([np.arange(P) + 1.0, P - np.arange(P) + 0.0]), (P, 2, P)).astype(np.float32)
    rope = np.zeros((TILES, P, 2, 64), np.float32)
    rope[:2, :, 0] = 1.0
    pos = np.arange(LAT)
    freqs = np.float32(10000.0) ** (-np.arange(16, dtype=np.float32) / np.float32(16))
    for axis, at in enumerate((pos // 64, pos % 64)):
        ang = (at.astype(np.float32)[:, None] * freqs).reshape(8, P, 16)
        c, s = np.cos(ang), np.sin(ang)
        rope[2:, :, 0, 32 * axis:32 * axis + 32] = np.concatenate([c, c], -1)
        rope[2:, :, 1, 32 * axis:32 * axis + 32] = np.concatenate([-s, s], -1)
    q, k = np.arange(P)[:, None], np.arange(3 * P)[None, :] - P
    win = np.zeros((TILES, P, 3 * P), np.float32)
    win[:2] = NEG
    for t in range(2, TILES):
        at = (t - 2) * P + k
        win[t] = np.where((np.abs(q - k) <= 128) & (at >= 0) & (at < LAT), 0.0, NEG)
    return mats, tri, ksteps, qsteps, rope, win


def signals(st, names):
    return {n: st.sem(n) for n in names.split()}


def settle(eng, passed):
    eng.sem_inc(passed, 1)


def prepare(nc, layer, proj, rope, conv_w, small, mats, tri, ksteps, qsteps, pack, feat, diag, tot, swq, swk):
    with Stage(nc, f"pre{layer}") as st:
        pr = st.sb("pr", [P, IN_W])
        before, after = st.sb("before", [P, 768]), st.sb("after", [P, 768])
        rp = st.sb("rp", [P, 2, 64])
        cw = st.sb("cw", [P, 3, 768])
        sm = st.sb("sm", [P, 3, 8])
        al, dtb, rate = sm[:, 0, :], sm[:, 1, :], sm[:, 2, :]
        lg = st.sb("lg", [P, 8])
        kd = st.sb("kd", [P, 2, RH])
        qd = st.sb("qd", [P, 2, 2, P])
        hot, swp = st.sb("hot", [P, 1152]), st.sb("swp", [P, 1152])
        hp = st.sb("hp", [P, 512])
        c0, c1, c2 = st.sb("c0", [P, 768]), st.sb("c1", [P, 768]), st.sb("c2", [P, 768])
        cv = st.sb("cv", [P, 768])
        sq = st.sb("sq", [P, 512])
        ss, rt, rn = st.sb("ss", [P, 8]), st.sb("rt", [P, 8]), st.sb("rn", [P, 8])
        xa, xn, xe, xl, g = (st.sb(n, [P, 8]) for n in ("xa", "xn", "xe", "xl", "g"))
        bm, be, b1, beta = (st.sb(n, [P, 8]) for n in ("bm", "be", "b1", "beta"))
        es = st.sb("es", [P, 32])
        nt, kt = st.sb("nt", [P, 8]), st.sb("kt", [P, 8])
        gu, mb, e1, de = (st.sb(n, [P, 2, 4, 64]) for n in ("gu", "mb", "e1", "de"))
        kh, qh = st.sb("kh", [P, 256]), st.sb("qh", [P, 256])
        qg = st.sb("qg", [P, 2, 4, 64])
        khT, qhT = st.sb("khT", [P, 2, P]), st.sb("qhT", [P, 2, P])
        pk = st.sb("pk", [P, T_W])
        ft = st.sb("ft", [P, F_N, P])
        sqT, skT = st.sb("sqT", [P, 4, P]), st.sb("skT", [P, P])
        one, eps = st.sb("one", [P, 1]), st.sb("eps", [P, 1])
        b_r, b_q, b_k, b_g, b_d, b_s, b_D, b_h = [st.ps(f"b_{n}", [P, 512]) for n in "rqkgdsDh"]
        s = signals(st, """set_in in_main in_side const expa lnready lgn expo decays alneg
            xa xn xe xl sp g bm be b1 beta gu sums es nt kt dsum e1 mb de c0 c1 c2 ca cb cv sq ss rt rn
            kh qh qg rot swapped rotated rk gv turned_r turned_q turned_k turned_g turned_d rv
            ftr ftf ftb ftd sqT skT khT qhT prod_e prod_o lt at nk ktp
            pe_passed sp_passed o_pack o_feat o_tot o_diag o_swq o_swk""")
        mat = lambda m: mats[:, m, :]
        B4 = [P, 2, 4, 64]

        def heads(ap, n):
            return ap.rearrange("p (h e) -> p h e", h=n)

        def per_head(ap8):
            return heads(ap8, 2).unsqueeze(3).broadcast_to(B4)

        def over_dirs(ap256):
            return heads(ap256, 4).unsqueeze(1).broadcast_to(B4)

        def packed(col, step=256):
            base = col // (2 * step) * (2 * step) if step > 256 else col
            both = pk[:, base:base + 2 * step].rearrange("p (a n) -> p a n", a=2)[:, :, col - base:col - base + 256]
            return both.rearrange("p a (h n) -> p a h n", h=4)

        with nc.Block() as block:
            @block.sync
            def _(sp):
                sp.dma_start(cw[:], conv_w[layer]).then_inc(s["set_in"], 16)
                sp.dma_start(sm[:], small[layer]).then_inc(s["set_in"], 16)

                def loads(t, row):
                    sp.wait_ge(s["swapped"], t * 8)
                    settle(sp, s["sp_passed"])
                    for q in (s["c0"], s["c2"], s["c1"], s["rot"], s["xa"], s["bm"], s["rv"]):
                        sp.wait_ge(q, t)
                    settle(sp, s["sp_passed"])
                    sp.dma_start(pr[:], proj[bass.ds(row, P), :]).then_inc(s["in_main"], 16)
                    sp.dma_start(rp[:], rope[bass.ds(t, 1)].rearrange("a p c n -> (a p) c n")).then_inc(s["in_main"], 16)
                    sp.dma_start(before[:], proj[bass.ds(row - 1, P), G_Q:G_Q + 768]).then_inc(s["in_side"], 16)
                    sp.dma_start(after[:], proj[bass.ds(row + 1, P), G_Q:G_Q + 768]).then_inc(s["in_side"], 16)

                def stores(t):
                    def got(*q):
                        for x in q:
                            sp.wait_ge(x, t + 1)
                        settle(sp, s["sp_passed"])

                    got(s["es"])
                    sp.dma_start(tot[bass.ds(t, 1)].rearrange("a p n -> (a p) n"), es[:, 16:32]).then_inc(s["o_tot"], 16)
                    got(s["sqT"], s["skT"])
                    sp.dma_start(swq[bass.ds(t, 1)].rearrange("a p c n -> (a p) c n"), sqT[:]).then_inc(s["o_swq"], 16)
                    sp.dma_start(swk[:, bass.ds(t * P + P, P)], skT[:]).then_inc(s["o_swk"], 16)
                    got(s["rk"], s["rv"], s["gv"], s["nk"], s["ktp"], s["lt"], s["at"])
                    sp.dma_start(pack[bass.ds(t, 1)].rearrange("a p n -> (a p) n"), pk[:]).then_inc(s["o_pack"], 16)
                    lt = pk[:, T_LT:T_LT + 512].rearrange("p (h i) -> p h i", h=8)
                    for b in range(4):
                        for d in range(2):
                            sp.dma_start(diag[d, bass.ds(t * 4 + b, 1)].rearrange("a h j i -> (a j) h i"),
                                         lt[32 * b:32 * b + 32, 4 * d:4 * d + 4, 32 * (b % 2):32 * (b % 2) + 32]).then_inc(s["o_diag"], 16)
                    sp.wait_ge(s["ftr"], t + 1)
                    settle(sp, s["sp_passed"])
                    got(s["ftf"], s["ftb"], s["ftd"])
                    for f0, f1 in ((0, F_D + F_GW), (F_D + F_DN, F_N - 2)):
                        sp.dma_start(feat[bass.ds(t, 1)].rearrange("a p f n -> (a p) f n")[:, f0:f1], ft[:, f0:f1]).then_inc(s["o_feat"], 16)

                sp.dma_start(pr[:], proj[row_of(0):row_of(0) + P, :]).then_inc(s["in_main"], 16)
                sp.dma_start(rp[:], rope[0]).then_inc(s["in_main"], 16)
                sp.dma_start(before[:], proj[row_of(0) - 1:row_of(0) - 1 + P, G_Q:G_Q + 768]).then_inc(s["in_side"], 16)
                sp.dma_start(after[:], proj[row_of(0) + 1:row_of(0) + 1 + P, G_Q:G_Q + 768]).then_inc(s["in_side"], 16)
                with sp.Fori(0, 1) as t:
                    loads(t + 1, t * P + row_of(1))
                    stores(t)
                with sp.Fori(1, TILES - 1) as t:
                    loads(t + 1, t * P + (row_of(2) - P))
                    stores(t)
                with sp.Fori(TILES - 1, TILES) as t:
                    stores(t)
                for q, n in ((s["o_tot"], 1), (s["o_swq"], 1), (s["o_swk"], 1), (s["o_pack"], 1), (s["o_feat"], 2), (s["o_diag"], 8)):
                    sp.wait_ge(q, TILES * 16 * n)

            @block.scalar
            def _(act):
                act.wait_ge(s["set_in"], 32)
                act.wait_ge(s["const"], 2)
                act.activation(al, al, ACT.Exp).then_inc(s["expa"], 1)
                act.activation(lg[:], rate, ACT.Exp, scale=-float(np.log(2.0))).then_inc(s["lnready"], 1)
                act.wait_ge(s["lnready"], 1)
                act.activation(lg[:], lg[:], ACT.Ln, scale=-1.0, bias=one[:]).then_inc(s["lgn"], 1)
                act.wait_ge(s["expo"], 9)
                act.activation(kd[:], kd[:], ACT.Exp).then_inc(s["decays"], 1)
                act.activation(qd[:], qd[:], ACT.Exp).then_inc(s["decays"], 1)
                with act.Fori(0, TILES) as t:
                    def got(*q):
                        for x in q:
                            act.wait_ge(x, t + 1)

                    def spent(*q):
                        for x in q:
                            act.wait_ge(x, t)

                    got(s["xn"]); spent(s["xl"])
                    act.activation(xe[:], xn[:], ACT.Exp).then_inc(s["xe"], 1)
                    got(s["bm"]); spent(s["b1"])
                    act.activation(be[:], bm[:], ACT.Exp, scale=-1.0).then_inc(s["be"], 1)
                    got(s["xe"]); spent(s["sp"])
                    act.activation(xl[:], xe[:], ACT.Ln, bias=one[:]).then_inc(s["xl"], 1)
                    got(s["sums"]); spent(s["nt"], s["kt"], s["qg"]); act.wait_ge(s["o_tot"], t * 16)
                    act.activation(es[:], b_s[:, 0:32], ACT.Exp).then_inc(s["es"], 1)
                    got(s["dsum"]); spent(s["de"])
                    act.activation(e1[:].rearrange("p a h n -> p (a h n)"), b_D[:], ACT.Exp).then_inc(s["e1"], 1)
                    got(s["cb"]); spent(s["sq"], s["kh"], s["qh"], s["gv"])
                    act.activation(cv[:], c1[:], ACT.Silu).then_inc(s["cv"], 1)
                    act.wait_ge(s["in_main"], t * 32 + 32); act.wait_ge(s["o_pack"], t * 16)
                    act.activation(pk[:, T_RV:T_RV + 256], pr[:, R_V:R_V + 256], ACT.Copy).then_inc(s["rv"], 1)
                    got(s["ss"]); spent(s["rn"])
                    act.activation(rt[:], ss[:], ACT.Sqrt, bias=eps[:]).then_inc(s["rt"], 1)
                    got(s["turned_q"]); act.wait_ge(s["o_swq"], t * 16)
                    act.activation(sqT[:].rearrange("p a n -> p (a n)"), b_q[:], ACT.Copy, scale=0.125).then_inc(s["sqT"], 1)
                    got(s["turned_k"]); act.wait_ge(s["o_swk"], t * 16)
                    act.activation(skT[:], b_k[:, 0:P], ACT.Copy).then_inc(s["skT"], 1)
                    got(s["turned_r"]); act.wait_ge(s["o_feat"], t * 32)
                    act.activation(ft[:, F_RQ:F_RQ + 4, :].rearrange("p a n -> p (a n)"), b_r[:], ACT.Copy).then_inc(s["ftr"], 1)
                    got(s["turned_g"]); spent(s["prod_e"], s["prod_o"])
                    act.activation(khT[:].rearrange("p a n -> p (a n)"), b_g[:, 0:256], ACT.Copy).then_inc(s["khT"], 1)
                    act.activation(qhT[:].rearrange("p a n -> p (a n)"), b_g[:, 256:512], ACT.Copy).then_inc(s["qhT"], 1)
                    got(s["turned_d"])
                    act.activation(ft[:, F_D:F_N, :].rearrange("p (d a) n -> p d a n", d=2)[:, :, F_GQD:F_GQD + 2, :],
                                   b_d[:].rearrange("p (d a n) -> p d a n", d=2, a=2), ACT.Copy).then_inc(s["ftd"], 1)

            @block.gpsimd
            def _(pool):
                pool.memset(one[:], 1.0).then_inc(s["const"], 1)
                pool.memset(eps[:], EPS).then_inc(s["const"], 1)
                pool.wait_ge(s["set_in"], 32)
                with pool.Fori(0, TILES) as t:
                    def got(*q):
                        for x in q:
                            pool.wait_ge(x, t + 1)

                    def spent(*q):
                        for x in q:
                            pool.wait_ge(x, t)

                    pool.wait_ge(s["in_side"], t * 32 + 32); spent(s["ca"])
                    pool.tensor_tensor(c0[:], before[:], cw[:, 0, :], ALU.mult).then_inc(s["c0"], 1)
                    spent(s["cb"])
                    pool.tensor_tensor(c2[:], after[:], cw[:, 2, :], ALU.mult).then_inc(s["c2"], 1)
                    pool.wait_ge(s["in_main"], t * 32 + 32); spent(s["rotated"])
                    for base, n, at in ((R_Q, 8, 0), (S_Q, 10, 512)):
                        src = pr[:, base:base + n * 64].rearrange("p (h a u f) -> p h a u f", h=n, a=2, u=2)
                        dst = swp[:, at:at + n * 64].rearrange("p (h a u f) -> p h a u f", h=n, a=2, u=2)
                        for half in range(2):
                            for axis in range(2):
                                sn = rp[:, 1, 32 * axis + 16 * half:32 * axis + 16 * half + 16].unsqueeze(1).broadcast_to([P, n, 16])
                                pool.tensor_tensor(dst[:, :, axis, half, :], src[:, :, axis, 1 - half, :], sn, ALU.mult).then_inc(s["swapped"], 1)
                    got(s["cv"]); spent(s["ss"])
                    pool.tensor_tensor(sq[:], cv[:, 0:512], cv[:, 0:512], ALU.mult).then_inc(s["sq"], 1)
                    got(s["beta"]); spent(s["de"])
                    pool.tensor_tensor(mb[:], tri[:].unsqueeze(2).broadcast_to(B4), per_head(beta[:]), ALU.mult).then_inc(s["mb"], 1)
                    got(s["kh"], s["nt"], s["kt"]); pool.wait_ge(s["o_pack"], t * 16)
                    pool.tensor_tensor(packed(T_NK), over_dirs(kh[:]), per_head(nt[:]), ALU.mult).then_inc(s["nk"], 1)
                    pool.tensor_tensor(packed(T_D + T_KT, 512), over_dirs(kh[:]), per_head(kt[:]), ALU.mult).then_inc(s["ktp"], 1)

            @block.vector
            def _(dve):
                dve.wait_ge(s["expa"], 1)
                dve.tensor_scalar(al, al, -1.0, None, ALU.mult).then_inc(s["alneg"], 1)
                dve.wait_ge(s["lgn"], 1)
                dve.tensor_tensor(kd[:], heads(lg[:], 2), ksteps[:].unsqueeze(2).broadcast_to([P, 2, RH]), ALU.mult).then_inc(s["expo"], 1)
                for h in range(RH):
                    half = slice(64 * (h % 2), 64 * (h % 2) + 64)
                    for d in range(2):
                        dve.tensor_scalar(qd[half, d, h // 2, :], qsteps[half, d, :], lg[half, 4 * d + h:4 * d + h + 1], None,
                                          ALU.mult).then_inc(s["expo"], 1)
                dve.wait_ge(s["decays"], 2)
                dve.wait_ge(s["alneg"], 1)
                with dve.Fori(0, TILES) as t:
                    def got(*q):
                        for x in q:
                            dve.wait_ge(x, t + 1)

                    def spent(*q):
                        for x in q:
                            dve.wait_ge(x, t)

                    dve.wait_ge(s["in_main"], t * 32 + 32)
                    spent(s["sp"])
                    dve.tensor_tensor(xa[:], pr[:, G_A:G_A + 8], dtb, ALU.add).then_inc(s["xa"], 1)
                    spent(s["be"])
                    dve.tensor_scalar(bm[:], pr[:, G_B:G_B + 8], -80.0, None, ALU.max).then_inc(s["bm"], 1)
                    got(s["xa"]); spent(s["xe"])
                    dve.scalar_tensor_tensor(xn[:], xa[:], -1.0, xa[:], ALU.mult, ALU.min).then_inc(s["xn"], 1)
                    got(s["be"]); spent(s["beta"])
                    dve.tensor_scalar(b1[:], be[:], 1.0, None, ALU.add).then_inc(s["b1"], 1)
                    got(s["b1"]); spent(s["mb"], s["kt"])
                    dve.reciprocal(beta[:], b1[:]).then_inc(s["beta"], 1)
                    got(s["xl"])
                    dve.scalar_tensor_tensor(xl[:], xa[:], 0.0, xl[:], ALU.max, ALU.add).then_inc(s["sp"], 1)
                    got(s["sp"]); spent(s["gu"], s["sums"])
                    dve.tensor_tensor(g[:], xl[:], al, ALU.mult).then_inc(s["g"], 1)
                    got(s["g"]); spent(s["dsum"])
                    dve.tensor_tensor(gu[:], tri[:].unsqueeze(2).broadcast_to(B4), per_head(g[:]), ALU.mult).then_inc(s["gu"], 1)
                    dve.wait_ge(s["turned_r"], t); dve.wait_ge(s["turned_q"], t); dve.wait_ge(s["turned_k"], t)
                    spent(s["rk"])
                    cos = lambda n: rp[:, 0, :].unsqueeze(1).broadcast_to([P, n, 64])
                    dve.tensor_tensor(heads(hot[:, 0:512], 8), heads(pr[:, R_Q:R_Q + 512], 8), cos(8), ALU.mult)
                    dve.tensor_tensor(heads(hot[:, 512:1152], 10), heads(pr[:, S_Q:S_Q + 640], 10), cos(10), ALU.mult).then_inc(s["rot"], 1)
                    got(s["rot"]); dve.wait_ge(s["swapped"], t * 8 + 8)
                    dve.tensor_tensor(hot[:, 0:512], hot[:, 0:512], swp[:, 0:512], ALU.add)
                    dve.tensor_tensor(hot[:, 1024:1152], hot[:, 1024:1152], swp[:, 1024:1152], ALU.add)
                    side = lambda ap: ap[:, 512:1024].rearrange("p (u c n) -> p u c n", u=2, c=4)
                    dve.tensor_tensor(hp[:].rearrange("p (c u n) -> p u c n", c=4, u=2), side(hot), side(swp), ALU.add).then_inc(s["rotated"], 1)
                    spent(s["cv"])
                    dve.tensor_tensor(c1[:], pr[:, G_Q:G_Q + 768], cw[:, 1, :], ALU.mult).then_inc(s["c1"], 1)
                    got(s["c1"], s["c0"])
                    dve.tensor_tensor(c1[:], c1[:], c0[:], ALU.add).then_inc(s["ca"], 1)
                    got(s["ca"], s["c2"])
                    dve.tensor_tensor(c1[:], c1[:], c2[:], ALU.add).then_inc(s["cb"], 1)
                    got(s["rotated"]); dve.wait_ge(s["o_pack"], t * 16); dve.wait_ge(s["o_diag"], t * 128)
                    dve.tensor_tensor(packed(T_RK, 512), over_dirs(hot[:, 256:512]), kd[:].unsqueeze(3).broadcast_to(B4), ALU.mult).then_inc(s["rk"], 1)
                    got(s["sq"]); spent(s["rt"])
                    dve.tensor_reduce(ss[:], heads(sq[:], 8), AX.X, ALU.add).then_inc(s["ss"], 1)
                    got(s["rt"]); spent(s["kh"], s["qh"])
                    dve.reciprocal(rn[:], rt[:]).then_inc(s["rn"], 1)
                    got(s["rn"]); spent(s["turned_g"], s["nk"], s["ktp"])
                    dve.tensor_tensor(heads(kh[:], 4), heads(cv[:, 256:512], 4), rn[:, 4:8].unsqueeze(2).broadcast_to([P, 4, 64]), ALU.mult).then_inc(s["kh"], 1)
                    spent(s["qg"])
                    dve.scalar_tensor_tensor(heads(qh[:], 4), heads(cv[:, 0:256], 4), 0.125, rn[:, 0:4].unsqueeze(2).broadcast_to([P, 4, 64]),
                                             ALU.mult, ALU.mult).then_inc(s["qh"], 1)
                    dve.tensor_copy(pk[:, T_GV:T_GV + 256], cv[:, 512:768]).then_inc(s["gv"], 1)
                    got(s["es"]); spent(s["nk"])
                    dve.tensor_scalar(nt[:], es[:, 0:8], -1.0, None, ALU.mult).then_inc(s["nt"], 1)
                    spent(s["ktp"])
                    dve.tensor_tensor(kt[:], es[:, 8:16], beta[:], ALU.mult).then_inc(s["kt"], 1)
                    got(s["qh"]); spent(s["turned_d"])
                    dve.tensor_tensor(qg[:], over_dirs(qh[:]), per_head(es[:, 0:8]), ALU.mult).then_inc(s["qg"], 1)
                    dve.wait_ge(s["ftr"], t + 1); dve.wait_ge(s["o_feat"], t * 32)
                    for d, col, q in ((0, F_D + F_RQD, s["ftf"]), (1, F_D + F_DN + F_RQD, s["ftb"])):
                        dve.tensor_tensor(ft[:, col:col + 2, :], b_r[:, 0:256].rearrange("p (a n) -> p a n", a=2), qd[:, d, :, :], ALU.mult).then_inc(q, 1)
                    got(s["e1"], s["mb"]); spent(s["lt"], s["at"])
                    dve.tensor_tensor(de[:], e1[:], mb[:], ALU.mult).then_inc(s["de"], 1)
                    got(s["de"], s["prod_e"], s["prod_o"])
                    for col, step, q, o in ((T_LT, 256, s["lt"], 0), (T_D + T_AT, 512, s["at"], 128)):
                        for d in range(2):
                            for odd, bank in ((0, b_h), (1, b_k)):
                                src = bank[:, 256 * odd + o:256 * odd + o + 128].rearrange("p (h n) -> p h n", h=2)
                                last = dve.tensor_tensor(packed(col, step)[:, d, odd::2, :], src, de[:, d, odd::2, :], ALU.mult)
                        last.then_inc(q, 1)

            @block.tensor
            def _(pe):
                with pe.Fori(0, TILES) as t:
                    def got(*q):
                        for x in q:
                            pe.wait_ge(x, t + 1)

                    def spent(*q):
                        for x in q:
                            pe.wait_ge(x, t)

                    got(s["g"]); spent(s["es"])
                    for m, c0_, c1_, gcol in ((C_LE, 0, 4, 0), (C_GE, 4, 8, 4), (C_GT, 8, 12, 0), (C_LT, 12, 16, 4),
                                              (C_C0, 16, 24, 0), (C_C1, 24, 32, 0)):
                        mm = pe.matmul(b_s[:, c0_:c1_], mat(m), g[:, gcol:gcol + c1_ - c0_], start=True, stop=True)
                    mm.then_inc(s["sums"], 1)
                    got(s["gu"]); spent(s["e1"])
                    pe.matmul(b_D[:, 0:256], mat(C_GT), gu[:, 0, :, :].rearrange("p h n -> p (h n)"), start=True, stop=True)
                    mm = pe.matmul(b_D[:, 256:512], mat(C_LT), gu[:, 1, :, :].rearrange("p h n -> p (h n)"), start=True, stop=True)
                    mm.then_inc(s["dsum"], 1)
                    got(s["rotated"]); spent(s["ftf"], s["ftb"]); pe.wait_ge(s["ftr"], t)
                    for c in range(4):
                        mm = pe.transpose(b_r[:, c * P:(c + 1) * P], hot[:, c * P:(c + 1) * P], mat(C_ID))
                    mm.then_inc(s["turned_r"], 1)
                    spent(s["sqT"])
                    for c in range(4):
                        mm = pe.transpose(b_q[:, c * P:(c + 1) * P], hp[:, c * P:(c + 1) * P], mat(C_ID))
                    mm.then_inc(s["turned_q"], 1)
                    spent(s["lt"], s["at"])
                    pe.transpose(b_k[:, 0:P], hot[:, 1024:1152], mat(C_ID)).then_inc(s["turned_k"], 1)
                    got(s["kh"], s["qh"]); spent(s["khT"], s["qhT"])
                    for c in range(4):
                        src = (kh, qh)[c // 2]
                        mm = pe.transpose(b_g[:, c * P:(c + 1) * P], src[:, (c % 2) * P:(c % 2 + 1) * P], mat(C_ID))
                    mm.then_inc(s["turned_g"], 1)
                    got(s["qg"]); spent(s["ftd"])
                    for c in range(4):
                        mm = pe.transpose(b_d[:, c * P:(c + 1) * P], qg[:, c // 2, 2 * (c % 2):2 * (c % 2) + 2, :], mat(C_ID))
                    mm.then_inc(s["turned_d"], 1)
                    got(s["khT"], s["qhT"], s["skT"])
                    settle(pe, s["pe_passed"])
                    for odd, bank, q in ((0, b_h, s["prod_e"]), (1, b_k, s["prod_o"])):
                        for pair in range(2):
                            for c in range(2):
                                d, j = slice(64 * odd, 64 * odd + 64), slice(64 * c, 64 * c + 64)
                                for o, rhs in ((0, khT), (128, qhT)):
                                    at = 256 * odd + o + 64 * pair
                                    mm = pe.matmul(bank[j, at:at + 64], khT[d, pair, j], rhs[d, pair, j], start=True, stop=True)
                        mm.then_inc(q, 1)


def solve(nc, layer, diag, inv, beside=None):
    NB = 2 * TILES * GH
    with Stage(nc, f"slv{layer}") as st:
        n_in = [st.sb(f"n{d}", [NB, 2, 32, 32]) for d in range(2)]
        neg = [st.sb(f"neg{d}", [NB, 2, 32, 32]) for d in range(2)]
        xt = [st.sb(f"xt{d}", [NB, 2, 32, 32]) for d in range(2)]
        xx = [st.sb(f"xx{d}", [NB, 2, 32, 32]) for d in range(2)]
        prod = [st.sb(f"prod{d}", [NB, 2, 32, 32]) for d in range(2)]
        landed = [st.sem(f"landed{d}") for d in range(2)]
        zeroed, unit, negated, turned = [[st.sem(f"{n}{d}") for d in range(2)] for n in ("zeroed", "unit", "negated", "turned")]
        multiplied, summed = [[st.sem(f"{n}{d}") for d in range(2)] for n in ("multiplied", "summed")]
        stored = st.sem("stored")
        half = 2 * TILES
        sync, scalar, tensor, gpsimd = beside(st) if beside else [None] * 4
        with nc.Block() as block:
            if beside:
                block.tensor(tensor)

            @block.sync
            def _(sp):
                for d in range(2):
                    for slot in range(2):
                        sp.dma_start(n_in[d][:, slot].rearrange("p j i -> p (j i)"),
                                     diag[d, slot * half:(slot + 1) * half].rearrange("a h j i -> (a h) (j i)")).then_inc(landed[d], 16)
                if beside:
                    sync(sp)

            @block.scalar
            def _(act):
                for d in range(2):
                    act.wait_ge(landed[d], 32)
                    act.activation(neg[d][:], n_in[d][:], ACT.Copy, scale=-1.0).then_inc(negated[d], 1)
                if beside:
                    scalar(act)

            def start(pool):
                for d in range(2):
                    pool.memset(xt[d][:], 0.0).then_inc(zeroed[d], 1)
                    pool.wait_ge(zeroed[d], 1)
                    flat = xt[d][:].rearrange("p s c j -> p s (c j)")
                    pool.memset(flat[:, :, 0:1024:33], 1.0).then_inc(unit[d], 1)

            def substitute(eng, d):
                eng.wait_ge(unit[d], 1)
                eng.wait_ge(negated[d], 1)
                for step in range(31):
                    r = step if d == 0 else 31 - step
                    after, cols = (slice(r + 1, 32), slice(0, r + 1)) if d == 0 else (slice(0, r), slice(r, 32))
                    n_c, n_a = step + 1, 31 - step
                    if step:
                        eng.wait_ge(summed[d], step)
                    row = xt[d][:, :, cols, r].unsqueeze(3).broadcast_to([NB, 2, n_c, n_a])
                    n_col = neg[d][:, :, r, after].unsqueeze(2).broadcast_to([NB, 2, n_c, n_a])
                    share = prod[d][:, :, 0:n_c, 0:n_a]
                    eng.tensor_tensor(share, row, n_col, ALU.mult).then_inc(multiplied[d], 1)
                    eng.wait_ge(multiplied[d], step + 1)
                    eng.tensor_tensor(xt[d][:, :, cols, after], xt[d][:, :, cols, after], share, ALU.add).then_inc(summed[d], 1)
                eng.wait_ge(summed[d], 31)
                eng.tensor_copy(xx[d][:], xt[d][:].rearrange("p s c j -> p s j c")).then_inc(turned[d], 1)

            @block.vector
            def _(dve):
                substitute(dve, 0)

            @block.gpsimd
            def _(pool):
                start(pool)
                substitute(pool, 1)
                for d in range(2):
                    pool.wait_ge(turned[d], 1)
                    for which, buf in ((0, xt), (1, xx)):
                        for slot in range(2):
                            pool.dma_start(inv[slot * half:(slot + 1) * half, :, 2 * which + d].rearrange("a h j i -> (a h) (j i)"),
                                           buf[d][:, slot].rearrange("p j i -> p (j i)")).then_inc(stored, 16)
                pool.wait_ge(stored, 8 * 16)
                if beside:
                    gpsimd(pool)


def join(nc, layer, pack, inv, feat, us):
    with Stage(nc, f"jn{layer}") as st:
        off = [st.sb(f"off{u}", [P, 8, P]) for u in range(2)]
        both = [st.sb(f"both{u}", [P, 16, P]) for u in range(2)]
        vn = [st.sb(f"vn{u}", [P, 768]) for u in range(2)]
        y = [st.sb(f"y{d}", [P, 4, P]) for d in range(2)]
        xt = [st.sb(f"xt{d}", [P, 4, P]) for d in range(2)]
        u_o = [st.sb(f"u{d}", [P, 2, 2, HD]) for d in range(2)]
        w_o = [st.sb(f"w{d}", [P, 2, P]) for d in range(2)]
        b_y, b_g, b_u, b_w = [[st.ps(f"b_{n}{d}", [P, 512]) for d in range(2)] for n in "yguw"]
        zeroed = st.sem("zeroed")
        landed = [st.sem(f"landed{u}") for u in range(2)]
        y_sum, y_out, g_sum, x_done, u_sum, w_sum, u_out, w_out, stored = [[st.sem(f"{n}{d}") for d in range(2)] for n in (
            "y_sum", "y_out", "g_sum", "x_done", "u_sum", "w_sum", "u_out", "w_out", "stored")]
        sp_passed, pool_passed = st.sem("sp_passed"), st.sem("pool_passed")
        with nc.Block() as block:
            @block.sync
            def _(sp):
                sp.wait_ge(zeroed, 4)

                def load(u, t):
                    for b in range(4):
                        rows = slice(32 * b, 32 * b + 32)
                        sp.dma_start(both[u][rows, :, rows], inv[bass.ds(t * 4 + b, 1)].rearrange("a h w c j -> (a c) (h w) j")).then_inc(landed[u], 16)
                        d, ib = (0, b + 1) if b % 2 == 0 else (1, b - 1)
                        src = pack[bass.ds(t, 1)].rearrange("a p n -> (a p) n")[rows, T_LT + 256 * d:T_LT + 256 * d + 256]
                        src = src.rearrange("p (h i) -> p h i", h=4)[:, :, 32 * (ib % 2):32 * (ib % 2) + 32]
                        sp.dma_start(off[u][rows, 4 * d:4 * d + 4, 32 * ib:32 * ib + 32], src).then_inc(landed[u], 16)
                    src = pack[bass.ds(t, 1)].rearrange("a p n -> (a p) n")
                    sp.dma_start(vn[u][:, 0:512], src[:, T_NK:T_NK + 512]).then_inc(landed[u], 16)
                    sp.dma_start(vn[u][:, 512:768], src[:, T_GV:T_GV + 256]).then_inc(landed[u], 16)

                for u in range(2):
                    load(u, u)
                with sp.Fori(0, TILES // 2 - 1) as n:
                    for u in range(2):
                        for q in (u_sum, w_sum):
                            for d in range(2):
                                sp.wait_ge(q[d], n * 2 + u + 1)
                                settle(sp, sp_passed)
                        load(u, n * 2 + u + 2)

            NL = 16 * (4 + 4 + 2)

            @block.tensor
            def _(pe):
                with pe.Fori(0, TILES // 2) as n:
                    for u in range(2):
                        t = n * 2 + u
                        pe.wait_ge(landed[u], n * NL + NL)
                        for d in range(2):
                            pe.wait_ge(y_out[d], t)
                            for h in range(4):
                                mm = pe.matmul(b_y[d][:, h * P:(h + 1) * P], off[u][:, 4 * d + h, :], both[u][:, 4 * h + 2 + d, :], start=True, stop=True)
                            mm.then_inc(y_sum[d], 1)
                        for d in range(2):
                            pe.wait_ge(y_out[d], t + 1)
                            pe.wait_ge(x_done[d], t)
                            for h in range(4):
                                mm = pe.matmul(b_g[d][:, h * P:(h + 1) * P], y[d][:, h, :], both[u][:, 4 * h + d, :], start=True, stop=True)
                            mm.then_inc(g_sum[d], 1)
                        for d in range(2):
                            pe.wait_ge(x_done[d], t + 1)
                            pe.wait_ge(w_out[d], t)
                            for h in range(4):
                                e = slice(64 * (h % 2), 64 * (h % 2) + 64)
                                k = 256 * d + 64 * h
                                mm = pe.matmul(b_w[d][e, (h // 2) * P:(h // 2 + 1) * P], vn[u][:, k:k + 64], xt[d][:, h, :], start=True, stop=True)
                            mm.then_inc(w_sum[d], 1)
                            pe.wait_ge(u_out[d], t * 2)
                            for h in range(4):
                                pair = slice(512 + 128 * (h // 2), 512 + 128 * (h // 2) + 128)
                                mm = pe.matmul(b_u[d][:, h * P:(h + 1) * P], xt[d][:, h, :], vn[u][:, pair], start=True, stop=True)
                            mm.then_inc(u_sum[d], 1)

            @block.scalar
            def _(act):
                with act.Fori(0, TILES // 2) as n:
                    for u in range(2):
                        t = n * 2 + u
                        for d in range(2):
                            act.wait_ge(y_sum[d], t + 1)
                            act.wait_ge(g_sum[d], t)
                            act.activation(y[d][:].rearrange("p h n -> p (h n)"), b_y[d][:], ACT.Copy).then_inc(y_out[d], 1)
                        for d in range(2):
                            act.wait_ge(w_sum[d], t + 1)
                            act.wait_ge(stored[d], t * 32)
                            act.activation(w_o[d][:].rearrange("p a n -> p (a n)"), b_w[d][:, 0:256], ACT.Copy).then_inc(w_out[d], 1)

            @block.vector
            def _(dve):
                with dve.Fori(0, TILES // 2) as n:
                    for u in range(2):
                        t = n * 2 + u
                        for d in range(2):
                            dve.wait_ge(g_sum[d], t + 1)
                            dve.wait_ge(u_sum[d], t)
                            dve.tensor_tensor(xt[d][:], both[u][:, d::4, :], b_g[d][:].rearrange("p (h n) -> p h n", h=4), ALU.subtract).then_inc(x_done[d], 1)
                        for d in range(2):
                            dve.wait_ge(u_sum[d], t + 1)
                            dve.wait_ge(stored[d], t * 32)
                            for p in range(2):
                                src = b_u[d][:].rearrange("p (a n) -> p a n", a=2)[:, :, 192 * p:192 * p + 64]
                                dve.tensor_copy(u_o[d][:, :, p, :], src).then_inc(u_out[d], 1)

            @block.gpsimd
            def _(pool):
                for u in range(2):
                    for buf in (off, both):
                        pool.memset(buf[u][:], 0.0).then_inc(zeroed, 1)
                with pool.Fori(0, TILES) as t:
                    for d in range(2):
                        pool.wait_ge(w_out[d], t + 1)
                        settle(pool, pool_passed)
                        slot = F_D + F_DN * d + F_GW
                        pool.dma_start(feat[bass.ds(t, 1)].rearrange("a p f n -> (a p) f n")[:, slot:slot + 2], w_o[d][:]).then_inc(stored[d], 16)
                        pool.wait_ge(u_out[d], t * 2 + 2)
                        settle(pool, pool_passed)
                        pool.dma_start(us[bass.ds(t, 1)].rearrange("a p n -> (a p) n")[:, 256 * d:256 * d + 256],
                                       u_o[d][:].rearrange("p a q e -> p (a q e)")).then_inc(stored[d], 16)
                for d in range(2):
                    pool.wait_ge(stored[d], TILES * 32)


def scan(nc, layer, pack, feat, tot, us, small, mats, o_ret, o_gdn):
    with Stage(nc, f"scn{layer}") as st:
        dual = lambda n, shape: [st.sb(f"{n}{u}", shape) for u in range(2)]
        gt = st.sb("gt", [P, TILES, 2, 2, 2, 2])
        gth = st.sb("gth", [P, TILES, 2, 2, 2])
        fd = dual("fd", [P, 2, F_DN, P])
        u_i = [dual(f"u_i{c}", [P, 256]) for c in range(2)]
        kaz = [dual(f"kaz{c}", [P, 2, 512]) for c in range(2)]
        rqz = dual("rqz", [P, 2, 2, P])
        rk, rkv = dual("rk", [P, 2, P]), dual("rkv", [P, 2, 512])
        S, Sg = st.sb("S", [P, 2, 2, P]), st.sb("Sg", [P, 2, 2, P])
        R, Rg = st.sb("R", [P, 2, 2, P]), st.sb("Rg", [P, 2, 2, P])
        z = st.sb("z", [P, 256])
        mask, scores = st.sb("mask", [P, 4, P]), st.sb("scores", [P, 4, P])
        sm, lg, cd, cdh = st.sb("sm", [P, 3, 8]), st.sb("lg", [P, 8]), st.sb("cd", [P, 2, 2, 2]), st.sb("cdh", [P, 2, 2])
        far, keep, eg, kept = (st.sb(n, [P, 2, P]) for n in ("far", "keep", "eg", "kept"))
        one = st.sb("one", [P, 1])
        b_z, b_o, b_S, b_k, b_r, b_R = [st.ps(f"b_{n}", [P, 512]) for n in ("z", "o", "S", "k", "r", "R")]
        s = signals(st, """set_in const zeroed rate_e lgs cds cdhs gths fars keeps egs masked1 mask_done
            in0 in1 z_sum z_done dS_sum Sg_done S_done o_sum o_out k_sum scored r_sum r_out dR_sum Rg_done R_done
            sp_passed dve_passed pool_passed act_passed""")
        in_s = (s["in0"], s["in1"])
        NL = 16 * 15
        half = lambda a: slice(64 * a, 64 * a + 64)
        dist = mats[:, C_DIST, :]

        def tile_pairs(eng, body):
            with eng.Fori(0, 1) as n:
                for u in range(2):
                    body(n, u, n * 2 + u, n * 0 + (1 - u))
            with eng.Fori(1, TILES // 2) as n:
                for u in range(2):
                    body(n, u, n * 2 + u, n * -2 + (TILES + 1 - u))

        with nc.Block() as block:
            @block.sync
            def _(sp):
                sp.dma_start(gt[:].rearrange("p t c d a q -> p t (c d a q)"), tot.rearrange("t p n -> p t n")).then_inc(s["set_in"], 16)
                sp.dma_start(sm[:], small[layer]).then_inc(s["set_in"], 16)
                sp.wait_ge(s["zeroed"], 8)

                def tile(ap, t):
                    return ap[bass.ds(t, 1)].rearrange("a p n -> (a p) n")

                def load(u, tf, tb):
                    q = in_s[u]
                    for d, t in ((0, tf), (1, tb)):
                        for c in range(2):
                            r = half(c if d == 0 else 1 - c)
                            sp.dma_start(u_i[c][u][r, :], tile(us, t)[r, 256 * d:256 * d + 256]).then_inc(q, 16)
                            sp.dma_start(kaz[c][u][r, d, :], tile(pack, t)[r, T_D + 512 * d:T_D + 512 * d + 512]).then_inc(q, 16)
                        ft = feat[bass.ds(t, 1)].rearrange("a p f n -> (a p) f n")
                        sp.dma_start(fd[u][:, d], ft[:, F_D + F_DN * d:F_D + F_DN * d + F_DN, :]).then_inc(q, 16)
                        sp.dma_start(rkv[u][:, d, :], tile(pack, t)[:, T_RK + 256 * d:T_RK + 256 * d + 512]).then_inc(q, 16)
                    ft = feat[bass.ds(tf, 1)].rearrange("a p f n -> (a p) f n")
                    for p in range(2):
                        sp.dma_start(rqz[u][half(p), :, p, :], ft[half(p), F_RQ:F_RQ + 2, :]).then_inc(q, 16)
                    sp.dma_start(rk[u][:], ft[:, F_RK:F_RK + 2, :]).then_inc(q, 16)

                def again(t):
                    for q, k in ((s["o_sum"], 2), (s["r_sum"], 1), (s["dR_sum"], 1), (s["dS_sum"], 2), (s["z_done"], 2)):
                        sp.wait_ge(q, (t - 1) * k)
                        settle(sp, s["sp_passed"])

                with sp.Fori(0, 1) as n:
                    for u in range(2):
                        load(u, n + u, n + (1 - u))
                with sp.Fori(1, TILES // 2) as n:
                    for u in range(2):
                        again(n * 2 + u)
                        load(u, n * 2 + u, n * -2 + (TILES + 1 - u))

            @block.gpsimd
            def _(pool):
                for u in range(2):
                    for buf in (kaz[0], kaz[1], rqz):
                        pool.memset(buf[u][:], 0.0).then_inc(s["zeroed"], 1)
                pool.memset(S[:], 0.0).then_inc(s["zeroed"], 1)
                pool.memset(R[:], 0.0).then_inc(s["zeroed"], 1)
                pool.memset(one[:], 1.0).then_inc(s["const"], 1)
                pool.wait_ge(s["gths"], 2); pool.wait_ge(s["cdhs"], 2); pool.wait_ge(s["zeroed"], 8)

                def body(n, u, t, tb):
                    for c in range(2):
                        pool.wait_ge(s["S_done"], t * 4 + 2 * c)
                        for d, tt, cc in ((0, t, c), (1, tb, 1 - c)):
                            g = gth[:, bass.ds(tt, 1), cc, d, :].rearrange("p a n -> p (a n)").unsqueeze(2).broadcast_to([P, 2, P])
                            pool.tensor_tensor(Sg[:, d], S[:, d], g, ALU.mult).then_inc(s["Sg_done"], 1)
                        if c == 0:
                            pool.wait_ge(s["R_done"], t * 2)
                            pool.tensor_tensor(Rg[:], R[:], cdh[:].unsqueeze(3).broadcast_to([P, 2, 2, P]), ALU.mult).then_inc(s["Rg_done"], 1)

                tile_pairs(pool, body)

            @block.scalar
            def _(act):
                act.wait_ge(s["set_in"], 32)
                act.wait_ge(s["const"], 1)
                act.activation(lg[:], sm[:, 2, :], ACT.Exp, scale=-float(np.log(2.0))).then_inc(s["rate_e"], 1)
                act.wait_ge(s["rate_e"], 1)
                act.activation(lg[:], lg[:], ACT.Ln, scale=-1.0, bias=one[:]).then_inc(s["lgs"], 1)
                act.wait_ge(s["lgs"], 1)
                act.activation(cd[:].rearrange("p d a q -> p (d a q)"), lg[:], ACT.Exp, scale=float(P)).then_inc(s["cds"], 1)
                act.wait_ge(s["fars"], 2)
                for h in range(4):
                    if h:
                        act.wait_ge(s["masked1"], h)
                    for d in range(2):
                        act.activation(eg[:, d, :], far[:, d, :], ACT.Exp, scale=lg[:, 4 * d + h:4 * d + h + 1]).then_inc(s["egs"], 1)

                def body(n, u, t, tb):
                    for c in range(2):
                        act.wait_ge(s["o_sum"], t * 2 + c + 1)
                        for d, tt, cc in ((0, t, c), (1, tb, 1 - c)):
                            act.activation(o_gdn[:, d, :, bass.ds(tt * P + 64 * cc, 64)],
                                           b_o[:, 0:256].rearrange("p (a n) -> p a n", a=2)[:, :, half(d)], ACT.Copy).then_inc(s["o_out"], 1)
                        if c == 0:
                            act.wait_ge(s["r_sum"], t + 1)
                            for d, tt in ((0, t), (1, tb)):
                                act.activation(o_ret[:, d, :, bass.ds(tt * P, P)],
                                               b_r[:, 256 * d:256 * d + 256].rearrange("p (a n) -> p a n", a=2), ACT.Copy,
                                               scale=0.125).then_inc(s["r_out"], 1)

                tile_pairs(act, body)

            @block.vector
            def _(dve):
                dve.wait_ge(s["set_in"], 32)
                for p in range(2):
                    dve.tensor_copy(gth[half(p)], gt[half(p), :, :, :, :, p]).then_inc(s["gths"], 1)
                dve.wait_ge(s["cds"], 1)
                for p in range(2):
                    dve.tensor_copy(cdh[half(p)], cd[half(p), :, :, p]).then_inc(s["cdhs"], 1)
                dve.tensor_scalar(far[:, 0, :], dist, 0.0, None, ALU.max).then_inc(s["fars"], 1)
                dve.tensor_scalar(far[:, 1, :], dist, -1.0, 0.0, ALU.mult, ALU.max).then_inc(s["fars"], 1)
                dve.tensor_scalar(keep[:, 0, :], dist, 0.0, None, ALU.is_ge).then_inc(s["keeps"], 1)
                dve.tensor_scalar(keep[:, 1, :], dist, 0.0, None, ALU.is_le).then_inc(s["keeps"], 1)
                dve.wait_ge(s["keeps"], 2)
                for h in range(4):
                    dve.wait_ge(s["egs"], 2 * h + 2)
                    if h:
                        dve.wait_ge(s["mask_done"], h)
                    dve.tensor_tensor(kept[:], eg[:], keep[:], ALU.mult).then_inc(s["masked1"], 1)
                    dve.wait_ge(s["masked1"], h + 1)
                    dve.tensor_tensor(mask[:, h, :], kept[:, 0, :], kept[:, 1, :], ALU.add).then_inc(s["mask_done"], 1)
                dve.wait_ge(s["mask_done"], 4)

                def body(n, u, t, tb):
                    for c in range(2):
                        dve.wait_ge(s["z_sum"], t * 2 + c + 1)
                        dve.wait_ge(in_s[u], n * NL + NL)
                        dve.wait_ge(s["o_sum"], t * 2 + c)
                        dve.tensor_tensor(z[:], b_z[:, 0:256], u_i[c][u][:], ALU.add).then_inc(s["z_done"], 1)
                        if c == 0:
                            dve.wait_ge(s["k_sum"], t + 1)
                            dve.wait_ge(s["r_sum"], t)
                            dve.tensor_tensor(scores[:], b_k[:].rearrange("p (h n) -> p h n", h=4), mask[:], ALU.mult).then_inc(s["scored"], 1)
                        dve.wait_ge(s["dS_sum"], t * 2 + c + 1)
                        dve.wait_ge(s["Sg_done"], t * 4 + 2 * c + 2)
                        for p in range(2):
                            at = lambda b: b[:].rearrange("p (d a n) -> p d a n", d=2, a=2)[half(p), :, :, half(p)]
                            dve.tensor_tensor(S[half(p), :, :, half(p)], Sg[half(p), :, :, half(p)], at(b_S), ALU.add).then_inc(s["S_done"], 1)
                        if c == 1:
                            dve.wait_ge(s["dR_sum"], t + 1)
                            dve.wait_ge(s["Rg_done"], t + 1)
                            for p in range(2):
                                at = lambda b: b[:].rearrange("p (d a n) -> p d a n", d=2, a=2)[half(p), :, :, half(p)]
                                dve.tensor_tensor(R[half(p), :, :, half(p)], Rg[half(p), :, :, half(p)], at(b_R), ALU.add).then_inc(s["R_done"], 1)

                tile_pairs(dve, body)

            @block.tensor
            def _(pe):
                pe.wait_ge(s["zeroed"], 8)

                def body(n, u, t, tb):
                    pe.wait_ge(in_s[u], n * NL + NL)
                    for c in range(2):
                        cc = (c, 1 - c)
                        pe.wait_ge(s["S_done"], t * 4 + 2 * c)
                        pe.wait_ge(s["z_done"], t * 2 + c)
                        for d in range(2):
                            for a in range(2):
                                mm = pe.matmul(b_z[half(cc[d]), a * P:(a + 1) * P], fd[u][:, d, F_GW + a, half(cc[d])], S[:, d, a, :], start=True, stop=True)
                        mm.then_inc(s["z_sum"], 1)
                        pe.wait_ge(s["o_out"], t * 4 + 2 * c)
                        for d in range(2):
                            for a in range(2):
                                for p in range(2):
                                    pe.matmul(b_o[half(p), a * P + 64 * d:a * P + 64 * d + 64], S[:, d, a, half(p)],
                                              fd[u][:, d, F_GQD + a, half(cc[d])], start=(d == 0 and a == 0), stop=False)
                        if c == 0:
                            pe.wait_ge(s["scored"], t)
                            for a in range(2):
                                mm = pe.matmul(b_k[:, 256 * a:256 * a + 256], rk[u][:, a, :], rqz[u][:, a].rearrange("p q n -> p (q n)"), start=True, stop=True)
                            mm.then_inc(s["k_sum"], 1)
                        else:
                            pe.wait_ge(s["R_done"], t * 2)
                            for d in range(2):
                                for a in range(2):
                                    at = 256 * d + 128 * a
                                    mm = pe.matmul(b_R[:, at:at + P], rkv[u][:, d, 256 * d + a * P:256 * d + (a + 1) * P],
                                                   rkv[u][:, d, 256 * (1 - d) + a * P:256 * (1 - d) + (a + 1) * P], start=True, stop=True)
                            mm.then_inc(s["dR_sum"], 1)
                        pe.wait_ge(s["z_done"], t * 2 + c + 1)
                        for d in range(2):
                            for a in range(2):
                                at = 256 * d + 128 * a
                                mm = pe.matmul(b_S[:, at:at + P], kaz[c][u][:, d, T_KT + a * P:T_KT + (a + 1) * P], z[:, a * P:(a + 1) * P], start=True, stop=True)
                        mm.then_inc(s["dS_sum"], 1)
                        for a in range(2):
                            for p in range(2):
                                h = 2 * a + p
                                mm = pe.matmul(b_o[half(p), a * P:(a + 1) * P], z[:, h * 64:h * 64 + 64],
                                               kaz[c][u][:, :, T_AT + h * 64:T_AT + h * 64 + 64], start=False, stop=(a == 1))
                        mm.then_inc(s["o_sum"], 1)
                        if c == 0:
                            pe.wait_ge(s["r_out"], t * 2)
                            pe.wait_ge(s["R_done"], t * 2)
                            for d in range(2):
                                for a in range(2):
                                    at = 256 * d + 128 * a
                                    pe.matmul(b_r[:, at:at + P], R[:, d, a, :], fd[u][:, d, F_RQD + a, :], start=(d == 0 and a == 0), stop=False)
                            pe.wait_ge(s["scored"], t + 1)
                            for a in range(2):
                                for p in range(2):
                                    h = 2 * a + p
                                    mm = pe.matmul(b_r[half(p), a * P:(a + 1) * P], rkv[u][:, 0, 256 + h * 64:256 + h * 64 + 64], scores[:, h, :], start=False, stop=(a == 1))
                            mm.then_inc(s["r_sum"], 1)

                tile_pairs(pe, body)


def window(nc, layer, t0, proj, swq, swk, win, sinks, mats, y_hi, y_lo):
    NT = TILES - t0
    K = 3 * P + CTX
    with Stage(nc, f"win{layer}") as st:
        keys = st.sb("keys", [P, TOK + 2 * P])
        vc = st.sb("vc", [P, 2, P])
        sink = st.sb("sink", [P, SH])
        qz = [st.sb(f"qz{u}", [P, 2, 4, P]) for u in range(2)]
        mask = [st.sb(f"mask{u}", [P, 3 * P]) for u in range(2)]
        vw = [st.sb(f"vw{u}", [P, 3, P]) for u in range(2)]
        prob = [st.sb(f"prob{i}", [P, K]) for i in range(2)]
        probT = [st.sb(f"probT{i}", [P, 5, P]) for i in range(2)]
        mx = [st.sb(f"mx{i}", [P, 2]) for i in range(2)]
        low = [st.sb(f"low{i}", [P, 1]) for i in range(2)]
        nmax = [st.sb(f"nmax{i}", [P, 1]) for i in range(2)]
        part = [st.sb(f"part{i}", [P, 3]) for i in range(2)]
        den, rden = [st.sb(f"den{i}", [P, 1]) for i in range(2)], [st.sb(f"rden{i}", [P, 1]) for i in range(2)]
        yt = st.sb("yt", [P, SH * HD])
        b_l, b_c, b_o = [[st.ps(f"b_{n}{i}", [P, 512]) for i in range(2)] for n in "lco"]
        b_t0, b_t1 = st.ps("b_t0", [P, 512]), st.ps("b_t1", [P, 512])
        s = signals(st, "set_in zeroed t0_out t1_out y_turned y_rounded y_split pe_passed dve_passed sp_passed")
        landed, s_sum, masked, cmax, lowered, m_done, e_loc, e_ctx, e_sink, t_sum, o_sum, summed, inverted, y_done = [
            [st.sem(f"{n}{i}") for i in range(2)] for n in
            "landed s_sum masked cmax lowered m_done e_loc e_ctx e_sink t_sum o_sum summed inverted y_done".split()]

        with nc.Block() as block:
            @block.sync
            def _(sp):
                sp.dma_start(keys[:], swk).then_inc(s["set_in"], 16)
                sp.dma_start(vc[:], proj[R0 + 1:R0 + 1 + CTX, S_V:S_V + P].rearrange("(b p) n -> p b n", p=P)).then_inc(s["set_in"], 16)
                sp.dma_start(sink[:], sinks[layer]).then_inc(s["set_in"], 16)
                sp.wait_ge(s["zeroed"], 2)

                def load(u, t, row):
                    for p in range(2):
                        r = slice(64 * p, 64 * p + 64)
                        sp.dma_start(qz[u][r, p], swq[bass.ds(t, 1)].rearrange("a p c n -> (a p) c n")[r]).then_inc(landed[u], 16)
                    sp.dma_start(mask[u][:], win[bass.ds(t, 1)].rearrange("a p n -> (a p) n")).then_inc(landed[u], 16)
                    sp.dma_start(vw[u][:], proj[bass.ds(row - P, 3 * P), S_V:S_V + P].rearrange("(b p) n -> p b n", p=P)).then_inc(landed[u], 16)

                for u in range(2):
                    with sp.Fori(t0 + u, t0 + u + 1) as t:
                        load(u, t, t * P + (row_of(t0) - t0 * P))
                with sp.Fori(1, NT // 2) as n:
                    for u in range(2):
                        for q in o_sum:
                            sp.wait_ge(q, (n * 2 + u - 1) * 4)
                            settle(sp, s["sp_passed"])
                        load(u, n * 2 + (u + t0), n * (2 * P) + ((u + t0) * P + row_of(2) - 2 * P))

            @block.gpsimd
            def _(pool):
                for u in range(2):
                    pool.memset(qz[u][:], 0.0).then_inc(s["zeroed"], 1)

            def at(n, g):
                u, h = g // SH, g % SH
                return u, h, n * 2 + u, g % 2, n * SH + g // 2

            G = 2 * SH

            def scores(pe, n, g):
                u, h, T, i, use = at(n, g)
                if h == 0:
                    pe.wait_ge(landed[u], n * 64 + 64)
                pe.wait_ge(masked[i], use)
                pe.wait_ge(e_ctx[i], use)
                q = qz[u][:, h // 4, h % 4, :]
                pe.matmul(b_l[i][:, 0:3 * P], q, keys[:, bass.ds(T * P + t0 * P, 3 * P)], start=True, stop=True)
                pe.matmul(b_c[i][:, 0:CTX], q, keys[:, P:P + CTX], start=True, stop=True).then_inc(s_sum[i], 1)

            def turn(pe, n, g):
                u, h, T, i, use = at(n, g)
                pe.wait_ge(e_loc[i], use + 1)
                pe.wait_ge(e_ctx[i], use + 1)
                pe.wait_ge(s["t0_out"], T * 8 + h)
                pe.wait_ge(s["t1_out"], T * 8 + h)
                if g in (0, SH + 1):
                    pe.wait_ge(s["y_split"], T)
                for b in range(5):
                    bank = b_t0[:, b * P:(b + 1) * P] if b < 3 else b_t1[:, (b - 3) * P:(b - 2) * P]
                    mm = pe.transpose(bank, prob[i][:, b * P:(b + 1) * P], mats[:, C_ID, :])
                mm.then_inc(t_sum[i], 1)

            def attend(pe, n, g):
                u, h, T, i, use = at(n, g)
                pe.wait_ge(s["t0_out"], T * 8 + h + 1)
                pe.wait_ge(s["t1_out"], T * 8 + h + 1)
                pe.wait_ge(y_done[i], use)
                for b in range(5):
                    v = vw[u][:, b, :] if b < 3 else vc[:, b - 3, :]
                    mm = pe.matmul(b_o[i][:, 0:P], probT[i][:, b, :], v, start=(b == 0), stop=(b == 4))
                mm.then_inc(o_sum[i], 1)

            def turn_output(pe, n, u):
                T = n * 2 + u
                for i in range(2):
                    pe.wait_ge(y_done[i], T * 4 + 4)
                pe.wait_ge(s["t0_out"], T * 8 + 8 + (1 if u == 0 else 0))
                for c in range(4):
                    mm = pe.transpose(b_t0[:, c * P:(c + 1) * P], yt[:, c * P:(c + 1) * P], mats[:, C_ID, :])
                mm.then_inc(s["y_turned"], 1)

            @block.tensor
            def _(pe):
                pe.wait_ge(s["set_in"], 48)
                with pe.Fori(0, NT // 2) as n:
                    scores(pe, n, 0)
                    scores(pe, n, 1)
                    for g in range(G):
                        turn(pe, n, g)
                        if g + 2 < G:
                            scores(pe, n, g + 2)
                        if g == SH:
                            turn_output(pe, n, 0)
                        attend(pe, n, g)
                    turn_output(pe, n, 1)

            def maximum(dve, n, g):
                u, h, T, i, use = at(n, g)
                if h == 0:
                    dve.wait_ge(landed[u], n * 64 + 64)
                dve.wait_ge(s_sum[i], use + 1)
                dve.wait_ge(t_sum[i], use)
                dve.wait_ge(lowered[i], use)
                settle(dve, s["dve_passed"])
                dve.tensor_tensor_reduce(prob[i][:, 0:3 * P], b_l[i][:, 0:3 * P], mask[u][:], 1.0, NEG, ALU.add, ALU.max,
                                         mx[i][:, 0:1]).then_inc(masked[i], 1)
                dve.tensor_reduce(mx[i][:, 1:2], b_c[i][:, 0:CTX], AX.X, ALU.max).then_inc(cmax[i], 1)
                dve.wait_ge(masked[i], use + 1)
                dve.wait_ge(cmax[i], use + 1)
                dve.wait_ge(m_done[i], use)
                dve.tensor_tensor(low[i][:], mx[i][:, 0:1], mx[i][:, 1:2], ALU.max).then_inc(lowered[i], 1)
                dve.wait_ge(lowered[i], use + 1)
                dve.wait_ge(e_sink[i], use)
                dve.tensor_scalar(nmax[i][:], low[i][:], sink[:, h:h + 1], -1.0, ALU.max, ALU.mult).then_inc(m_done[i], 1)

            def weigh(dve, n, g):
                u, h, T, i, use = at(n, g)
                dve.wait_ge(o_sum[i], use + 1)
                dve.wait_ge(inverted[i], use + 1)
                if h == 0:
                    dve.wait_ge(s["y_turned"], T)
                e = slice(64 * (h // 4), 64 * (h // 4) + 64)
                dve.tensor_scalar(yt[:, h * 64:h * 64 + 64], b_o[i][:, e], rden[i][:], None, ALU.mult).then_inc(y_done[i], 1)

            def split_output(dve, n, u):
                T = n * 2 + u
                tok = bass.ds(T * P + t0 * P, P)
                dve.wait_ge(s["y_rounded"], T + 1)
                dve.tensor_tensor(y_lo[:, 2:6, tok], b_t0[:].rearrange("p (c n) -> p c n", c=4), y_hi[:, 2:6, tok].bitcast(F32),
                                  ALU.subtract).then_inc(s["y_split"], 1)

            @block.vector
            def _(dve):
                dve.wait_ge(s["set_in"], 48)
                with dve.Fori(0, NT // 2) as n:
                    maximum(dve, n, 0)
                    maximum(dve, n, 1)
                    for g in range(G):
                        u, h, T, i, use = at(n, g)
                        if g:
                            weigh(dve, n, g - 1)
                        dve.wait_ge(t_sum[i], use + 1)
                        dve.wait_ge(o_sum[i], use)
                        dve.tensor_copy(probT[i][:, 3:5, :].rearrange("p a n -> p (a n)"), b_t1[:, 0:2 * P]).then_inc(s["t1_out"], 1)
                        dve.wait_ge(e_sink[i], use + 1)
                        dve.wait_ge(inverted[i], use)
                        dve.scalar_tensor_tensor(den[i][:], part[i][:, 0:1], part[i][:, 1:2], part[i][:, 2:3], ALU.add, ALU.add).then_inc(summed[i], 1)
                        dve.wait_ge(summed[i], use + 1)
                        dve.wait_ge(y_done[i], use)
                        dve.reciprocal(rden[i][:], den[i][:]).then_inc(inverted[i], 1)
                        if g == SH:
                            split_output(dve, n, 0)
                        if g + 2 < G:
                            maximum(dve, n, g + 2)
                    weigh(dve, n, G - 1)
                    split_output(dve, n, 1)

            def exponentials(act, n, g):
                u, h, T, i, use = at(n, g)
                act.wait_ge(m_done[i], use + 1)
                act.wait_ge(summed[i], use)
                act.activation(prob[i][:, 0:3 * P], prob[i][:, 0:3 * P], ACT.Exp, bias=nmax[i][:], accum_out=part[i][:, 0:1]).then_inc(e_loc[i], 1)
                act.activation(prob[i][:, 3 * P:K], b_c[i][:, 0:CTX], ACT.Exp, bias=nmax[i][:], accum_out=part[i][:, 1:2]).then_inc(e_ctx[i], 1)
                act.activation(part[i][:, 2:3], sink[:, h:h + 1], ACT.Exp, bias=nmax[i][:]).then_inc(e_sink[i], 1)

            def round_output(act, n, u):
                T = n * 2 + u
                tok = bass.ds(T * P + t0 * P, P)
                act.wait_ge(s["y_turned"], T + 1)
                act.activation(y_hi[:, 2:6, tok], b_t0[:].rearrange("p (c n) -> p c n", c=4), ACT.Copy).then_inc(s["y_rounded"], 1)

            @block.scalar
            def _(act):
                with act.Fori(0, NT // 2) as n:
                    exponentials(act, n, 0)
                    exponentials(act, n, 1)
                    for g in range(G):
                        u, h, T, i, use = at(n, g)
                        act.wait_ge(t_sum[i], use + 1)
                        act.wait_ge(o_sum[i], use)
                        act.activation(probT[i][:, 0:3, :].rearrange("p a n -> p (a n)"), b_t0[:, 0:3 * P], ACT.Copy).then_inc(s["t0_out"], 1)
                        if g == SH:
                            round_output(act, n, 0)
                        if g + 2 < G:
                            exponentials(act, n, g + 2)
                    round_output(act, n, 1)


def gated(nc, layer, t0, proj, norm_w, mats, o_ret, o_gdn, y_hi, y_lo, eps):
    NG = (TILES - t0) // 2
    W = 2 * P
    with Stage(nc, f"gate{layer}") as st:
        gin = [st.sb(f"gin{u}", [P, 2, 512]) for u in range(2)]
        nw = st.sb("nw", [P, 4])
        mean = st.sb("mean", [P, P])
        os_, sq, sg, logs, root, y1, yf = (st.sb(n, [P, 4, W]) for n in ("os", "sq", "sg", "logs", "root", "y1", "yf"))
        b_g, b_m = [[st.ps(f"b_{n}{i}", [P, 512]) for i in range(2)] for n in "gm"]
        s = signals(st, "set_in mean0 mean1 in0 in1 added squared turned silued summed logged rooted normed gated rounded split sp_passed")
        ins = (s["in0"], s["in1"])
        with nc.Block() as block:
            @block.sync
            def _(sp):
                sp.dma_start(nw[:], norm_w[layer]).then_inc(s["set_in"], 16)

                for g in range(NG):
                    if g >= 2:
                        sp.wait_ge(s["turned"], g - 1)
                    row = row_of(t0 + 2 * g)
                    for half, col in ((0, R_G), (1, G_Z)):
                        sp.dma_start(gin[g % 2][:, :, 256 * half:256 * half + 256],
                                     proj[row:row + W, col:col + 256].rearrange("(b p) n -> p b n", p=P)).then_inc(ins[g % 2], 16)

            @block.gpsimd
            def _(pool):
                pool.memset(mean[:], 0.0).then_inc(s["mean0"], 1)
                pool.wait_ge(s["mean0"], 1)
                for p in range(2):
                    r = slice(64 * p, 64 * p + 64)
                    pool.memset(mean[r, r], 1.0 / HD).then_inc(s["mean1"], 1)
                pool.wait_ge(s["mean1"], 2)
                with pool.Fori(0, NG) as g:
                    tok = bass.ds(g * W + t0 * P, W)
                    pool.wait_ge(s["normed"], g)
                    pool.wait_ge(s["squared"], g)
                    pool.tensor_tensor(os_[:, 0:2, :], o_ret[:, 0, :, tok], o_ret[:, 1, :, tok], ALU.add).then_inc(s["added"], 1)
                    pool.tensor_tensor(os_[:, 2:4, :], o_gdn[:, 0, :, tok], o_gdn[:, 1, :, tok], ALU.add).then_inc(s["added"], 1)

            @block.tensor
            def _(pe):
                pe.wait_ge(s["mean1"], 2)
                for g in range(NG):
                    pe.wait_ge(ins[g % 2], (g // 2 + 1) * 32)
                    if g:
                        pe.wait_ge(s["silued"], 2 * g)
                    for c in range(4):
                        for b in range(2):
                            at = (c % 2) * W + b * P
                            mm = pe.transpose(b_g[c // 2][:, at:at + P], gin[g % 2][:, b, c * P:(c + 1) * P], mats[:, C_ID, :])
                    mm.then_inc(s["turned"], 1)
                    pe.wait_ge(s["squared"], g + 1)
                    if g:
                        pe.wait_ge(s["logged"], 2 * g)
                    for i in range(2):
                        mm = pe.matmul(b_m[i][:], mean[:], sq[:, 2 * i:2 * i + 2, :].rearrange("p c n -> p (c n)"), start=True, stop=True)
                    mm.then_inc(s["summed"], 1)

            flat = lambda b, i: b[:, 2 * i:2 * i + 2, :].rearrange("p c n -> p (c n)")

            @block.scalar
            def _(act):
                with act.Fori(0, NG) as g:
                    tok = bass.ds(g * W + t0 * P, W)
                    act.wait_ge(s["added"], g * 2 + 2)
                    act.wait_ge(s["summed"], g)
                    act.activation(sq[:], os_[:], ACT.Square).then_inc(s["squared"], 1)
                    act.wait_ge(s["summed"], g + 1)
                    act.wait_ge(s["normed"], g)
                    for i in range(2):
                        act.activation(flat(logs, i), b_m[i][:], ACT.Ln, bias=eps[:]).then_inc(s["logged"], 1)
                    act.wait_ge(s["logged"], g * 2 + 2)
                    act.activation(root[:], logs[:], ACT.Exp, scale=-0.5).then_inc(s["rooted"], 1)
                    act.wait_ge(s["turned"], g + 1)
                    act.wait_ge(s["gated"], g * 4)
                    for i in range(2):
                        act.activation(flat(sg, i), b_g[i][:], ACT.Silu).then_inc(s["silued"], 1)
                    act.wait_ge(s["gated"], g * 4 + 4)
                    for i, c in ((0, 0), (1, 6)):
                        act.activation(y_hi[:, c:c + 2, tok], yf[:, 2 * i:2 * i + 2, :], ACT.Copy).then_inc(s["rounded"], 1)

            @block.vector
            def _(dve):
                dve.wait_ge(s["set_in"], 16)
                with dve.Fori(0, NG) as g:
                    tok = bass.ds(g * W + t0 * P, W)
                    dve.wait_ge(s["rooted"], g + 1)
                    dve.wait_ge(s["gated"], g * 4)
                    dve.tensor_tensor(y1[:], os_[:], root[:], ALU.mult).then_inc(s["normed"], 1)
                    dve.wait_ge(s["normed"], g + 1)
                    dve.wait_ge(s["silued"], g * 2 + 2)
                    dve.wait_ge(s["split"], g * 2)
                    for c in range(4):
                        dve.scalar_tensor_tensor(yf[:, c, :], y1[:, c, :], nw[:, c:c + 1], sg[:, c, :], ALU.mult, ALU.mult).then_inc(s["gated"], 1)
                    dve.wait_ge(s["rounded"], g * 2 + 2)
                    for i, c in ((0, 0), (1, 6)):
                        dve.tensor_tensor(y_lo[:, c:c + 2, tok], yf[:, 2 * i:2 * i + 2, :], y_hi[:, c:c + 2, tok].bitcast(F32),
                                          ALU.subtract).then_inc(s["split"], 1)


def mixed(nc, layer, lo, x, units, mod, y_hi, y_lo):
    slices = token_slices(lo)
    NS, TURNS = len(slices), KC // 2
    with Stage(nc, f"mix{layer}") as st:
        w = WeightUnits(st, units)
        bank = [[st.ps(f"bank{u}{s}", [P, 512]) for s in range(NS)] for u in range(2)]
        full = [[st.sem(f"full{u}{s}") for s in range(NS)] for u in range(2)]
        free = [[st.sem(f"free{u}{s}") for s in range(NS)] for u in range(2)]
        with nc.Block() as block:
            @block.sync
            def _(sp):
                w.load_all(sp, TURNS)

            @block.scalar
            def _(act):
                with act.Fori(0, TURNS) as n:
                    for u in range(2):
                        w.round(act, u, n)

            @block.tensor
            def _(pe):
                with pe.Fori(0, TURNS) as n:
                    for u in range(2):
                        pe.wait_ge(w.ready[u], n + 1)
                        for s, (t0, ln) in enumerate(slices):
                            pe.wait_ge(free[u][s], n)
                            for k in range(KC):
                                f = slice(k * P, (k + 1) * P)
                                mm = three_passes(pe, bank[u][s][:, 0:ln], w.hi[u][:, f], w.lo[u][:, f],
                                                  y_hi[:, k, t0:t0 + ln], y_lo[:, k, t0:t0 + ln], k == 0, k == KC - 1)
                            mm.then_inc(full[u][s], 1)
                        pe.wait_ge(full[u][NS - 1], n + 1)
                        pe.sem_inc(w.used[u], 1)

            @block.vector
            def _(dve):
                def add(n, u):
                    for s, (t0, ln) in enumerate(slices):
                        v = 1 if t0 < CTX else 0
                        dve.wait_ge(full[u][s], n + 1)
                        xs = x[:, bass.ds(n * 2 + u, 1), t0:t0 + ln].rearrange("p a n -> p (a n)")
                        dve.scalar_tensor_tensor(xs, bank[u][s][:, 0:ln], mod[:, bass.ds(n * 2 + (u + 2 * KC), 1), v], xs,
                                                 ALU.mult, ALU.add).then_inc(free[u][s], 1)

                for u in range(2):
                    w.rest(dve, u, 0)
                with dve.Fori(0, TURNS - 1) as n:
                    for u in range(2):
                        add(n, u)
                        w.rest(dve, u, n + 1)
                with dve.Fori(TURNS - 1, TURNS) as n:
                    for u in range(2):
                        add(n, u)


def final(nc, x, norm_w, out, ones, eps):
    with Stage(nc, "fin") as st:
        nw = st.sb("nw", [P, KC])
        sq = [st.sb(f"sq{i}", [P, 512]) for i in range(2)]
        root, inv = st.sb("root", [P, 512]), [st.sb(f"inv{i}", [P, 512]) for i in range(2)]
        y = st.sb("y", [P, KC, LAT])
        ms = [st.ps(f"ms{s}", [P, 512]) for s in range(2)]
        s = signals(st, "set_in squared summed rooted inverted done stored")
        with nc.Block() as block:
            @block.sync
            def _(sp):
                sp.dma_start(nw[:], norm_w).then_inc(s["set_in"], 16)
                for i in range(2 * KC):
                    sp.wait_ge(s["done"], i + 1)
                    at = slice((i // KC) * 512, (i // KC) * 512 + 512)
                    sp.dma_start(out[:, i % KC, at], y[:, i % KC, at]).then_inc(s["stored"], 16)
                sp.wait_ge(s["stored"], 2 * KC * 16)

            @block.scalar
            def _(act):
                for sl in range(2):
                    t = CTX + 512 * sl
                    for k in range(KC):
                        i = sl * KC + k
                        if i >= 2:
                            act.wait_ge(s["summed"], i - 1)
                        act.activation(sq[i % 2][:], x[:, k, t:t + 512], ACT.Square).then_inc(s["squared"], 1)
                    act.wait_ge(s["summed"], (sl + 1) * KC)
                    if sl:
                        act.wait_ge(s["inverted"], 1)
                    act.activation(root[:], ms[sl][:], ACT.Sqrt, bias=eps[:]).then_inc(s["rooted"], 1)

            @block.tensor
            def _(pe):
                for i in range(2 * KC):
                    pe.wait_ge(s["squared"], i + 1)
                    pe.matmul(ms[i // KC][:], ones[:], sq[i % 2][:], start=(i % KC == 0), stop=(i % KC == KC - 1)).then_inc(s["summed"], 1)

            @block.vector
            def _(dve):
                dve.wait_ge(s["set_in"], 16)
                for sl in range(2):
                    t = CTX + 512 * sl
                    dve.wait_ge(s["rooted"], sl + 1)
                    dve.reciprocal(inv[sl][:], root[:]).then_inc(s["inverted"], 1)
                    dve.wait_ge(s["inverted"], sl + 1)
                    for k in range(KC):
                        dve.scalar_tensor_tensor(y[:, k, sl * 512:sl * 512 + 512], x[:, k, t:t + 512], nw[:, k:k + 1], inv[sl][:],
                                                 ALU.mult, ALU.mult).then_inc(s["done"], 1)


def begin(nc, loads, zeros, fills):
    with Stage(nc, "begin") as st:
        zero = st.sb("zero", [P, G_Z - S_V])
        loaded, zeroed, filled, stored = (st.sem(n) for n in ("loaded", "zeroed", "filled", "stored"))
        with nc.Block() as block:
            @block.sync
            def _(sp):
                for dst, src in loads:
                    sp.dma_start(dst, src).then_inc(loaded, 16)
                sp.wait_ge(zeroed, 1)
                for dst in zeros:
                    sp.dma_start(dst, zero[0:dst.shape[0], 0:dst.shape[1]]).then_inc(stored, 16)
                sp.wait_ge(stored, 16 * len(zeros))
                sp.wait_ge(loaded, 16 * len(loads))

            @block.vector
            def _(dve):
                dve.memset(zero[:], 0.0).then_inc(zeroed, 1)
                for dst, value in fills:
                    dve.memset(dst, value).then_inc(filled, 1)
                dve.wait_ge(filled, len(fills))


def program(nc, x_in, cs, ada_w, ada_b, norm_mix, norm_ffn, w_in, small, sinks, conv_w, mix_norm, w_out, w_ffn,
            final_norm, mats_in, tri_in, ksteps_in, qsteps_in, rope, win, out):
    scratch = lambda name, shape: nc.dram_tensor(name, shape, F32, kind="Internal").ap()
    proj = scratch("proj", (ROWS, IN_W))
    pack = scratch("pack", (TILES, P, T_W))
    feat = scratch("feat", (TILES, P, F_N, P))
    diag = scratch("diag", (2, 4 * TILES, GH, 32, 32))
    inv = scratch("inv", (4 * TILES, GH, 4, 32, 32))
    tot = scratch("tot", (TILES, P, 16))
    swq = scratch("swq", (TILES, P, 4, P))
    swk = scratch("swk", (P, TOK + 2 * P))
    us = scratch("us", (TILES, P, 512))
    with ExitStack() as mem:
        def sb(name, shape):
            return mem.enter_context(nc.sbuf_tensor(name, shape, F32))

        x = sb("x", [P, KC, TOK])
        mats, tri, ksteps, qsteps = sb("mats", [P, 8, P]), sb("tri", [P, 2, HD]), sb("ksteps", [P, 2]), sb("qsteps", [P, 2, P])
        ones, eps = sb("ones", [P, P]), sb("eps", [P, 1])
        mods = [(sb(f"mod{l}", [P, NMOD * KC, 2]), sb(f"amix{l}", [P, KC, 2]), sb(f"affn{l}", [P, KC, 2])) for l in range(DEPTH)]
        pads = [(0, P), (P, P + 1), (R0 + 1 + CTX, R0 + 2 + CTX), (ROWS - P - 1, ROWS - 1), (ROWS - 1, ROWS)]
        begin(nc, [(x[:], x_in), (mats[:], mats_in), (tri[:], tri_in), (ksteps[:], ksteps_in), (qsteps[:], qsteps_in)],
              [proj[a:b, S_V:G_Z] for a, b in pads] + [swk[:, 0:P], swk[:, TOK + P:TOK + 2 * P]],
              [(ones[:], 1.0 / DM), (eps[:], EPS)])
        for layer in range(DEPTH):
            lo = 0 if layer < DEPTH - 1 else CTX
            t0 = lo // P
            mod, amix, affn = mods[layer]
            if layer == 0:
                modulation(nc, layer, cs, ada_w, ada_b, norm_mix, norm_ffn, mats[:, C_ID, :], mod, amix, affn)
            project(nc, layer, x, w_in, proj, mod, amix, ones, eps)
            prepare(nc, layer, proj, rope, conv_w, small, mats, tri, ksteps, qsteps, pack, feat, diag, tot, swq, swk)
            solve(nc, layer, diag, inv, (lambda st: modulating(nc, st, layer + 1, cs, ada_w, ada_b, norm_mix, norm_ffn, mats[:, C_ID, :],
                                                               *mods[layer + 1])) if layer + 1 < DEPTH else None)
            join(nc, layer, pack, inv, feat, us)
            with Stage(nc, f"o{layer}") as so:
                o_ret, o_gdn = so.sb("o_ret", [P, 2, 2, TOK]), so.sb("o_gdn", [P, 2, 2, TOK])
                scan(nc, layer, pack, feat, tot, us, small, mats, o_ret, o_gdn)
                y_hi, y_lo = so.sb("y_hi", [P, KC, TOK], F32R), so.sb("y_lo", [P, KC, TOK], F32R)
                gated(nc, layer, t0, proj, mix_norm, mats, o_ret, o_gdn, y_hi, y_lo, eps)
                window(nc, layer, t0, proj, swq, swk, win, sinks, mats, y_hi, y_lo)
                mixed(nc, layer, lo, x, w_out[layer], mod, y_hi, y_lo)
            ffn(nc, layer, x, lo, w_ffn[layer], mod, affn, ones, eps)
        final(nc, x, final_norm, out, ones, eps)


def ffn_units(w1, w2):
    units = []
    for j0 in range(0, FC, 4):
        js = min(4, FC - j0)
        for j in range(j0, j0 + js):
            for half in range(2):
                c = w1[:, half * DFF + j * P:half * DFF + (j + 1) * P]
                units.append(c.reshape(KC, P, P).transpose(1, 0, 2).reshape(P, DM))
        wide = DM // js
        rows = w2[j0 * P:(j0 + js) * P].reshape(js, P, DM)
        for m in range(0, DM, wide):
            units.append(rows[:, :, m:m + wide].transpose(1, 0, 2).reshape(P, DM))
    return np.stack(units)


def kernel(**inputs):
    import concourse.bacc as bacc
    from concourse.bass_utils import run_bass_kernel_spmd

    a = {k: np.asarray(v) for k, v in inputs.items()}
    feature = lambda v: np.ascontiguousarray(v.reshape(-1, P).T)
    spread = lambda v: np.broadcast_to(v.reshape(1, -1), (P, v.size))
    mats, tri, ksteps, qsteps, rope, win = constants()
    tokens = np.concatenate([a["ctx"][0], a["x"][0]], 0)
    arrays = {
        "x_in": tokens.T.reshape(KC, P, TOK).transpose(1, 0, 2),
        "cs": np.stack([feature(a["c"][0]), feature(a["c_ctx"])], -1),
        "ada_w": a["ada_w"],
        "ada_b": np.stack([feature(v) for v in a["ada_b"]]),
        "norm_mix": np.stack([feature(v) for v in a["norm_mix_w"]]),
        "norm_ffn": np.stack([feature(v) for v in a["norm_ffn_w"]]),
        "w_in": a["w_in"],
        "small": np.stack([np.stack([spread(a[n][l]) for n in ("gdn_a_log", "gdn_dt_bias", "ret_rate")], 1) for l in range(DEPTH)]),
        "sinks": np.stack([spread(v) for v in a["swa_sinks"]]),
        "conv_w": np.broadcast_to(a["gdn_conv_w"][:, None], (DEPTH, P, 3, 768)),
        "mix_norm": np.stack([np.concatenate([feature(a["ret_norm_w"][l]), feature(np.tile(a["gdn_norm_w"][l], 4))], 1) for l in range(DEPTH)]),
        "w_out": a["w_out"].reshape(DEPTH, KC, P, KC, P).transpose(0, 3, 2, 1, 4).reshape(DEPTH, KC, P, DM),
        "w_ffn": np.stack([ffn_units(a["w_ffn_in"][l], a["w_ffn_out"][l]) for l in range(DEPTH)]),
        "final_norm": feature(a["final_norm_w"]),
        "mats_in": mats, "tri_in": tri, "ksteps_in": ksteps, "qsteps_in": qsteps, "rope": rope, "win": win,
    }
    arrays = {k: np.ascontiguousarray(v) for k, v in arrays.items()}
    nc = bacc.Bacc("TRN2", target_bir_lowering=False, num_devices=1)
    args = [nc.dram_tensor(k, v.shape, mybir.dt.from_np(v.dtype), kind="ExternalInput").ap() for k, v in arrays.items()]
    args.append(nc.dram_tensor("out", (P, KC, LAT), F32, kind="ExternalOutput").ap())
    program(nc, *args)
    r = run_bass_kernel_spmd(nc, [arrays], core_ids=[0])
    out = r.results[0]["out"]
    return np.ascontiguousarray(out.transpose(1, 0, 2).reshape(DM, LAT).T)[None]
```

```python
from contextlib import ExitStack

import numpy as np

import concourse.bass as bass
from concourse import mybir

ALU = mybir.AluOpType
ACT = mybir.ActivationFunctionType
AX = mybir.AxisListType
F32 = mybir.dt.float32
F32R = mybir.dt.float32r

P = 128
DM = 1024
KC = DM // P
CTX, LAT = 256, 1024
TOK = CTX + LAT
TILES = TOK // P
DEPTH = 2
HD = 64
RH, SH, GH = 4, 8, 4
IN_W = 2832
GROUPS, GW = 6, IN_W // 6
DFF = 2816
FC = DFF // P
NMOD = 6
EPS = 1e-6
NEG = -1e30

R_Q, R_K, R_V, R_G = 0, 256, 512, 768
S_Q, S_K, S_V = 1024, 1536, 1664
G_Q, G_K, G_V, G_Z, G_A, G_B = 1792, 2048, 2304, 2560, 2816, 2824
R0 = P
ROWS = R0 + TOK + 3 + P


def row_of(t):
    return R0 + 1 + t * P + (t >= 2)



def token_slices(lo):
    full = [(0, 256), (256, 512), (768, 512)]
    return full if lo == 0 else full[1:]


class Stage:

    def __init__(self, nc, name):
        self.nc, self.name, self.sems = nc, name, []

    def __enter__(self):
        self.mem = ExitStack()
        return self

    def sb(self, name, shape, dt=F32):
        return self.mem.enter_context(self.nc.sbuf_tensor(f"{self.name}_{name}", shape, dt))

    def ps(self, name, shape, dt=F32):
        return self.mem.enter_context(self.nc.psum_tensor(f"{self.name}_{name}", shape, dt))

    def sem(self, name):
        s = self.mem.enter_context(self.nc.semaphore(f"{self.name}_{name}"))
        self.sems.append(s)
        return s

    def __exit__(self, *a):
        if a[0] is None:
            self.nc.clear_and_free_semaphores(self.sems)
            self.nc.all_engine_barrier()
        self.mem.close()


def mix_part(layer):
    return layer, 0, 2


def rest_part(layer):
    return layer, 2, NMOD - 2


def modulation(nc, parts, cs, ada_w, ada_b, norms, ident, mods):
    with Stage(nc, "ada") as st:
        sync, scalar, tensor, gpsimd = modulating(nc, st, parts, cs, ada_w, ada_b, norms, ident, mods)
        with nc.Block() as block:
            block.sync(sync)
            block.scalar(scalar)
            block.tensor(tensor)
            block.gpsimd(gpsimd)


def modulating(nc, st, parts, cs, ada_w, ada_b, norms, ident, mods):
    TURNS = sum(n for layer, first, n in parts)
    NM = TURNS * KC
    c_in = st.sb("m_c_in", [P, KC, 2])
    c_s = st.sb("m_c_s", [P, KC, 2])
    w = [st.sb(f"m_w{u}", [P, KC, 512]) for u in range(2)]
    rows = st.sb("m_rows", [2, TURNS * DM])
    bias = st.sb("m_bias", [P, NM])
    product = st.sb("m_product", [P, NM, 2])
    nw = st.sb("m_nw", [P, len(parts), KC])
    acc = [st.ps(f"m_acc{u}", [2, 512]) for u in range(2)]
    cols = st.ps("m_cols", [P, NM * 2])
    small_in, silu_done, turned, cols_out = st.sem("m_small_in"), st.sem("m_silu_done"), st.sem("m_turned"), st.sem("m_cols_out")
    w_in = [st.sem(f"m_w_in{u}") for u in range(2)]
    acc_done = [st.sem(f"m_acc_done{u}") for u in range(2)]
    row_done = [st.sem(f"m_row_done{u}") for u in range(2)]
    mod_done, plus_one, scale_done = st.sem("m_mod_done"), st.sem("m_plus_one"), st.sem("m_scale_done")
    starts = [sum(n for _, _, n in parts[:i]) for i in range(len(parts))]

    def sync(sp):
        sp.dma_start(c_in[:], cs).then_inc(small_in, 16)
        for i, (layer, first, n) in enumerate(parts):
            sp.dma_start(bias[:, starts[i] * KC:(starts[i] + n) * KC], ada_b[layer][:, first * KC:(first + n) * KC]).then_inc(small_in, 16)
            sp.dma_start(nw[:, i, :], norms[0 if first == 0 else 1][layer]).then_inc(small_in, 16)
        for i, (layer, first, n) in enumerate(parts):
            src = ada_w[layer].rearrange("(k p) n -> p k n", p=P)
            with sp.Fori(0, n) as g:
                for u in range(2):
                    sp.wait_ge(acc_done[u], g + starts[i])
                    sp.dma_start(w[u][:], src[:, :, bass.ds(g * 1024 + (first * 1024 + u * 512), 512)]).then_inc(w_in[u], 16)

    def scalar(act):
        act.wait_ge(small_in, 16 + 32 * len(parts))
        act.activation(c_s[:], c_in[:], ACT.Silu).then_inc(silu_done, 1)
        with act.Fori(0, TURNS) as g:
            for u in range(2):
                act.wait_ge(acc_done[u], g + 1)
                act.activation(rows[:, bass.ds(g * 1024 + u * 512, 512)], acc[u][:], ACT.Copy).then_inc(row_done[u], 1)
        act.wait_ge(turned, 1)
        act.activation(product[:].rearrange("p m v -> p (m v)"), cols[:], ACT.Copy).then_inc(cols_out, 1)

    def tensor(pe):
        pe.wait_ge(silu_done, 1)
        with pe.Fori(0, TURNS) as g:
            for u in range(2):
                pe.wait_ge(w_in[u], g * 16 + 16)
                pe.wait_ge(row_done[u], g)
                for k in range(KC):
                    mm = pe.matmul(acc[u][:], c_s[:, k, :], w[u][:, k, :], start=(k == 0), stop=(k == KC - 1))
                mm.then_inc(acc_done[u], 1)
        for u in range(2):
            pe.wait_ge(row_done[u], TURNS)
        for m in range(NM):
            mm = pe.transpose(cols[:, 2 * m:2 * m + 2], rows[:, m * P:(m + 1) * P], ident[0:2, 0:2])
        mm.then_inc(turned, 1)

    def gpsimd(pool):
        pool.wait_ge(small_in, 16 + 32 * len(parts))
        pool.wait_ge(cols_out, 1)
        for i, (layer, first, n) in enumerate(parts):
            mod, amix, affn = mods[layer]
            here = slice(starts[i] * KC, (starts[i] + n) * KC)
            pool.tensor_tensor(mod[:, first * KC:(first + n) * KC, :], product[:, here, :],
                               bias[:, here].unsqueeze(2).broadcast_to([P, n * KC, 2]), ALU.add).then_inc(mod_done, 1)
            pool.wait_ge(mod_done, i + 1)
            sc, out = (mod[:, KC:2 * KC, :], amix) if first == 0 else (mod[:, 4 * KC:5 * KC, :], affn)
            pool.tensor_scalar(out[:], sc, 1.0, None, ALU.add).then_inc(plus_one, 1)
            pool.wait_ge(plus_one, i + 1)
            pool.tensor_tensor(out[:], out[:], nw[:, i, :].unsqueeze(2).broadcast_to([P, KC, 2]), ALU.mult).then_inc(scale_done, 1)
        pool.wait_ge(scale_done, len(parts))

    return sync, scalar, tensor, gpsimd


def normed(nc, st, x, scale, mod, shift0, lo, hi_t, lo_t, ones, eps, bufs=None, ms=None):
    slices = token_slices(lo)
    if bufs is None:
        bufs = ([st.sb(f"sq{u}", [P, 512])[:] for u in range(2)], [st.sb(f"scaled{u}", [P, 512])[:] for u in range(2)],
                [st.sb(f"inv{s}", [P, n])[:] for s, (t0, n) in enumerate(slices)])
        ms = [st.ps(f"ms{s}", [P, 512]) for s in range(len(slices))]
    sq, scaled, inv = bufs
    squared, summed, rooted, inverted = st.sem("squared"), st.sem("summed"), st.sem("rooted"), st.sem("inverted")
    scaled_s, rounded, h_ready = st.sem("scaled"), st.sem("rounded"), st.sem("h_ready")

    def act_norm(act, between=None):
        for s, (t0, n) in enumerate(slices):
            for k in range(KC):
                i = s * KC + k
                if i >= 2:
                    act.wait_ge(summed, i - 1)
                act.activation(sq[i % 2][:, 0:n], x[:, k, t0:t0 + n], ACT.Square).then_inc(squared, 1)
        for s, (t0, n) in enumerate(slices):
            act.wait_ge(summed, (s + 1) * KC)
            act.activation(inv[s], ms[s][:, 0:n], ACT.Sqrt, bias=eps[:]).then_inc(rooted, 1)
        if between:
            between(act)
        for s, (t0, n) in enumerate(slices):
            v = 1 if t0 < CTX else 0
            for k in range(KC):
                act.wait_ge(scaled_s, s * KC + k + 1)
                act.activation(hi_t[:, k, t0:t0 + n], scaled[(s * KC + k) % 2][:, 0:n], ACT.Identity,
                               bias=mod[:, shift0 + k, v:v + 1]).then_inc(rounded, 1)

    def pe_norm(pe):
        for s, (t0, n) in enumerate(slices):
            for k in range(KC):
                pe.wait_ge(squared, s * KC + k + 1)
                pe.matmul(ms[s][:, 0:n], ones[:], sq[(s * KC + k) % 2][:, 0:n], start=(k == 0), stop=(k == KC - 1)).then_inc(summed, 1)

    def dve_norm(dve):
        def scale_one(i):
            s, k = i // KC, i % KC
            t0, n = slices[s]
            v = 1 if t0 < CTX else 0
            if k == 0:
                dve.wait_ge(rooted, s + 1)
                dve.reciprocal(inv[s], inv[s]).then_inc(inverted, 1)
                dve.wait_ge(inverted, s + 1)
            if i >= 2:
                dve.wait_ge(h_ready, i - 1)
            dve.scalar_tensor_tensor(scaled[i % 2][:, 0:n], x[:, k, t0:t0 + n], scale[:, k, v:v + 1], inv[s],
                                     ALU.mult, ALU.mult).then_inc(scaled_s, 1)

        parts = len(slices) * KC
        scale_one(0)
        for i in range(parts):
            s, k = i // KC, i % KC
            t0, n = slices[s]
            v = 1 if t0 < CTX else 0
            if i + 1 < parts:
                scale_one(i + 1)
            dve.wait_ge(rounded, i + 1)
            dve.scalar_tensor_tensor(lo_t[:, k, t0:t0 + n], scaled[i % 2][:, 0:n], mod[:, shift0 + k, v:v + 1],
                                     hi_t[:, k, t0:t0 + n].bitcast(F32), ALU.add, ALU.subtract).then_inc(h_ready, 1)

    return act_norm, pe_norm, dve_norm, h_ready


def project(nc, layer, x, w_in, proj, mod, amix, ones, eps):
    with Stage(nc, f"prj{layer}") as st:
        h_hi = st.sb("h_hi", [P, KC, TOK], F32R)
        h_lo = st.sb("h_lo", [P, KC, TOK], F32R)
        act_norm, pe_norm, dve_norm, h_ready = normed(nc, st, x, amix, mod, 0, 0, h_hi, h_lo, ones, eps)
        raw = st.sb("raw", [P, KC, GW])
        w_hi = st.sb("w_hi", [P, KC, GW], F32R)
        w_lo = st.sb("w_lo", [P, KC, GW], F32R)
        out = st.sb("out", [P, 5, GW])
        acc = [st.ps(f"acc{b}", [P, 512]) for b in range(5)]
        w_landed = [st.sem(f"w_landed{k}") for k in range(KC)]
        w_rounded, w_split, w_used = st.sem("w_rounded"), st.sem("w_split"), st.sem("w_used")
        summed = st.sem("psum_done")
        copied = [st.sem(f"copied{b}") for b in range(5)]
        stored = [st.sem(f"stored{b}") for b in range(5)]
        src = w_in[layer].rearrange("(k p) n -> p k n", p=P)
        with nc.Block() as block:
            @block.sync
            def _(sp):
                with sp.Fori(0, GROUPS) as g:
                    for k in range(KC):
                        sp.wait_ge(w_split, g * KC)
                        sp.dma_start(raw[:, k, :], src[:, k, bass.ds(g * GW, GW)]).then_inc(w_landed[k], 16)

            def split_hi(act, g):
                for k in range(KC):
                    act.wait_ge(w_landed[k], g * 16 + 16)
                    if k < KC - 1:
                        act.wait_ge(w_used, g * (KC - 1) + k + 1)
                    else:
                        act.wait_ge(summed, g * TILES)
                    act.activation(w_hi[:, k, :], raw[:, k, :], ACT.Copy).then_inc(w_rounded, 1)

            def split_lo(dve, g):
                for k in range(KC):
                    dve.wait_ge(w_rounded, g * KC + k + 1)
                    dve.tensor_tensor(w_lo[:, k, :], raw[:, k, :], w_hi[:, k, :].bitcast(F32), ALU.subtract).then_inc(w_split, 1)

            @block.scalar
            def _(act):
                act_norm(act, between=lambda act: split_hi(act, 0))

                def copy(g, t):
                    act.wait_ge(summed, g * TILES + t + 1)
                    act.wait_ge(stored[t % 5], (g * 2 + t // 5) * 16)
                    act.activation(out[:, t % 5, :], acc[t % 5][:, 0:GW], ACT.Copy).then_inc(copied[t % 5], 1)

                with act.Fori(0, GROUPS - 1) as g:
                    for t in range(0, TILES, 2):
                        copy(g, t)
                    split_hi(act, g + 1)
                for t in range(0, TILES, 2):
                    copy(GROUPS - 1, t)

            @block.vector
            def _(dve):
                split_lo(dve, 0)
                dve_norm(dve)

                def copy(g, t):
                    dve.wait_ge(summed, g * TILES + t + 1)
                    dve.wait_ge(stored[t % 5], (g * 2 + t // 5) * 16)
                    dve.tensor_copy(out[:, t % 5, :], acc[t % 5][:, 0:GW]).then_inc(copied[t % 5], 1)

                with dve.Fori(0, GROUPS - 1) as g:
                    for t in range(1, TILES - 1, 2):
                        copy(g, t)
                    split_lo(dve, g + 1)
                    copy(g, TILES - 1)
                for t in range(1, TILES, 2):
                    copy(GROUPS - 1, t)

            @block.tensor
            def _(pe):
                pe.sem_inc(w_used, KC - 1)
                pe_norm(pe)
                with pe.Fori(0, GROUPS) as g:
                    for t in range(TILES):
                        tok = slice(t * P, (t + 1) * P)
                        pe.wait_ge(h_ready, (1 + sum(t * P >= t0 + n for t0, n in token_slices(0))) * KC)
                        pe.wait_ge(copied[t % 5], g * 2 + t // 5)
                        for k in range(KC):
                            if t == 0:
                                pe.wait_ge(w_split, g * KC + k + 1)
                            for a, b, s in ((h_hi, w_hi, 0), (h_lo, w_hi, 1), (h_hi, w_lo, 2)):
                                mm = pe.matmul(acc[t % 5][:, 0:GW], a[:, k, tok], b[:, k, :],
                                               start=(k == 0 and s == 0), stop=(k == KC - 1 and s == 2))
                            if t == TILES - 1 and k < KC - 1:
                                mm.then_inc(w_used, 1)
                        mm.then_inc(summed, 1)

            @block.gpsimd
            def _(pool):
                with pool.Fori(0, GROUPS) as g:
                    for t in range(TILES):
                        pool.wait_ge(copied[t % 5], g * 2 + t // 5 + 1)
                        row = row_of(t)
                        pool.dma_start(proj[row:row + P, bass.ds(g * GW, GW)], out[:, t % 5, :]).then_inc(stored[t % 5], 16)
                for b in range(5):
                    pool.wait_ge(stored[b], GROUPS * 2 * 16)


class WeightUnits:

    def __init__(self, st, units):
        self.units = units
        self.raw = [st.sb(f"raw{u}", [P, DM]) for u in range(2)]
        self.hi = [st.sb(f"w_hi{u}", [P, DM], F32R) for u in range(2)]
        self.lo = [st.sb(f"w_lo{u}", [P, DM], F32R) for u in range(2)]
        self.landed = [st.sem(f"w_landed{u}") for u in range(2)]
        self.rounded = [st.sem(f"w_rounded{u}") for u in range(2)]
        self.ready = [st.sem(f"w_ready{u}") for u in range(2)]
        self.used = [st.sem(f"w_used{u}") for u in range(2)]

    def load_all(self, sp, turns):
        with sp.Fori(0, turns) as n:
            for u in range(2):
                sp.wait_ge(self.ready[u], n)
                sp.dma_start(self.raw[u][:], self.units[bass.ds(n * 2 + u, 1)].rearrange("a p n -> (a p) n")).then_inc(self.landed[u], 16)

    def round(self, act, u, n):
        act.wait_ge(self.landed[u], n * 16 + 16)
        act.wait_ge(self.used[u], n + u)
        act.activation(self.hi[u][:], self.raw[u][:], ACT.Copy).then_inc(self.rounded[u], 1)

    def rest(self, dve, u, n):
        dve.wait_ge(self.rounded[u], n + 1)
        dve.tensor_tensor(self.lo[u][:], self.raw[u][:], self.hi[u][:].bitcast(F32), ALU.subtract).then_inc(self.ready[u], 1)


def three_passes(pe, out, w_hi, w_lo, b_hi, b_lo, first, last, begun=None):
    mm = pe.matmul(out, w_hi, b_hi, start=first, stop=False)
    if begun is not None:
        mm.then_inc(begun, 1)
    pe.matmul(out, w_hi, b_lo, start=False, stop=False)
    return pe.matmul(out, w_lo, b_hi, start=False, stop=last)


def ffn(nc, layer, x, lo, units, mod, affn, ones, eps):
    J = 4
    NFULL, REST = FC // J, FC % J
    TURNS = 6
    SETS = 8
    LAST, LSET = NFULL * TURNS, NFULL * SETS
    slices = token_slices(lo)
    with Stage(nc, f"ffn{layer}") as st:
        h_hi = st.sb("h_hi", [P, KC, TOK], F32R)
        h_lo = st.sb("h_lo", [P, KC, TOK], F32R)
        a_hi = st.sb("a_hi", [P, J, TOK], F32R)
        a_lo = st.sb("a_lo", [P, J, TOK], F32R)
        sil = st.sb("sil", [P, TOK])
        prod = st.sb("prod", [P, TOK])
        bank = [[st.ps(f"bank{i}{s}", [P, 512]) for s in range(len(slices))] for i in range(2)]
        bufs = ([st.sb(f"sq{u}", [P, 512])[:] for u in range(2)], [prod[:, 0:512], prod[:, 512:1024]],
                [sil[:, t0:t0 + ln] for t0, ln in slices])
        act_norm, pe_norm, dve_norm, h_ready = normed(nc, st, x, affn, mod, 3 * KC, lo, h_hi, h_lo, ones, eps, bufs, bank[1])
        w = WeightUnits(st, units)
        full = [[st.sem(f"full{i}{s}") for s in range(len(slices))] for i in range(2)]
        free = [[st.sem(f"free{i}{s}") for s in range(len(slices))] for i in range(2)]
        a_rounded, a_ready = st.sem("a_rounded"), st.sem("a_ready")
        NS = len(slices)

        def pe_up(pe, n, b):
            for u in range(2):
                pe.wait_ge(w.ready[u], n + 1)
                for s, (t0, ln) in enumerate(slices):
                    pe.wait_ge(h_ready, (s + 1) * KC)
                    pe.wait_ge(free[u][s], b)
                    for k in range(KC):
                        f = slice(k * P, (k + 1) * P)
                        mm = three_passes(pe, bank[u][s][:, 0:ln], w.hi[u][:, f], w.lo[u][:, f],
                                          h_hi[:, k, t0:t0 + ln], h_lo[:, k, t0:t0 + ln], k == 0, k == KC - 1,
                                          w.used[1 - u] if s == 0 and k == 0 else None)
                    mm.then_inc(full[u][s], 1)

        def act_up(act, j, c, n, b, before):
            for s, (t0, ln) in enumerate(slices):
                act.wait_ge(full[0][s], b + 1)
                act.wait_ge(free[1][s], b)
                act.activation(sil[:, t0:t0 + ln], bank[0][s][:, 0:ln], ACT.Silu).then_inc(free[0][s], 1)
            w.round(act, 0, n + 1)
            act.wait_ge(w.used[1], before + 1)
            for s, (t0, ln) in enumerate(slices):
                act.wait_ge(free[1][s], b + 1)
                act.activation(a_hi[:, j, t0:t0 + ln], prod[:, t0:t0 + ln], ACT.Copy).then_inc(a_rounded, 1)
            w.round(act, 1, n + 1)

        def dve_up(dve, j, c, n, b):
            w.rest(dve, 0, n + 1)

            def rest(s):
                t0, ln = slices[s]
                dve.wait_ge(a_rounded, c * NS + s + 1)
                dve.tensor_tensor(a_lo[:, j, t0:t0 + ln], prod[:, t0:t0 + ln], a_hi[:, j, t0:t0 + ln].bitcast(F32),
                                  ALU.subtract).then_inc(a_ready, 1)

            for s, (t0, ln) in enumerate(slices):
                dve.wait_ge(a_ready, c * NS)
                dve.wait_ge(full[1][s], b + 1)
                dve.wait_ge(free[0][s], b + 1)
                dve.tensor_tensor(prod[:, t0:t0 + ln], sil[:, t0:t0 + ln], bank[1][s][:, 0:ln], ALU.mult).then_inc(free[1][s], 1)
                if s >= 1:
                    rest(s - 1)
            rest(NS - 1)
            w.rest(dve, 1, n + 1)

        def pe_down(pe, n, b, js, each, c):
            pe.wait_ge(a_ready, (c - 1) * NS)
            for u in range(2):
                pe.wait_ge(w.ready[u], n + 1)
                wide = each * P
                for e in range(each):
                    i, use = e % 2, b + u * (each // 2) + e // 2
                    for s, (t0, ln) in enumerate(slices):
                        pe.wait_ge(free[i][s], use)
                        for j in range(js):
                            if j == js - 1:
                                pe.wait_ge(a_ready, (c - 1) * NS + s + 1)
                            f = slice(j * wide + e * P, j * wide + (e + 1) * P)
                            mm = three_passes(pe, bank[i][s][:, 0:ln], w.hi[u][:, f], w.lo[u][:, f],
                                              a_hi[:, j, t0:t0 + ln], a_lo[:, j, t0:t0 + ln], j == 0, j == js - 1,
                                              w.used[1 - u] if e == 0 and s == 0 and j == 0 else None)
                        mm.then_inc(full[i][s], 1)

        def dve_down(dve, n, b, m0, each, more):
            for u in range(2):
                for e in range(each):
                    i, use = e % 2, b + u * (each // 2) + e // 2
                    m = m0 + (u * each + e)
                    for s, (t0, ln) in enumerate(slices):
                        v = 1 if t0 < CTX else 0
                        dve.wait_ge(full[i][s], use + 1)
                        xs = x[:, bass.ds(m, 1), t0:t0 + ln].rearrange("p a n -> p (a n)")
                        dve.scalar_tensor_tensor(xs, bank[i][s][:, 0:ln], mod[:, bass.ds(m + 5 * KC, 1), v], xs,
                                                 ALU.mult, ALU.add).then_inc(free[i][s], 1)
                if more:
                    w.rest(dve, u, n + 1)

        def act_down(act, n, more):
            if more:
                for u in range(2):
                    w.round(act, u, n + 1)

        with nc.Block() as block:
            @block.sync
            def _(sp):
                w.load_all(sp, LAST + REST + 1)

            @block.scalar
            def _(act):
                act_norm(act, between=lambda act: w.round(act, 0, 0))
                w.round(act, 1, 0)
                with act.Fori(0, NFULL) as g:
                    with act.Fori(0, J) as j:
                        act_up(act, bass.ds(j, 1), g * J + j, g * TURNS + j, g * SETS + j, g * TURNS)
                    with act.Fori(0, 2) as q:
                        act_down(act, g * TURNS + J + q, True)
                for j in range(REST):
                    act_up(act, bass.ds(j, 1), NFULL * J + j, LAST + j, LSET + j, LAST)

            @block.vector
            def _(dve):
                w.rest(dve, 0, 0)
                dve_norm(dve)
                w.rest(dve, 1, 0)
                with dve.Fori(0, NFULL) as g:
                    with dve.Fori(0, J) as j:
                        dve_up(dve, bass.ds(j, 1), g * J + j, g * TURNS + j, g * SETS + j)
                    with dve.Fori(0, 2) as q:
                        dve_down(dve, g * TURNS + J + q, g * SETS + J + q * 2, q * 4, 2, True)
                for j in range(REST):
                    dve_up(dve, bass.ds(j, 1), NFULL * J + j, LAST + j, LSET + j)
                dve_down(dve, LAST + REST, LSET + REST, 0, 4, False)

            @block.tensor
            def _(pe):
                pe_norm(pe)
                with pe.Fori(0, NFULL) as g:
                    with pe.Fori(0, J) as j:
                        pe_up(pe, g * TURNS + j, g * SETS + j)
                    with pe.Fori(0, 2) as q:
                        pe_down(pe, g * TURNS + J + q, g * SETS + J + q * 2, J, 2, g * J + J)
                for j in range(REST):
                    pe_up(pe, LAST + j, LSET + j)
                pe_down(pe, LAST + REST, LSET + REST, REST, 4, FC)


T_RK, T_RV, T_NK, T_LT, T_GV = 0, 256, 768, 1280, 1792
T_D, T_KT, T_AT = 2048, 0, 256
T_W = 3072
F_RQ, F_RK = 0, 2
F_D, F_DN, F_RQD, F_GQD, F_GW = 4, 6, 0, 2, 4
F_N = F_D + 2 * F_DN
C_ID, C_LE, C_GE, C_GT, C_LT, C_C0, C_C1, C_DIST = range(8)


def constants():
    l, i = np.arange(P)[:, None], np.arange(P)[None, :]
    same = (l // 64) == (i // 64)
    mats = [l == i, same & (l <= i), same & (l >= i), same & (l > i), same & (l < i),
            (l < 64) & (i >= 0), (l >= 64) & (i >= 0)]
    mats = [m.astype(np.float32) for m in mats] + [(i - l).astype(np.float32)]
    mats = np.stack(mats, 1)
    lc, ic = (np.arange(P) % 64)[:, None], np.arange(64)[None, :]
    tri = np.stack([lc <= ic, lc >= ic], 1).astype(np.float32)
    ksteps = np.stack([P - 1.0 - np.arange(P), np.arange(P) + 0.0], 1).astype(np.float32)
    qsteps = np.broadcast_to(np.stack([np.arange(P) + 1.0, P - np.arange(P) + 0.0]), (P, 2, P)).astype(np.float32)
    rope = np.zeros((TILES, P, 2, 64), np.float32)
    rope[:2, :, 0] = 1.0
    pos = np.arange(LAT)
    freqs = np.float32(10000.0) ** (-np.arange(16, dtype=np.float32) / np.float32(16))
    for axis, at in enumerate((pos // 64, pos % 64)):
        ang = (at.astype(np.float32)[:, None] * freqs).reshape(8, P, 16)
        c, s = np.cos(ang), np.sin(ang)
        rope[2:, :, 0, 32 * axis:32 * axis + 32] = np.concatenate([c, c], -1)
        rope[2:, :, 1, 32 * axis:32 * axis + 32] = np.concatenate([-s, s], -1)
    q, k = np.arange(P)[:, None], np.arange(3 * P)[None, :] - P
    win = np.zeros((TILES, P, 3 * P), np.float32)
    win[:2] = NEG
    for t in range(2, TILES):
        at = (t - 2) * P + k
        win[t] = np.where((np.abs(q - k) <= 128) & (at >= 0) & (at < LAT), 0.0, NEG)
    return mats, tri, ksteps, qsteps, rope, win


def signals(st, names):
    return {n: st.sem(n) for n in names.split()}


def settle(eng, passed):
    eng.sem_inc(passed, 1)


def prepare(nc, layer, proj, rope, conv_w, small, mats, tri, ksteps, qsteps, pack, feat, diag, tot, swq, swk):
    with Stage(nc, f"pre{layer}") as st:
        dual = lambda n, shape: [st.sb(f"{n}{u}", shape) for u in range(2)]
        pr = dual("pr", [P, IN_W])
        before, after = dual("before", [P, 768]), dual("after", [P, 768])
        rp = dual("rp", [P, 2, 64])
        cw = st.sb("cw", [P, 3, 768])
        sm = st.sb("sm", [P, 3, 8])
        al, dtb, rate = sm[:, 0, :], sm[:, 1, :], sm[:, 2, :]
        lg = st.sb("lg", [P, 8])
        kd = st.sb("kd", [P, 2, RH])
        qd = st.sb("qd", [P, 2, 2, P])
        hot, swp = st.sb("hot", [P, 1152]), st.sb("swp", [P, 1152])
        hp = st.sb("hp", [P, 512])
        c0, c1, c2 = st.sb("c0", [P, 768]), st.sb("c1", [P, 768]), st.sb("c2", [P, 768])
        cv = st.sb("cv", [P, 768])
        sq = st.sb("sq", [P, 512])
        ss, rt, rn = st.sb("ss", [P, 8]), st.sb("rt", [P, 8]), st.sb("rn", [P, 8])
        ab = st.sb("ab", [P, TILES, 16])
        xa, xn, xe, xl, g = (st.sb(n, [P, TILES, 8]) for n in ("xa", "xn", "xe", "xl", "g"))
        bm, be, b1, beta = (st.sb(n, [P, TILES, 8]) for n in ("bm", "be", "b1", "beta"))
        es = st.sb("es", [P, 32])
        nt, kt = st.sb("nt", [P, 8]), st.sb("kt", [P, 8])
        gu, mb, e1, de = (st.sb(n, [P, 2, 4, 64]) for n in ("gu", "mb", "e1", "de"))
        kh, qh = st.sb("kh", [P, 256]), st.sb("qh", [P, 256])
        qg = st.sb("qg", [P, 2, 4, 64])
        khT, qhT = st.sb("khT", [P, 2, P]), st.sb("qhT", [P, 2, P])
        pk = dual("pk", [P, T_W])
        ft = dual("ft", [P, F_N, P])
        sqT, skT = st.sb("sqT", [P, 4, P]), st.sb("skT", [P, P])
        one, eps = st.sb("one", [P, 1]), st.sb("eps", [P, 1])
        b_r, b_q, b_k, b_g, b_d, b_s, b_D, b_h = [st.ps(f"b_{n}", [P, 512]) for n in "rqkgdsDh"]
        s = signals(st, """set_in in_gates in_main0 in_main1 in_side0 in_side1 const expa lnready lgn expo decays alneg
            xa xn xe xl sp g bm be b1 beta gu sums es nt kt dsum e1 mb de c0 c1 c2 ca cb cv sq ss rt rn
            kh qh qg rot swapped rotated rk gv turned_r turned_q turned_k turned_g turned_d rv
            ftr ftf ftb ftd sqT skT khT qhT prod_e prod_o lt at nk ktp
            pe_passed sp_passed o_pack0 o_pack1 o_feat0 o_feat1 o_tot o_diag0 o_diag1 o_swq o_swk""")
        in_main, in_side, o_pack, o_feat, o_diag = ([s[f"{n}{u}"] for u in range(2)] for n in ("in_main", "in_side", "o_pack", "o_feat", "o_diag"))
        mat = lambda m: mats[:, m, :]
        B4 = [P, 2, 4, 64]

        def heads(ap, n):
            return ap.rearrange("p (h e) -> p h e", h=n)

        def per_head(ap8):
            return heads(ap8, 2).unsqueeze(3).broadcast_to(B4)

        def over_dirs(ap256):
            return heads(ap256, 4).unsqueeze(1).broadcast_to(B4)

        def tiles(eng, tile):
            with eng.Fori(0, TILES // 2) as n:
                for u in range(2):
                    tile(n, u, n * 2 + u)

        def of_tile(buf, t):
            return buf[:, bass.ds(t, 1), :].rearrange("p a n -> p (a n)")

        def packed(u, col, step=256):
            base = col // (2 * step) * (2 * step) if step > 256 else col
            both = pk[u][:, base:base + 2 * step].rearrange("p (a n) -> p a n", a=2)[:, :, col - base:col - base + 256]
            return both.rearrange("p a (h n) -> p a h n", h=4)

        with nc.Block() as block:
            @block.sync
            def _(sp):
                def wait(q, v):
                    sp.wait_ge(q, v)
                    settle(sp, s["sp_passed"])

                def loads(u, t, row):
                    src = proj[bass.ds(row, P), :]
                    for a, b in ((R_Q, R_G), (S_Q, G_Z)):
                        sp.dma_start(pr[u][:, a:b], src[:, a:b]).then_inc(in_main[u], 16)
                    sp.dma_start(rp[u][:], rope[bass.ds(t, 1)].rearrange("a p c n -> (a p) c n")).then_inc(in_main[u], 16)
                    sp.dma_start(before[u][:], proj[bass.ds(row - 1, P), G_Q:G_Q + 768]).then_inc(in_side[u], 16)
                    sp.dma_start(after[u][:], proj[bass.ds(row + 1, P), G_Q:G_Q + 768]).then_inc(in_side[u], 16)

                def stores(u, t):
                    wait(s["es"], t + 1)
                    sp.dma_start(tot[bass.ds(t, 1)].rearrange("a p n -> (a p) n"), es[:, 16:32]).then_inc(s["o_tot"], 16)
                    for q in (s["sqT"], s["skT"]):
                        wait(q, t + 1)
                    sp.dma_start(swq[bass.ds(t, 1)].rearrange("a p c n -> (a p) c n"), sqT[:]).then_inc(s["o_swq"], 16)
                    sp.dma_start(swk[:, bass.ds(t * P + P, P)], skT[:]).then_inc(s["o_swk"], 16)
                    for q in (s["rk"], s["rv"], s["gv"], s["nk"], s["ktp"], s["lt"], s["at"]):
                        wait(q, t + 1)
                    sp.dma_start(pack[bass.ds(t, 1)].rearrange("a p n -> (a p) n"), pk[u][:]).then_inc(o_pack[u], 16)
                    lt = pk[u][:, T_LT:T_LT + 512].rearrange("p (h i) -> p h i", h=8)
                    for b in range(4):
                        for d in range(2):
                            sp.dma_start(diag[d, bass.ds(t * 4 + b, 1)].rearrange("a h j i -> (a j) h i"),
                                         lt[32 * b:32 * b + 32, 4 * d:4 * d + 4, 32 * (b % 2):32 * (b % 2) + 32]).then_inc(o_diag[u], 16)
                    for q in (s["ftr"], s["ftf"], s["ftb"], s["ftd"]):
                        wait(q, t + 1)
                    for f0, f1 in ((0, F_D + F_GW), (F_D + F_DN, F_N - 2)):
                        sp.dma_start(feat[bass.ds(t, 1)].rearrange("a p f n -> (a p) f n")[:, f0:f1], ft[u][:, f0:f1]).then_inc(o_feat[u], 16)

                sp.dma_start(cw[:], conv_w[layer]).then_inc(s["set_in"], 16)
                sp.dma_start(sm[:], small[layer]).then_inc(s["set_in"], 16)
                for t0, t1 in ((0, 2), (2, TILES)):
                    sp.dma_start(ab[:, t0:t1, :], proj[row_of(t0):row_of(t0) + (t1 - t0) * P, G_A:IN_W].rearrange("(t p) n -> p t n", p=P)).then_inc(s["in_gates"], 16)
                with sp.Fori(0, 1) as t:
                    for u in range(2):
                        loads(u, t + u, t + row_of(u))
                with sp.Fori(0, TILES // 2 - 1) as n:
                    for u in range(2):
                        wait(s["swapped"], (n * 2 + u) * 8 + 8)
                        for q in (s["c0"], s["c2"], s["c1"], s["rot"], s["rv"]):
                            wait(q, n * 2 + u + 1)
                        loads(u, n * 2 + u + 2, n * (2 * P) + row_of(u + 2))
                        stores(u, n * 2 + u)
                with sp.Fori(TILES // 2 - 1, TILES // 2) as n:
                    for u in range(2):
                        stores(u, n * 2 + u)
                for q, n in ((s["o_tot"], 2), (s["o_swq"], 2), (s["o_swk"], 2), (o_pack[0], 1), (o_pack[1], 1), (o_feat[0], 2), (o_feat[1], 2),
                             (o_diag[0], 8), (o_diag[1], 8)):
                    sp.wait_ge(q, TILES // 2 * 16 * n)

            @block.scalar
            def _(act):
                act.wait_ge(s["set_in"], 32)
                act.wait_ge(s["const"], 2)
                act.activation(al, al, ACT.Exp).then_inc(s["expa"], 1)
                act.activation(lg[:], rate, ACT.Exp, scale=-float(np.log(2.0))).then_inc(s["lnready"], 1)
                act.wait_ge(s["lnready"], 1)
                act.activation(lg[:], lg[:], ACT.Ln, scale=-1.0, bias=one[:]).then_inc(s["lgn"], 1)
                act.wait_ge(s["xn"], 1)
                act.activation(xe[:], xn[:], ACT.Exp).then_inc(s["xe"], 1)
                act.wait_ge(s["bm"], 1)
                act.activation(be[:], bm[:], ACT.Exp, scale=-1.0).then_inc(s["be"], 1)
                act.wait_ge(s["xe"], 1)
                act.activation(xl[:], xe[:], ACT.Ln, bias=one[:]).then_inc(s["xl"], 1)
                act.wait_ge(s["expo"], 9)
                act.activation(kd[:], kd[:], ACT.Exp).then_inc(s["decays"], 1)
                act.activation(qd[:], qd[:], ACT.Exp).then_inc(s["decays"], 1)
                def tile(n, u, t):
                    def got(*q):
                        for x in q:
                            act.wait_ge(x, t + 1)

                    def spent(*q):
                        for x in q:
                            act.wait_ge(x, t)

                    got(s["sums"]); spent(s["nt"], s["kt"], s["qg"]); act.wait_ge(s["o_tot"], t * 16)
                    act.activation(es[:], b_s[:, 0:32], ACT.Exp).then_inc(s["es"], 1)
                    got(s["dsum"]); spent(s["de"])
                    act.activation(e1[:].rearrange("p a h n -> p (a h n)"), b_D[:], ACT.Exp).then_inc(s["e1"], 1)
                    got(s["cb"]); spent(s["sq"], s["kh"], s["qh"], s["gv"])
                    act.activation(cv[:], c1[:], ACT.Silu).then_inc(s["cv"], 1)
                    got(s["cv"]); spent(s["ss"])
                    act.activation(sq[:], cv[:, 0:512], ACT.Square).then_inc(s["sq"], 1)
                    act.wait_ge(in_main[u], n * 48 + 48); act.wait_ge(o_pack[u], n * 16)
                    act.activation(pk[u][:, T_RV:T_RV + 256], pr[u][:, R_V:R_V + 256], ACT.Copy).then_inc(s["rv"], 1)
                    got(s["ss"]); spent(s["rn"])
                    act.activation(rt[:], ss[:], ACT.Sqrt, bias=eps[:]).then_inc(s["rt"], 1)
                    got(s["turned_q"]); act.wait_ge(s["o_swq"], t * 16)
                    act.activation(sqT[:].rearrange("p a n -> p (a n)"), b_q[:], ACT.Copy, scale=0.125).then_inc(s["sqT"], 1)
                    got(s["turned_k"]); act.wait_ge(s["o_swk"], t * 16)
                    act.activation(skT[:], b_k[:, 0:P], ACT.Copy).then_inc(s["skT"], 1)
                    got(s["turned_r"]); act.wait_ge(o_feat[u], n * 32)
                    act.activation(ft[u][:, F_RQ:F_RQ + 4, :].rearrange("p a n -> p (a n)"), b_r[:], ACT.Copy).then_inc(s["ftr"], 1)
                    got(s["turned_g"]); spent(s["prod_e"], s["prod_o"])
                    act.activation(khT[:].rearrange("p a n -> p (a n)"), b_g[:, 0:256], ACT.Copy).then_inc(s["khT"], 1)
                    act.activation(qhT[:].rearrange("p a n -> p (a n)"), b_g[:, 256:512], ACT.Copy).then_inc(s["qhT"], 1)
                    got(s["turned_d"])
                    act.activation(ft[u][:, F_D:F_N, :].rearrange("p (d a) n -> p d a n", d=2)[:, :, F_GQD:F_GQD + 2, :],
                                   b_d[:].rearrange("p (d a n) -> p d a n", d=2, a=2), ACT.Copy).then_inc(s["ftd"], 1)

                tiles(act, tile)

            @block.gpsimd
            def _(pool):
                pool.memset(one[:], 1.0).then_inc(s["const"], 1)
                pool.memset(eps[:], EPS).then_inc(s["const"], 1)
                pool.wait_ge(s["set_in"], 32)
                def got(t, *q):
                    for x in q:
                        pool.wait_ge(x, t + 1)

                def spent(t, *q):
                    for x in q:
                        pool.wait_ge(x, t)

                def taps(n, u, t):
                    pool.wait_ge(in_side[u], n * 32 + 32); spent(t, s["ca"])
                    pool.tensor_tensor(c0[:], before[u][:], cw[:, 0, :], ALU.mult).then_inc(s["c0"], 1)
                    spent(t, s["cb"])
                    pool.tensor_tensor(c2[:], after[u][:], cw[:, 2, :], ALU.mult).then_inc(s["c2"], 1)

                def swap(n, u, t):
                    pool.wait_ge(in_main[u], n * 48 + 48); spent(t, s["rotated"])
                    for base, hs, at in ((R_Q, 8, 0), (S_Q, 10, 512)):
                        src = pr[u][:, base:base + hs * 64].rearrange("p (h a u f) -> p h a u f", h=hs, a=2, u=2)
                        dst = swp[:, at:at + hs * 64].rearrange("p (h a u f) -> p h a u f", h=hs, a=2, u=2)
                        for half in range(2):
                            for axis in range(2):
                                sn = rp[u][:, 1, 32 * axis + 16 * half:32 * axis + 16 * half + 16].unsqueeze(1).broadcast_to([P, hs, 16])
                                pool.tensor_tensor(dst[:, :, axis, half, :], src[:, :, axis, 1 - half, :], sn, ALU.mult).then_inc(s["swapped"], 1)

                def tile(n, u, t, last):
                    if not last:
                        swap(n + u, 1 - u, t + 1)
                    pool.wait_ge(s["beta"], 1); spent(t, s["de"])
                    pool.tensor_tensor(mb[:], tri[:].unsqueeze(2).broadcast_to(B4), per_head(of_tile(beta, t)), ALU.mult).then_inc(s["mb"], 1)
                    got(t, s["kh"], s["nt"], s["kt"]); pool.wait_ge(o_pack[u], n * 16)
                    pool.tensor_tensor(packed(u, T_NK), over_dirs(kh[:]), per_head(nt[:]), ALU.mult).then_inc(s["nk"], 1)
                    pool.tensor_tensor(packed(u, T_D + T_KT, 512), over_dirs(kh[:]), per_head(kt[:]), ALU.mult).then_inc(s["ktp"], 1)
                    if not last:
                        taps(n + u, 1 - u, t + 1)

                with pool.Fori(0, 1) as n:
                    taps(n, 0, n)
                    swap(n, 0, n)
                with pool.Fori(0, TILES // 2 - 1) as n:
                    for u in range(2):
                        tile(n, u, n * 2 + u, False)
                with pool.Fori(TILES // 2 - 1, TILES // 2) as n:
                    for u in range(2):
                        tile(n, u, n * 2 + u, u == 1)

            @block.vector
            def _(dve):
                over_tiles = lambda ap8: ap8.unsqueeze(1).broadcast_to([P, TILES, 8])
                dve.wait_ge(s["in_gates"], 32)
                dve.wait_ge(s["set_in"], 32)
                dve.tensor_tensor(xa[:], ab[:, :, 0:8], over_tiles(dtb), ALU.add).then_inc(s["xa"], 1)
                dve.tensor_scalar(bm[:], ab[:, :, 8:16], -80.0, None, ALU.max).then_inc(s["bm"], 1)
                dve.wait_ge(s["xa"], 1)
                dve.scalar_tensor_tensor(xn[:], xa[:], -1.0, xa[:], ALU.mult, ALU.min).then_inc(s["xn"], 1)
                dve.wait_ge(s["expa"], 1)
                dve.tensor_scalar(al, al, -1.0, None, ALU.mult).then_inc(s["alneg"], 1)
                dve.wait_ge(s["lgn"], 1)
                dve.tensor_tensor(kd[:], heads(lg[:], 2), ksteps[:].unsqueeze(2).broadcast_to([P, 2, RH]), ALU.mult).then_inc(s["expo"], 1)
                for h in range(RH):
                    half = slice(64 * (h % 2), 64 * (h % 2) + 64)
                    for d in range(2):
                        dve.tensor_scalar(qd[half, d, h // 2, :], qsteps[half, d, :], lg[half, 4 * d + h:4 * d + h + 1], None,
                                          ALU.mult).then_inc(s["expo"], 1)
                dve.wait_ge(s["be"], 1)
                dve.tensor_scalar(b1[:], be[:], 1.0, None, ALU.add).then_inc(s["b1"], 1)
                dve.wait_ge(s["b1"], 1)
                dve.reciprocal(beta[:], b1[:]).then_inc(s["beta"], 1)
                dve.wait_ge(s["xl"], 1)
                dve.scalar_tensor_tensor(xl[:], xa[:], 0.0, xl[:], ALU.max, ALU.add).then_inc(s["sp"], 1)
                dve.wait_ge(s["sp"], 1)
                dve.wait_ge(s["alneg"], 1)
                dve.tensor_tensor(g[:], xl[:], over_tiles(al), ALU.mult).then_inc(s["g"], 1)
                dve.wait_ge(s["g"], 1)
                dve.wait_ge(s["beta"], 1)
                dve.wait_ge(s["decays"], 2)
                def tile(n, u, t):
                    def got(*q):
                        for x in q:
                            dve.wait_ge(x, t + 1)

                    def spent(*q):
                        for x in q:
                            dve.wait_ge(x, t)

                    dve.wait_ge(in_main[u], n * 48 + 48)
                    spent(s["dsum"])
                    dve.tensor_tensor(gu[:], tri[:].unsqueeze(2).broadcast_to(B4), per_head(of_tile(g, t)), ALU.mult).then_inc(s["gu"], 1)
                    dve.wait_ge(s["turned_r"], t); dve.wait_ge(s["turned_q"], t); dve.wait_ge(s["turned_k"], t)
                    spent(s["rk"])
                    cos = lambda n: rp[u][:, 0, :].unsqueeze(1).broadcast_to([P, n, 64])
                    dve.tensor_tensor(heads(hot[:, 0:512], 8), heads(pr[u][:, R_Q:R_Q + 512], 8), cos(8), ALU.mult)
                    dve.tensor_tensor(heads(hot[:, 512:1152], 10), heads(pr[u][:, S_Q:S_Q + 640], 10), cos(10), ALU.mult).then_inc(s["rot"], 1)
                    got(s["rot"]); dve.wait_ge(s["swapped"], t * 8 + 8)
                    dve.tensor_tensor(hot[:, 0:512], hot[:, 0:512], swp[:, 0:512], ALU.add)
                    dve.tensor_tensor(hot[:, 1024:1152], hot[:, 1024:1152], swp[:, 1024:1152], ALU.add)
                    side = lambda ap: ap[:, 512:1024].rearrange("p (u c n) -> p u c n", u=2, c=4)
                    dve.tensor_tensor(hp[:].rearrange("p (c u n) -> p u c n", c=4, u=2), side(hot), side(swp), ALU.add).then_inc(s["rotated"], 1)
                    spent(s["cv"])
                    dve.tensor_tensor(c1[:], pr[u][:, G_Q:G_Q + 768], cw[:, 1, :], ALU.mult).then_inc(s["c1"], 1)
                    got(s["c1"], s["c0"])
                    dve.tensor_tensor(c1[:], c1[:], c0[:], ALU.add).then_inc(s["ca"], 1)
                    got(s["ca"], s["c2"])
                    dve.tensor_tensor(c1[:], c1[:], c2[:], ALU.add).then_inc(s["cb"], 1)
                    got(s["rotated"]); dve.wait_ge(o_pack[u], n * 16); dve.wait_ge(o_diag[u], n * 128)
                    dve.tensor_tensor(packed(u, T_RK, 512), over_dirs(hot[:, 256:512]), kd[:].unsqueeze(3).broadcast_to(B4), ALU.mult).then_inc(s["rk"], 1)
                    got(s["sq"]); spent(s["rt"])
                    dve.tensor_reduce(ss[:], heads(sq[:], 8), AX.X, ALU.add).then_inc(s["ss"], 1)
                    got(s["rt"]); spent(s["kh"], s["qh"])
                    dve.reciprocal(rn[:], rt[:]).then_inc(s["rn"], 1)
                    got(s["rn"]); spent(s["turned_g"], s["nk"], s["ktp"])
                    dve.tensor_tensor(heads(kh[:], 4), heads(cv[:, 256:512], 4), rn[:, 4:8].unsqueeze(2).broadcast_to([P, 4, 64]), ALU.mult).then_inc(s["kh"], 1)
                    spent(s["qg"])
                    dve.scalar_tensor_tensor(heads(qh[:], 4), heads(cv[:, 0:256], 4), 0.125, rn[:, 0:4].unsqueeze(2).broadcast_to([P, 4, 64]),
                                             ALU.mult, ALU.mult).then_inc(s["qh"], 1)
                    dve.tensor_copy(pk[u][:, T_GV:T_GV + 256], cv[:, 512:768]).then_inc(s["gv"], 1)
                    got(s["es"]); spent(s["nk"])
                    dve.tensor_scalar(nt[:], es[:, 0:8], -1.0, None, ALU.mult).then_inc(s["nt"], 1)
                    spent(s["ktp"])
                    dve.tensor_tensor(kt[:], es[:, 8:16], of_tile(beta, t), ALU.mult).then_inc(s["kt"], 1)
                    got(s["qh"]); spent(s["turned_d"])
                    dve.tensor_tensor(qg[:], over_dirs(qh[:]), per_head(es[:, 0:8]), ALU.mult).then_inc(s["qg"], 1)
                    dve.wait_ge(s["ftr"], t + 1); dve.wait_ge(o_feat[u], n * 32)
                    for d, col, q in ((0, F_D + F_RQD, s["ftf"]), (1, F_D + F_DN + F_RQD, s["ftb"])):
                        dve.tensor_tensor(ft[u][:, col:col + 2, :], b_r[:, 0:256].rearrange("p (a n) -> p a n", a=2), qd[:, d, :, :], ALU.mult).then_inc(q, 1)
                    got(s["e1"], s["mb"]); spent(s["lt"], s["at"])
                    dve.tensor_tensor(de[:], e1[:], mb[:], ALU.mult).then_inc(s["de"], 1)
                    got(s["de"], s["prod_e"], s["prod_o"])
                    for col, step, q, o in ((T_LT, 256, s["lt"], 0), (T_D + T_AT, 512, s["at"], 128)):
                        for d in range(2):
                            for odd, bank in ((0, b_h), (1, b_k)):
                                src = bank[:, 256 * odd + o:256 * odd + o + 128].rearrange("p (h n) -> p h n", h=2)
                                last = dve.tensor_tensor(packed(u, col, step)[:, d, odd::2, :], src, de[:, d, odd::2, :], ALU.mult)
                        last.then_inc(q, 1)

                tiles(dve, tile)

            @block.tensor
            def _(pe):
                def tile(n, u, t):
                    def got(*q):
                        for x in q:
                            pe.wait_ge(x, t + 1)

                    def spent(*q):
                        for x in q:
                            pe.wait_ge(x, t)

                    pe.wait_ge(s["g"], 1); spent(s["es"])
                    for m, c0_, c1_, gcol in ((C_LE, 0, 4, 0), (C_GE, 4, 8, 4), (C_GT, 8, 12, 0), (C_LT, 12, 16, 4),
                                              (C_C0, 16, 24, 0), (C_C1, 24, 32, 0)):
                        mm = pe.matmul(b_s[:, c0_:c1_], mat(m), of_tile(g, t)[:, gcol:gcol + c1_ - c0_], start=True, stop=True)
                    mm.then_inc(s["sums"], 1)
                    got(s["gu"]); spent(s["e1"])
                    pe.matmul(b_D[:, 0:256], mat(C_GT), gu[:, 0, :, :].rearrange("p h n -> p (h n)"), start=True, stop=True)
                    mm = pe.matmul(b_D[:, 256:512], mat(C_LT), gu[:, 1, :, :].rearrange("p h n -> p (h n)"), start=True, stop=True)
                    mm.then_inc(s["dsum"], 1)
                    got(s["rotated"]); spent(s["ftf"], s["ftb"]); pe.wait_ge(s["ftr"], t)
                    for c in range(4):
                        mm = pe.transpose(b_r[:, c * P:(c + 1) * P], hot[:, c * P:(c + 1) * P], mat(C_ID))
                    mm.then_inc(s["turned_r"], 1)
                    spent(s["sqT"])
                    for c in range(4):
                        mm = pe.transpose(b_q[:, c * P:(c + 1) * P], hp[:, c * P:(c + 1) * P], mat(C_ID))
                    mm.then_inc(s["turned_q"], 1)
                    spent(s["lt"], s["at"])
                    pe.transpose(b_k[:, 0:P], hot[:, 1024:1152], mat(C_ID)).then_inc(s["turned_k"], 1)
                    got(s["kh"], s["qh"]); spent(s["khT"], s["qhT"])
                    for c in range(4):
                        src = (kh, qh)[c // 2]
                        mm = pe.transpose(b_g[:, c * P:(c + 1) * P], src[:, (c % 2) * P:(c % 2 + 1) * P], mat(C_ID))
                    mm.then_inc(s["turned_g"], 1)
                    got(s["qg"]); spent(s["ftd"])
                    for c in range(4):
                        mm = pe.transpose(b_d[:, c * P:(c + 1) * P], qg[:, c // 2, 2 * (c % 2):2 * (c % 2) + 2, :], mat(C_ID))
                    mm.then_inc(s["turned_d"], 1)
                    got(s["khT"], s["qhT"], s["skT"])
                    settle(pe, s["pe_passed"])
                    for odd, bank, q in ((0, b_h, s["prod_e"]), (1, b_k, s["prod_o"])):
                        for pair in range(2):
                            for c in range(2):
                                d, j = slice(64 * odd, 64 * odd + 64), slice(64 * c, 64 * c + 64)
                                for o, rhs in ((0, khT), (128, qhT)):
                                    at = 256 * odd + o + 64 * pair
                                    mm = pe.matmul(bank[j, at:at + 64], khT[d, pair, j], rhs[d, pair, j], start=True, stop=True)
                        mm.then_inc(q, 1)

                tiles(pe, tile)


def solve(nc, layer, diag, inv, beside):
    NB = 2 * TILES * GH
    with Stage(nc, f"slv{layer}") as st:
        n_in = [st.sb(f"n{d}", [NB, 2, 32, 32]) for d in range(2)]
        neg = [st.sb(f"neg{d}", [NB, 2, 32, 32]) for d in range(2)]
        xt = [st.sb(f"xt{d}", [NB, 2, 32, 32]) for d in range(2)]
        xx = [st.sb(f"xx{d}", [NB, 2, 32, 32]) for d in range(2)]
        prod = [st.sb(f"prod{d}", [NB, 2, 32, 32]) for d in range(2)]
        landed = [st.sem(f"landed{d}") for d in range(2)]
        zeroed, unit, negated, turned = [[st.sem(f"{n}{d}") for d in range(2)] for n in ("zeroed", "unit", "negated", "turned")]
        multiplied, summed = [[st.sem(f"{n}{d}") for d in range(2)] for n in ("multiplied", "summed")]
        stored = st.sem("stored")
        half = 2 * TILES
        sync, scalar, tensor, gpsimd = beside(st)
        with nc.Block() as block:
            block.tensor(tensor)

            @block.sync
            def _(sp):
                for d in range(2):
                    for slot in range(2):
                        sp.dma_start(n_in[d][:, slot].rearrange("p j i -> p (j i)"),
                                     diag[d, slot * half:(slot + 1) * half].rearrange("a h j i -> (a h) (j i)")).then_inc(landed[d], 16)
                sync(sp)

            @block.scalar
            def _(act):
                for d in range(2):
                    act.wait_ge(landed[d], 32)
                    act.activation(neg[d][:], n_in[d][:], ACT.Copy, scale=-1.0).then_inc(negated[d], 1)
                scalar(act)

            def start(pool):
                for d in range(2):
                    pool.memset(xt[d][:], 0.0).then_inc(zeroed[d], 1)
                    pool.wait_ge(zeroed[d], 1)
                    flat = xt[d][:].rearrange("p s c j -> p s (c j)")
                    pool.memset(flat[:, :, 0:1024:33], 1.0).then_inc(unit[d], 1)

            def substitute(eng, d):
                eng.wait_ge(unit[d], 1)
                eng.wait_ge(negated[d], 1)
                for step in range(31):
                    r = step if d == 0 else 31 - step
                    after, cols = (slice(r + 1, 32), slice(0, r + 1)) if d == 0 else (slice(0, r), slice(r, 32))
                    n_c, n_a = step + 1, 31 - step
                    if step:
                        eng.wait_ge(summed[d], step)
                    row = xt[d][:, :, cols, r].unsqueeze(3).broadcast_to([NB, 2, n_c, n_a])
                    n_col = neg[d][:, :, r, after].unsqueeze(2).broadcast_to([NB, 2, n_c, n_a])
                    share = prod[d][:, :, 0:n_c, 0:n_a]
                    eng.tensor_tensor(share, row, n_col, ALU.mult).then_inc(multiplied[d], 1)
                    eng.wait_ge(multiplied[d], step + 1)
                    eng.tensor_tensor(xt[d][:, :, cols, after], xt[d][:, :, cols, after], share, ALU.add).then_inc(summed[d], 1)

            @block.vector
            def _(dve):
                substitute(dve, 0)
                for d in range(2):
                    dve.wait_ge(summed[d], 31)
                    dve.tensor_copy(xx[d][:], xt[d][:].rearrange("p s c j -> p s j c")).then_inc(turned[d], 1)

            @block.gpsimd
            def _(pool):
                start(pool)
                substitute(pool, 1)
                for d in range(2):
                    for which, buf, ready, n in ((0, xt, summed, 31), (1, xx, turned, 1)):
                        pool.wait_ge(ready[d], n)
                        for slot in range(2):
                            pool.dma_start(inv[slot * half:(slot + 1) * half, :, 2 * which + d].rearrange("a h j i -> (a h) (j i)"),
                                           buf[d][:, slot].rearrange("p j i -> p (j i)")).then_inc(stored, 16)
                pool.wait_ge(stored, 8 * 16)
                gpsimd(pool)


def join(nc, layer, pack, inv, feat, us):
    with Stage(nc, f"jn{layer}") as st:
        off = [st.sb(f"off{u}", [P, 8, P]) for u in range(2)]
        both = [st.sb(f"both{u}", [P, 16, P]) for u in range(2)]
        vn = [st.sb(f"vn{u}", [P, 768]) for u in range(2)]
        y = [st.sb(f"y{d}", [P, 4, P]) for d in range(2)]
        xt = [st.sb(f"xt{d}", [P, 4, P]) for d in range(2)]
        u_o = [st.sb(f"u{d}", [P, 2, 2, HD]) for d in range(2)]
        w_o = [st.sb(f"w{d}", [P, 2, P]) for d in range(2)]
        b_y, b_g, b_u, b_w = [[st.ps(f"b_{n}{d}", [P, 512]) for d in range(2)] for n in "yguw"]
        zeroed = st.sem("zeroed")
        landed = [st.sem(f"landed{u}") for u in range(2)]
        y_sum, y_out, g_sum, x_done, u_sum, w_sum, u_out, w_out, stored = [[st.sem(f"{n}{d}") for d in range(2)] for n in (
            "y_sum", "y_out", "g_sum", "x_done", "u_sum", "w_sum", "u_out", "w_out", "stored")]
        sp_passed, pool_passed = st.sem("sp_passed"), st.sem("pool_passed")
        with nc.Block() as block:
            @block.sync
            def _(sp):
                sp.wait_ge(zeroed, 4)

                def load(u, t):
                    for b in range(4):
                        rows = slice(32 * b, 32 * b + 32)
                        sp.dma_start(both[u][rows, :, rows], inv[bass.ds(t * 4 + b, 1)].rearrange("a h w c j -> (a c) (h w) j")).then_inc(landed[u], 16)
                        d, ib = (0, b + 1) if b % 2 == 0 else (1, b - 1)
                        src = pack[bass.ds(t, 1)].rearrange("a p n -> (a p) n")[rows, T_LT + 256 * d:T_LT + 256 * d + 256]
                        src = src.rearrange("p (h i) -> p h i", h=4)[:, :, 32 * (ib % 2):32 * (ib % 2) + 32]
                        sp.dma_start(off[u][rows, 4 * d:4 * d + 4, 32 * ib:32 * ib + 32], src).then_inc(landed[u], 16)
                    src = pack[bass.ds(t, 1)].rearrange("a p n -> (a p) n")
                    sp.dma_start(vn[u][:, 0:512], src[:, T_NK:T_NK + 512]).then_inc(landed[u], 16)
                    sp.dma_start(vn[u][:, 512:768], src[:, T_GV:T_GV + 256]).then_inc(landed[u], 16)

                for u in range(2):
                    load(u, u)
                with sp.Fori(0, TILES // 2 - 1) as n:
                    for u in range(2):
                        for q in (u_sum, w_sum):
                            for d in range(2):
                                sp.wait_ge(q[d], n * 2 + u + 1)
                                settle(sp, sp_passed)
                        load(u, n * 2 + u + 2)

            NL = 16 * (4 + 4 + 2)

            @block.tensor
            def _(pe):
                with pe.Fori(0, TILES // 2) as n:
                    for u in range(2):
                        t = n * 2 + u
                        pe.wait_ge(landed[u], n * NL + NL)
                        for d in range(2):
                            pe.wait_ge(y_out[d], t)
                            for h in range(4):
                                mm = pe.matmul(b_y[d][:, h * P:(h + 1) * P], off[u][:, 4 * d + h, :], both[u][:, 4 * h + 2 + d, :], start=True, stop=True)
                            mm.then_inc(y_sum[d], 1)
                        for d in range(2):
                            pe.wait_ge(y_out[d], t + 1)
                            pe.wait_ge(x_done[d], t)
                            for h in range(4):
                                mm = pe.matmul(b_g[d][:, h * P:(h + 1) * P], y[d][:, h, :], both[u][:, 4 * h + d, :], start=True, stop=True)
                            mm.then_inc(g_sum[d], 1)
                        for d in range(2):
                            pe.wait_ge(x_done[d], t + 1)
                            pe.wait_ge(w_out[d], t)
                            for h in range(4):
                                e = slice(64 * (h % 2), 64 * (h % 2) + 64)
                                k = 256 * d + 64 * h
                                mm = pe.matmul(b_w[d][e, (h // 2) * P:(h // 2 + 1) * P], vn[u][:, k:k + 64], xt[d][:, h, :], start=True, stop=True)
                            mm.then_inc(w_sum[d], 1)
                            pe.wait_ge(u_out[d], t * 2)
                            for h in range(4):
                                pair = slice(512 + 128 * (h // 2), 512 + 128 * (h // 2) + 128)
                                mm = pe.matmul(b_u[d][:, h * P:(h + 1) * P], xt[d][:, h, :], vn[u][:, pair], start=True, stop=True)
                            mm.then_inc(u_sum[d], 1)

            @block.scalar
            def _(act):
                with act.Fori(0, TILES // 2) as n:
                    for u in range(2):
                        t = n * 2 + u
                        for d in range(2):
                            act.wait_ge(y_sum[d], t + 1)
                            act.wait_ge(g_sum[d], t)
                            act.activation(y[d][:].rearrange("p h n -> p (h n)"), b_y[d][:], ACT.Copy).then_inc(y_out[d], 1)
                        for d in range(2):
                            act.wait_ge(w_sum[d], t + 1)
                            act.wait_ge(stored[d], t * 32)
                            act.activation(w_o[d][:].rearrange("p a n -> p (a n)"), b_w[d][:, 0:256], ACT.Copy).then_inc(w_out[d], 1)

            @block.vector
            def _(dve):
                for buf in (off, both):
                    dve.memset(buf[1][:], 0.0).then_inc(zeroed, 1)
                with dve.Fori(0, TILES // 2) as n:
                    for u in range(2):
                        t = n * 2 + u
                        for d in range(2):
                            dve.wait_ge(g_sum[d], t + 1)
                            dve.wait_ge(u_sum[d], t)
                            dve.tensor_tensor(xt[d][:], both[u][:, d::4, :], b_g[d][:].rearrange("p (h n) -> p h n", h=4), ALU.subtract).then_inc(x_done[d], 1)
                        for d in range(2):
                            dve.wait_ge(u_sum[d], t + 1)
                            dve.wait_ge(stored[d], t * 32)
                            for p in range(2):
                                src = b_u[d][:].rearrange("p (a n) -> p a n", a=2)[:, :, 192 * p:192 * p + 64]
                                dve.tensor_copy(u_o[d][:, :, p, :], src).then_inc(u_out[d], 1)

            @block.gpsimd
            def _(pool):
                for buf in (off, both):
                    pool.memset(buf[0][:], 0.0).then_inc(zeroed, 1)
                with pool.Fori(0, TILES) as t:
                    for d in range(2):
                        pool.wait_ge(w_out[d], t + 1)
                        settle(pool, pool_passed)
                        slot = F_D + F_DN * d + F_GW
                        pool.dma_start(feat[bass.ds(t, 1)].rearrange("a p f n -> (a p) f n")[:, slot:slot + 2], w_o[d][:]).then_inc(stored[d], 16)
                        pool.wait_ge(u_out[d], t * 2 + 2)
                        settle(pool, pool_passed)
                        pool.dma_start(us[bass.ds(t, 1)].rearrange("a p n -> (a p) n")[:, 256 * d:256 * d + 256],
                                       u_o[d][:].rearrange("p a q e -> p (a q e)")).then_inc(stored[d], 16)
                for d in range(2):
                    pool.wait_ge(stored[d], TILES * 32)


def scan(nc, layer, pack, feat, tot, us, small, mats, o_ret, o_gdn):
    with Stage(nc, f"scn{layer}") as st:
        dual = lambda n, shape: [st.sb(f"{n}{u}", shape) for u in range(2)]
        gt = st.sb("gt", [P, TILES, 2, 2, 2, 2])
        gth = st.sb("gth", [P, TILES, 2, 2, 2])
        fd = dual("fd", [P, 2, F_DN, P])
        u_i = [dual(f"u_i{c}", [P, 256]) for c in range(2)]
        kaz = [dual(f"kaz{c}", [P, 2, 512]) for c in range(2)]
        rqz = dual("rqz", [P, 2, 2, P])
        rk, rkv = dual("rk", [P, 2, P]), dual("rkv", [P, 2, 512])
        S, Sg = st.sb("S", [P, 2, 2, P]), st.sb("Sg", [P, 2, 2, P])
        R, Rg = st.sb("R", [P, 2, 2, P]), st.sb("Rg", [P, 2, 2, P])
        z = st.sb("z", [P, 256])
        mask, scores = st.sb("mask", [P, 4, P]), st.sb("scores", [P, 4, P])
        sm, lg, cd, cdh = st.sb("sm", [P, 3, 8]), st.sb("lg", [P, 8]), st.sb("cd", [P, 2, 2, 2]), st.sb("cdh", [P, 2, 2])
        far, keep, eg, kept = (st.sb(n, [P, 2, P]) for n in ("far", "keep", "eg", "kept"))
        one = st.sb("one", [P, 1])
        b_z, b_o, b_S, b_k, b_r, b_R = [st.ps(f"b_{n}", [P, 512]) for n in ("z", "o", "S", "k", "r", "R")]
        s = signals(st, """set_in const zeroed rate_e lgs cds cdhs gths fars keeps egs masked1 mask_done
            in0 in1 z_sum z_done dS_sum Sg_done S_done o_sum o_out k_sum scored r_sum r_out dR_sum Rg_done R_done
            sp_passed dve_passed pool_passed act_passed""")
        in_s = (s["in0"], s["in1"])
        NL = 16 * 15
        half = lambda a: slice(64 * a, 64 * a + 64)
        dist = mats[:, C_DIST, :]

        def tile_pairs(eng, body):
            with eng.Fori(0, 1) as n:
                for u in range(2):
                    body(n, u, n * 2 + u, n * 0 + (1 - u))
            with eng.Fori(1, TILES // 2) as n:
                for u in range(2):
                    body(n, u, n * 2 + u, n * -2 + (TILES + 1 - u))

        with nc.Block() as block:
            @block.sync
            def _(sp):
                sp.dma_start(gt[:].rearrange("p t c d a q -> p t (c d a q)"), tot.rearrange("t p n -> p t n")).then_inc(s["set_in"], 16)
                sp.dma_start(sm[:], small[layer]).then_inc(s["set_in"], 16)
                sp.wait_ge(s["zeroed"], 8)

                def tile(ap, t):
                    return ap[bass.ds(t, 1)].rearrange("a p n -> (a p) n")

                def load(u, tf, tb):
                    q = in_s[u]
                    for d, t in ((0, tf), (1, tb)):
                        for c in range(2):
                            r = half(c if d == 0 else 1 - c)
                            sp.dma_start(u_i[c][u][r, :], tile(us, t)[r, 256 * d:256 * d + 256]).then_inc(q, 16)
                            sp.dma_start(kaz[c][u][r, d, :], tile(pack, t)[r, T_D + 512 * d:T_D + 512 * d + 512]).then_inc(q, 16)
                        ft = feat[bass.ds(t, 1)].rearrange("a p f n -> (a p) f n")
                        sp.dma_start(fd[u][:, d], ft[:, F_D + F_DN * d:F_D + F_DN * d + F_DN, :]).then_inc(q, 16)
                        sp.dma_start(rkv[u][:, d, :], tile(pack, t)[:, T_RK + 256 * d:T_RK + 256 * d + 512]).then_inc(q, 16)
                    ft = feat[bass.ds(tf, 1)].rearrange("a p f n -> (a p) f n")
                    for p in range(2):
                        sp.dma_start(rqz[u][half(p), :, p, :], ft[half(p), F_RQ:F_RQ + 2, :]).then_inc(q, 16)
                    sp.dma_start(rk[u][:], ft[:, F_RK:F_RK + 2, :]).then_inc(q, 16)

                def again(t):
                    for q, k in ((s["o_sum"], 2), (s["r_sum"], 1), (s["dR_sum"], 1), (s["dS_sum"], 2), (s["z_done"], 2)):
                        sp.wait_ge(q, (t - 1) * k)
                        settle(sp, s["sp_passed"])

                with sp.Fori(0, 1) as n:
                    for u in range(2):
                        load(u, n + u, n + (1 - u))
                with sp.Fori(1, TILES // 2) as n:
                    for u in range(2):
                        again(n * 2 + u)
                        load(u, n * 2 + u, n * -2 + (TILES + 1 - u))

            @block.gpsimd
            def _(pool):
                for buf in (kaz[0], kaz[1], rqz):
                    pool.memset(buf[0][:], 0.0).then_inc(s["zeroed"], 1)
                pool.memset(R[:], 0.0).then_inc(s["zeroed"], 1)
                pool.memset(one[:], 1.0).then_inc(s["const"], 1)
                pool.wait_ge(s["gths"], 2); pool.wait_ge(s["cdhs"], 2); pool.wait_ge(s["zeroed"], 8)

                def body(n, u, t, tb):
                    for c in range(2):
                        pool.wait_ge(s["S_done"], t * 4 + 2 * c)
                        for d, tt, cc in ((0, t, c), (1, tb, 1 - c)):
                            g = gth[:, bass.ds(tt, 1), cc, d, :].rearrange("p a n -> p (a n)").unsqueeze(2).broadcast_to([P, 2, P])
                            pool.tensor_tensor(Sg[:, d], S[:, d], g, ALU.mult).then_inc(s["Sg_done"], 1)
                        if c == 0:
                            pool.wait_ge(s["R_done"], t * 2)
                            pool.tensor_tensor(Rg[:], R[:], cdh[:].unsqueeze(3).broadcast_to([P, 2, 2, P]), ALU.mult).then_inc(s["Rg_done"], 1)

                tile_pairs(pool, body)

            @block.scalar
            def _(act):
                act.wait_ge(s["set_in"], 32)
                act.wait_ge(s["const"], 1)
                act.activation(lg[:], sm[:, 2, :], ACT.Exp, scale=-float(np.log(2.0))).then_inc(s["rate_e"], 1)
                act.wait_ge(s["rate_e"], 1)
                act.activation(lg[:], lg[:], ACT.Ln, scale=-1.0, bias=one[:]).then_inc(s["lgs"], 1)
                act.wait_ge(s["lgs"], 1)
                act.activation(cd[:].rearrange("p d a q -> p (d a q)"), lg[:], ACT.Exp, scale=float(P)).then_inc(s["cds"], 1)
                act.wait_ge(s["fars"], 2)
                for h in range(4):
                    if h:
                        act.wait_ge(s["masked1"], h)
                    for d in range(2):
                        act.activation(eg[:, d, :], far[:, d, :], ACT.Exp, scale=lg[:, 4 * d + h:4 * d + h + 1]).then_inc(s["egs"], 1)

                def body(n, u, t, tb):
                    for c in range(2):
                        act.wait_ge(s["o_sum"], t * 2 + c + 1)
                        for d, tt, cc in ((0, t, c), (1, tb, 1 - c)):
                            act.activation(o_gdn[:, d, :, bass.ds(tt * P + 64 * cc, 64)],
                                           b_o[:, 0:256].rearrange("p (a n) -> p a n", a=2)[:, :, half(d)], ACT.Copy).then_inc(s["o_out"], 1)
                        if c == 0:
                            act.wait_ge(s["r_sum"], t + 1)
                            for d, tt in ((0, t), (1, tb)):
                                act.activation(o_ret[:, d, :, bass.ds(tt * P, P)],
                                               b_r[:, 256 * d:256 * d + 256].rearrange("p (a n) -> p a n", a=2), ACT.Copy,
                                               scale=0.125).then_inc(s["r_out"], 1)

                tile_pairs(act, body)

            @block.vector
            def _(dve):
                for buf in (kaz[0], kaz[1], rqz):
                    dve.memset(buf[1][:], 0.0).then_inc(s["zeroed"], 1)
                dve.memset(S[:], 0.0).then_inc(s["zeroed"], 1)
                dve.wait_ge(s["set_in"], 32)
                for p in range(2):
                    dve.tensor_copy(gth[half(p)], gt[half(p), :, :, :, :, p]).then_inc(s["gths"], 1)
                dve.wait_ge(s["cds"], 1)
                for p in range(2):
                    dve.tensor_copy(cdh[half(p)], cd[half(p), :, :, p]).then_inc(s["cdhs"], 1)
                dve.tensor_scalar(far[:, 0, :], dist, 0.0, None, ALU.max).then_inc(s["fars"], 1)
                dve.tensor_scalar(far[:, 1, :], dist, -1.0, 0.0, ALU.mult, ALU.max).then_inc(s["fars"], 1)
                dve.tensor_scalar(keep[:, 0, :], dist, 0.0, None, ALU.is_ge).then_inc(s["keeps"], 1)
                dve.tensor_scalar(keep[:, 1, :], dist, 0.0, None, ALU.is_le).then_inc(s["keeps"], 1)
                dve.wait_ge(s["keeps"], 2)
                for h in range(4):
                    dve.wait_ge(s["egs"], 2 * h + 2)
                    if h:
                        dve.wait_ge(s["mask_done"], h)
                    dve.tensor_tensor(kept[:], eg[:], keep[:], ALU.mult).then_inc(s["masked1"], 1)
                    dve.wait_ge(s["masked1"], h + 1)
                    dve.tensor_tensor(mask[:, h, :], kept[:, 0, :], kept[:, 1, :], ALU.add).then_inc(s["mask_done"], 1)
                dve.wait_ge(s["mask_done"], 4)
                dve.wait_ge(s["zeroed"], 8)

                def body(n, u, t, tb):
                    for c in range(2):
                        dve.wait_ge(s["z_sum"], t * 2 + c + 1)
                        dve.wait_ge(in_s[u], n * NL + NL)
                        dve.wait_ge(s["o_sum"], t * 2 + c)
                        dve.tensor_tensor(z[:], b_z[:, 0:256], u_i[c][u][:], ALU.add).then_inc(s["z_done"], 1)
                        if c == 0:
                            dve.wait_ge(s["k_sum"], t + 1)
                            dve.wait_ge(s["r_sum"], t)
                            dve.tensor_tensor(scores[:], b_k[:].rearrange("p (h n) -> p h n", h=4), mask[:], ALU.mult).then_inc(s["scored"], 1)
                        dve.wait_ge(s["dS_sum"], t * 2 + c + 1)
                        dve.wait_ge(s["Sg_done"], t * 4 + 2 * c + 2)
                        for p in range(2):
                            at = lambda b: b[:].rearrange("p (d a n) -> p d a n", d=2, a=2)[half(p), :, :, half(p)]
                            dve.tensor_tensor(S[half(p), :, :, half(p)], Sg[half(p), :, :, half(p)], at(b_S), ALU.add).then_inc(s["S_done"], 1)
                        if c == 1:
                            dve.wait_ge(s["dR_sum"], t + 1)
                            dve.wait_ge(s["Rg_done"], t + 1)
                            for p in range(2):
                                at = lambda b: b[:].rearrange("p (d a n) -> p d a n", d=2, a=2)[half(p), :, :, half(p)]
                                dve.tensor_tensor(R[half(p), :, :, half(p)], Rg[half(p), :, :, half(p)], at(b_R), ALU.add).then_inc(s["R_done"], 1)

                tile_pairs(dve, body)

            @block.tensor
            def _(pe):
                pe.wait_ge(s["zeroed"], 8)

                def body(n, u, t, tb):
                    pe.wait_ge(in_s[u], n * NL + NL)
                    for c in range(2):
                        cc = (c, 1 - c)
                        pe.wait_ge(s["S_done"], t * 4 + 2 * c)
                        pe.wait_ge(s["z_done"], t * 2 + c)
                        for d in range(2):
                            for a in range(2):
                                mm = pe.matmul(b_z[half(cc[d]), a * P:(a + 1) * P], fd[u][:, d, F_GW + a, half(cc[d])], S[:, d, a, :], start=True, stop=True)
                        mm.then_inc(s["z_sum"], 1)
                        pe.wait_ge(s["o_out"], t * 4 + 2 * c)
                        for d in range(2):
                            for a in range(2):
                                for p in range(2):
                                    pe.matmul(b_o[half(p), a * P + 64 * d:a * P + 64 * d + 64], S[:, d, a, half(p)],
                                              fd[u][:, d, F_GQD + a, half(cc[d])], start=(d == 0 and a == 0), stop=False)
                        if c == 0:
                            pe.wait_ge(s["scored"], t)
                            for a in range(2):
                                mm = pe.matmul(b_k[:, 256 * a:256 * a + 256], rk[u][:, a, :], rqz[u][:, a].rearrange("p q n -> p (q n)"), start=True, stop=True)
                            mm.then_inc(s["k_sum"], 1)
                        else:
                            pe.wait_ge(s["R_done"], t * 2)
                            for d in range(2):
                                for a in range(2):
                                    at = 256 * d + 128 * a
                                    mm = pe.matmul(b_R[:, at:at + P], rkv[u][:, d, 256 * d + a * P:256 * d + (a + 1) * P],
                                                   rkv[u][:, d, 256 * (1 - d) + a * P:256 * (1 - d) + (a + 1) * P], start=True, stop=True)
                            mm.then_inc(s["dR_sum"], 1)
                        pe.wait_ge(s["z_done"], t * 2 + c + 1)
                        for d in range(2):
                            for a in range(2):
                                at = 256 * d + 128 * a
                                mm = pe.matmul(b_S[:, at:at + P], kaz[c][u][:, d, T_KT + a * P:T_KT + (a + 1) * P], z[:, a * P:(a + 1) * P], start=True, stop=True)
                        mm.then_inc(s["dS_sum"], 1)
                        for a in range(2):
                            for p in range(2):
                                h = 2 * a + p
                                mm = pe.matmul(b_o[half(p), a * P:(a + 1) * P], z[:, h * 64:h * 64 + 64],
                                               kaz[c][u][:, :, T_AT + h * 64:T_AT + h * 64 + 64], start=False, stop=(a == 1))
                        mm.then_inc(s["o_sum"], 1)
                        if c == 0:
                            pe.wait_ge(s["r_out"], t * 2)
                            pe.wait_ge(s["R_done"], t * 2)
                            for d in range(2):
                                for a in range(2):
                                    at = 256 * d + 128 * a
                                    pe.matmul(b_r[:, at:at + P], R[:, d, a, :], fd[u][:, d, F_RQD + a, :], start=(d == 0 and a == 0), stop=False)
                            pe.wait_ge(s["scored"], t + 1)
                            for a in range(2):
                                for p in range(2):
                                    h = 2 * a + p
                                    mm = pe.matmul(b_r[half(p), a * P:(a + 1) * P], rkv[u][:, 0, 256 + h * 64:256 + h * 64 + 64], scores[:, h, :], start=False, stop=(a == 1))
                            mm.then_inc(s["r_sum"], 1)

                tile_pairs(pe, body)


def window(nc, layer, t0, proj, swq, swk, win, sinks, mats, y_hi, y_lo):
    NT = TILES - t0
    K = 3 * P + CTX
    with Stage(nc, f"win{layer}") as st:
        keys = st.sb("keys", [P, TOK + 2 * P])
        vc = st.sb("vc", [P, 2, P])
        sink = st.sb("sink", [P, SH])
        qz = [st.sb(f"qz{u}", [P, 2, 4, P]) for u in range(2)]
        mask = [st.sb(f"mask{u}", [P, 3 * P]) for u in range(2)]
        vw = [st.sb(f"vw{u}", [P, 3, P]) for u in range(2)]
        prob = [st.sb(f"prob{i}", [P, K]) for i in range(2)]
        probT = [st.sb(f"probT{i}", [P, 5, P]) for i in range(2)]
        mx = [st.sb(f"mx{i}", [P, 2]) for i in range(2)]
        low = [st.sb(f"low{i}", [P, 1]) for i in range(2)]
        nmax = [st.sb(f"nmax{i}", [P, 1]) for i in range(2)]
        part = [st.sb(f"part{i}", [P, 3]) for i in range(2)]
        den, rden = [st.sb(f"den{i}", [P, 1]) for i in range(2)], [st.sb(f"rden{i}", [P, 1]) for i in range(2)]
        yt = st.sb("yt", [P, SH * HD])
        b_l, b_c, b_o = [[st.ps(f"b_{n}{i}", [P, 512]) for i in range(2)] for n in "lco"]
        b_t0, b_t1 = st.ps("b_t0", [P, 512]), st.ps("b_t1", [P, 512])
        s = signals(st, "set_in zeroed t0_out t1_out y_turned y_rounded y_split pe_passed dve_passed sp_passed")
        landed, s_sum, masked, cmax, lowered, m_done, e_loc, e_ctx, e_sink, t_sum, o_sum, summed, inverted, y_done = [
            [st.sem(f"{n}{i}") for i in range(2)] for n in
            "landed s_sum masked cmax lowered m_done e_loc e_ctx e_sink t_sum o_sum summed inverted y_done".split()]

        with nc.Block() as block:
            @block.sync
            def _(sp):
                sp.dma_start(keys[:], swk).then_inc(s["set_in"], 16)
                sp.dma_start(vc[:], proj[R0 + 1:R0 + 1 + CTX, S_V:S_V + P].rearrange("(b p) n -> p b n", p=P)).then_inc(s["set_in"], 16)
                sp.dma_start(sink[:], sinks[layer]).then_inc(s["set_in"], 16)
                sp.wait_ge(s["zeroed"], 2)

                def load(u, t, row):
                    for p in range(2):
                        r = slice(64 * p, 64 * p + 64)
                        sp.dma_start(qz[u][r, p], swq[bass.ds(t, 1)].rearrange("a p c n -> (a p) c n")[r]).then_inc(landed[u], 16)
                    sp.dma_start(mask[u][:], win[bass.ds(t, 1)].rearrange("a p n -> (a p) n")).then_inc(landed[u], 16)
                    sp.dma_start(vw[u][:], proj[bass.ds(row - P, 3 * P), S_V:S_V + P].rearrange("(b p) n -> p b n", p=P)).then_inc(landed[u], 16)

                for u in range(2):
                    with sp.Fori(t0 + u, t0 + u + 1) as t:
                        load(u, t, t * P + (row_of(t0) - t0 * P))
                with sp.Fori(1, NT // 2) as n:
                    for u in range(2):
                        for q in o_sum:
                            sp.wait_ge(q, (n * 2 + u - 1) * 4)
                            settle(sp, s["sp_passed"])
                        load(u, n * 2 + (u + t0), n * (2 * P) + ((u + t0) * P + row_of(2) - 2 * P))

            @block.gpsimd
            def _(pool):
                for u in range(2):
                    pool.memset(qz[u][:], 0.0).then_inc(s["zeroed"], 1)

            def at(n, g):
                u, h = g // SH, g % SH
                return u, h, n * 2 + u, g % 2, n * SH + g // 2

            G = 2 * SH

            def ahead(step, eng, n, g, last, by=2):
                if g + by < G:
                    step(eng, n, g + by)
                elif not last:
                    step(eng, n + 1, g + by - G)

            def turns(eng, step, turn, by=2):
                with eng.Fori(0, 1) as n:
                    for g in range(by):
                        step(eng, n, g)
                with eng.Fori(0, NT // 2 - 1) as n:
                    turn(n, False)
                with eng.Fori(NT // 2 - 1, NT // 2) as n:
                    turn(n, True)

            def scores(pe, n, g):
                u, h, T, i, use = at(n, g)
                if h == 0:
                    pe.wait_ge(landed[u], n * 64 + 64)
                pe.wait_ge(masked[i], use)
                pe.wait_ge(e_ctx[i], use)
                q = qz[u][:, h // 4, h % 4, :]
                pe.matmul(b_l[i][:, 0:3 * P], q, keys[:, bass.ds(T * P + t0 * P, 3 * P)], start=True, stop=True)
                pe.matmul(b_c[i][:, 0:CTX], q, keys[:, P:P + CTX], start=True, stop=True).then_inc(s_sum[i], 1)

            def turn(pe, n, g):
                u, h, T, i, use = at(n, g)
                pe.wait_ge(e_loc[i], use + 1)
                pe.wait_ge(e_ctx[i], use + 1)
                pe.wait_ge(s["t0_out"], T * 8 + h)
                pe.wait_ge(s["t1_out"], T * 8 + h)
                if g in (0, SH + 1):
                    pe.wait_ge(s["y_split"], T)
                for b in range(5):
                    bank = b_t0[:, b * P:(b + 1) * P] if b < 3 else b_t1[:, (b - 3) * P:(b - 2) * P]
                    mm = pe.transpose(bank, prob[i][:, b * P:(b + 1) * P], mats[:, C_ID, :])
                mm.then_inc(t_sum[i], 1)

            def attend(pe, n, g):
                u, h, T, i, use = at(n, g)
                pe.wait_ge(s["t0_out"], T * 8 + h + 1)
                pe.wait_ge(s["t1_out"], T * 8 + h + 1)
                pe.wait_ge(y_done[i], use)
                for b in range(5):
                    v = vw[u][:, b, :] if b < 3 else vc[:, b - 3, :]
                    mm = pe.matmul(b_o[i][:, 0:P], probT[i][:, b, :], v, start=(b == 0), stop=(b == 4))
                mm.then_inc(o_sum[i], 1)

            def turn_output(pe, n, u):
                T = n * 2 + u
                for i in range(2):
                    pe.wait_ge(y_done[i], T * 4 + 4)
                pe.wait_ge(s["t0_out"], T * 8 + 8 + (1 if u == 0 else 0))
                for c in range(4):
                    mm = pe.transpose(b_t0[:, c * P:(c + 1) * P], yt[:, c * P:(c + 1) * P], mats[:, C_ID, :])
                mm.then_inc(s["y_turned"], 1)

            @block.tensor
            def _(pe):
                pe.wait_ge(s["set_in"], 48)

                def one(n, last):
                    for g in range(G):
                        turn(pe, n, g)
                        ahead(scores, pe, n, g, last)
                        if g == SH:
                            turn_output(pe, n, 0)
                        attend(pe, n, g)
                    turn_output(pe, n, 1)

                turns(pe, scores, one)

            def maximum(dve, n, g):
                u, h, T, i, use = at(n, g)
                if h == 0:
                    dve.wait_ge(landed[u], n * 64 + 64)
                dve.wait_ge(s_sum[i], use + 1)
                dve.wait_ge(t_sum[i], use)
                dve.wait_ge(lowered[i], use)
                settle(dve, s["dve_passed"])
                dve.tensor_tensor_reduce(prob[i][:, 0:3 * P], b_l[i][:, 0:3 * P], mask[u][:], 1.0, NEG, ALU.add, ALU.max,
                                         mx[i][:, 0:1]).then_inc(masked[i], 1)
                dve.tensor_reduce(mx[i][:, 1:2], b_c[i][:, 0:CTX], AX.X, ALU.max).then_inc(cmax[i], 1)
                dve.wait_ge(masked[i], use + 1)
                dve.wait_ge(cmax[i], use + 1)
                dve.wait_ge(m_done[i], use)
                dve.tensor_tensor(low[i][:], mx[i][:, 0:1], mx[i][:, 1:2], ALU.max).then_inc(lowered[i], 1)
                dve.wait_ge(lowered[i], use + 1)
                dve.wait_ge(e_sink[i], use)
                dve.tensor_scalar(nmax[i][:], low[i][:], sink[:, h:h + 1], -1.0, ALU.max, ALU.mult).then_inc(m_done[i], 1)

            def weigh(dve, n, g):
                u, h, T, i, use = at(n, g)
                dve.wait_ge(o_sum[i], use + 1)
                dve.wait_ge(inverted[i], use + 1)
                if h == 0:
                    dve.wait_ge(s["y_turned"], T)
                e = slice(64 * (h // 4), 64 * (h // 4) + 64)
                dve.tensor_scalar(yt[:, h * 64:h * 64 + 64], b_o[i][:, e], rden[i][:], None, ALU.mult).then_inc(y_done[i], 1)

            def split_output(dve, n, u):
                T = n * 2 + u
                tok = bass.ds(T * P + t0 * P, P)
                dve.wait_ge(s["y_rounded"], T + 1)
                dve.tensor_tensor(y_lo[:, 2:6, tok], b_t0[:].rearrange("p (c n) -> p c n", c=4), y_hi[:, 2:6, tok].bitcast(F32),
                                  ALU.subtract).then_inc(s["y_split"], 1)

            @block.vector
            def _(dve):
                dve.wait_ge(s["set_in"], 48)

                def one(n, last):
                    for g in range(G):
                        u, h, T, i, use = at(n, g)
                        if g:
                            weigh(dve, n, g - 1)
                        dve.wait_ge(t_sum[i], use + 1)
                        dve.wait_ge(o_sum[i], use)
                        dve.tensor_copy(probT[i][:, 3:5, :].rearrange("p a n -> p (a n)"), b_t1[:, 0:2 * P]).then_inc(s["t1_out"], 1)
                        dve.wait_ge(e_sink[i], use + 1)
                        dve.wait_ge(inverted[i], use)
                        dve.scalar_tensor_tensor(den[i][:], part[i][:, 0:1], part[i][:, 1:2], part[i][:, 2:3], ALU.add, ALU.add).then_inc(summed[i], 1)
                        dve.wait_ge(summed[i], use + 1)
                        dve.wait_ge(y_done[i], use)
                        dve.reciprocal(rden[i][:], den[i][:]).then_inc(inverted[i], 1)
                        if g == SH:
                            split_output(dve, n, 0)
                        ahead(maximum, dve, n, g, last)
                    weigh(dve, n, G - 1)
                    split_output(dve, n, 1)

                turns(dve, maximum, one)

            def exponentials(act, n, g):
                u, h, T, i, use = at(n, g)
                act.wait_ge(m_done[i], use + 1)
                act.wait_ge(summed[i], use)
                act.activation(prob[i][:, 0:3 * P], prob[i][:, 0:3 * P], ACT.Exp, bias=nmax[i][:], accum_out=part[i][:, 0:1]).then_inc(e_loc[i], 1)
                act.activation(prob[i][:, 3 * P:K], b_c[i][:, 0:CTX], ACT.Exp, bias=nmax[i][:], accum_out=part[i][:, 1:2]).then_inc(e_ctx[i], 1)
                act.activation(part[i][:, 2:3], sink[:, h:h + 1], ACT.Exp, bias=nmax[i][:]).then_inc(e_sink[i], 1)

            def round_output(act, n, u):
                T = n * 2 + u
                tok = bass.ds(T * P + t0 * P, P)
                act.wait_ge(s["y_turned"], T + 1)
                act.activation(y_hi[:, 2:6, tok], b_t0[:].rearrange("p (c n) -> p c n", c=4), ACT.Copy).then_inc(s["y_rounded"], 1)

            @block.scalar
            def _(act):
                def one(n, last):
                    for g in range(G):
                        u, h, T, i, use = at(n, g)
                        act.wait_ge(t_sum[i], use + 1)
                        act.wait_ge(o_sum[i], use)
                        act.activation(probT[i][:, 0:3, :].rearrange("p a n -> p (a n)"), b_t0[:, 0:3 * P], ACT.Copy).then_inc(s["t0_out"], 1)
                        if g == SH:
                            round_output(act, n, 0)
                        ahead(exponentials, act, n, g, last, 1)
                    round_output(act, n, 1)

                turns(act, exponentials, one, 1)


def gated(nc, layer, t0, proj, norm_w, mats, o_ret, o_gdn, y_hi, y_lo, eps):
    NG = (TILES - t0) // 2
    W = 2 * P
    with Stage(nc, f"gate{layer}") as st:
        gin = [st.sb(f"gin{u}", [P, 2, 512]) for u in range(2)]
        nw = st.sb("nw", [P, 4])
        mean = st.sb("mean", [P, P])
        os_, sq, sg, logs, root, y1, yf = (st.sb(n, [P, 4, W]) for n in ("os", "sq", "sg", "logs", "root", "y1", "yf"))
        b_g, b_m = [[st.ps(f"b_{n}{i}", [P, 512]) for i in range(2)] for n in "gm"]
        s = signals(st, "set_in mean0 mean1 in0 in1 added squared turned silued summed logged rooted normed gated rounded split sp_passed")
        ins = (s["in0"], s["in1"])
        with nc.Block() as block:
            @block.sync
            def _(sp):
                sp.dma_start(nw[:], norm_w[layer]).then_inc(s["set_in"], 16)

                for g in range(NG):
                    if g >= 2:
                        sp.wait_ge(s["turned"], g - 1)
                    row = row_of(t0 + 2 * g)
                    for half, col in ((0, R_G), (1, G_Z)):
                        sp.dma_start(gin[g % 2][:, :, 256 * half:256 * half + 256],
                                     proj[row:row + W, col:col + 256].rearrange("(b p) n -> p b n", p=P)).then_inc(ins[g % 2], 16)

            @block.gpsimd
            def _(pool):
                pool.memset(mean[:], 0.0).then_inc(s["mean0"], 1)
                pool.wait_ge(s["mean0"], 1)
                for p in range(2):
                    r = slice(64 * p, 64 * p + 64)
                    pool.memset(mean[r, r], 1.0 / HD).then_inc(s["mean1"], 1)
                pool.wait_ge(s["mean1"], 2)
                with pool.Fori(0, NG) as g:
                    tok = bass.ds(g * W + t0 * P, W)
                    pool.wait_ge(s["normed"], g)
                    pool.wait_ge(s["squared"], g)
                    pool.tensor_tensor(os_[:, 0:2, :], o_ret[:, 0, :, tok], o_ret[:, 1, :, tok], ALU.add).then_inc(s["added"], 1)
                    pool.tensor_tensor(os_[:, 2:4, :], o_gdn[:, 0, :, tok], o_gdn[:, 1, :, tok], ALU.add).then_inc(s["added"], 1)

            @block.tensor
            def _(pe):
                pe.wait_ge(s["mean1"], 2)
                for g in range(NG):
                    pe.wait_ge(ins[g % 2], (g // 2 + 1) * 32)
                    if g:
                        pe.wait_ge(s["silued"], 2 * g)
                    for c in range(4):
                        for b in range(2):
                            at = (c % 2) * W + b * P
                            mm = pe.transpose(b_g[c // 2][:, at:at + P], gin[g % 2][:, b, c * P:(c + 1) * P], mats[:, C_ID, :])
                    mm.then_inc(s["turned"], 1)
                    pe.wait_ge(s["squared"], g + 1)
                    if g:
                        pe.wait_ge(s["logged"], 2 * g)
                    for i in range(2):
                        mm = pe.matmul(b_m[i][:], mean[:], sq[:, 2 * i:2 * i + 2, :].rearrange("p c n -> p (c n)"), start=True, stop=True)
                    mm.then_inc(s["summed"], 1)

            flat = lambda b, i: b[:, 2 * i:2 * i + 2, :].rearrange("p c n -> p (c n)")

            @block.scalar
            def _(act):
                with act.Fori(0, NG) as g:
                    tok = bass.ds(g * W + t0 * P, W)
                    act.wait_ge(s["added"], g * 2 + 2)
                    act.wait_ge(s["summed"], g)
                    act.activation(sq[:], os_[:], ACT.Square).then_inc(s["squared"], 1)
                    act.wait_ge(s["summed"], g + 1)
                    act.wait_ge(s["normed"], g)
                    for i in range(2):
                        act.activation(flat(logs, i), b_m[i][:], ACT.Ln, bias=eps[:]).then_inc(s["logged"], 1)
                    act.wait_ge(s["logged"], g * 2 + 2)
                    act.activation(root[:], logs[:], ACT.Exp, scale=-0.5).then_inc(s["rooted"], 1)
                    act.wait_ge(s["turned"], g + 1)
                    act.wait_ge(s["gated"], g * 4)
                    for i in range(2):
                        act.activation(flat(sg, i), b_g[i][:], ACT.Silu).then_inc(s["silued"], 1)
                    act.wait_ge(s["gated"], g * 4 + 4)
                    for i, c in ((0, 0), (1, 6)):
                        act.activation(y_hi[:, c:c + 2, tok], yf[:, 2 * i:2 * i + 2, :], ACT.Copy).then_inc(s["rounded"], 1)

            @block.vector
            def _(dve):
                dve.wait_ge(s["set_in"], 16)
                with dve.Fori(0, NG) as g:
                    tok = bass.ds(g * W + t0 * P, W)
                    dve.wait_ge(s["rooted"], g + 1)
                    dve.wait_ge(s["gated"], g * 4)
                    dve.tensor_tensor(y1[:], os_[:], root[:], ALU.mult).then_inc(s["normed"], 1)
                    dve.wait_ge(s["normed"], g + 1)
                    dve.wait_ge(s["silued"], g * 2 + 2)
                    dve.wait_ge(s["split"], g * 2)
                    for c in range(4):
                        dve.scalar_tensor_tensor(yf[:, c, :], y1[:, c, :], nw[:, c:c + 1], sg[:, c, :], ALU.mult, ALU.mult).then_inc(s["gated"], 1)
                    dve.wait_ge(s["rounded"], g * 2 + 2)
                    for i, c in ((0, 0), (1, 6)):
                        dve.tensor_tensor(y_lo[:, c:c + 2, tok], yf[:, 2 * i:2 * i + 2, :], y_hi[:, c:c + 2, tok].bitcast(F32),
                                          ALU.subtract).then_inc(s["split"], 1)


def mixed(nc, layer, lo, x, units, mod, y_hi, y_lo):
    slices = token_slices(lo)
    NS, TURNS = len(slices), KC // 2
    with Stage(nc, f"mix{layer}") as st:
        w = WeightUnits(st, units)
        bank = [[st.ps(f"bank{u}{s}", [P, 512]) for s in range(NS)] for u in range(2)]
        full = [[st.sem(f"full{u}{s}") for s in range(NS)] for u in range(2)]
        free = [[st.sem(f"free{u}{s}") for s in range(NS)] for u in range(2)]
        with nc.Block() as block:
            @block.sync
            def _(sp):
                w.load_all(sp, TURNS)

            @block.scalar
            def _(act):
                with act.Fori(0, TURNS) as n:
                    for u in range(2):
                        w.round(act, u, n)

            @block.tensor
            def _(pe):
                with pe.Fori(0, TURNS) as n:
                    for u in range(2):
                        pe.wait_ge(w.ready[u], n + 1)
                        for s, (t0, ln) in enumerate(slices):
                            pe.wait_ge(free[u][s], n)
                            for k in range(KC):
                                f = slice(k * P, (k + 1) * P)
                                mm = three_passes(pe, bank[u][s][:, 0:ln], w.hi[u][:, f], w.lo[u][:, f],
                                                  y_hi[:, k, t0:t0 + ln], y_lo[:, k, t0:t0 + ln], k == 0, k == KC - 1,
                                                  w.used[1 - u] if s == 0 and k == 0 else None)
                            mm.then_inc(full[u][s], 1)

            @block.vector
            def _(dve):
                def add(n, u):
                    for s, (t0, ln) in enumerate(slices):
                        v = 1 if t0 < CTX else 0
                        dve.wait_ge(full[u][s], n + 1)
                        xs = x[:, bass.ds(n * 2 + u, 1), t0:t0 + ln].rearrange("p a n -> p (a n)")
                        dve.scalar_tensor_tensor(xs, bank[u][s][:, 0:ln], mod[:, bass.ds(n * 2 + (u + 2 * KC), 1), v], xs,
                                                 ALU.mult, ALU.add).then_inc(free[u][s], 1)

                for u in range(2):
                    w.rest(dve, u, 0)
                with dve.Fori(0, TURNS - 1) as n:
                    for u in range(2):
                        add(n, u)
                        w.rest(dve, u, n + 1)
                with dve.Fori(TURNS - 1, TURNS) as n:
                    for u in range(2):
                        add(n, u)


def final(nc, x, norm_w, out, ones, eps):
    with Stage(nc, "fin") as st:
        nw = st.sb("nw", [P, KC])
        sq = [st.sb(f"sq{i}", [P, 512]) for i in range(2)]
        root, inv = st.sb("root", [P, 512]), [st.sb(f"inv{i}", [P, 512]) for i in range(2)]
        y = st.sb("y", [P, KC, LAT])
        ms = [st.ps(f"ms{s}", [P, 512]) for s in range(2)]
        s = signals(st, "set_in squared summed rooted inverted done stored")
        with nc.Block() as block:
            @block.sync
            def _(sp):
                sp.dma_start(nw[:], norm_w).then_inc(s["set_in"], 16)
                for i in range(2 * KC):
                    sp.wait_ge(s["done"], i + 1)
                    at = slice((i // KC) * 512, (i // KC) * 512 + 512)
                    sp.dma_start(out[:, i % KC, at], y[:, i % KC, at]).then_inc(s["stored"], 16)
                sp.wait_ge(s["stored"], 2 * KC * 16)

            @block.scalar
            def _(act):
                for sl in range(2):
                    t = CTX + 512 * sl
                    for k in range(KC):
                        i = sl * KC + k
                        if i >= 2:
                            act.wait_ge(s["summed"], i - 1)
                        act.activation(sq[i % 2][:], x[:, k, t:t + 512], ACT.Square).then_inc(s["squared"], 1)
                    act.wait_ge(s["summed"], (sl + 1) * KC)
                    if sl:
                        act.wait_ge(s["inverted"], 1)
                    act.activation(root[:], ms[sl][:], ACT.Sqrt, bias=eps[:]).then_inc(s["rooted"], 1)

            @block.tensor
            def _(pe):
                for i in range(2 * KC):
                    pe.wait_ge(s["squared"], i + 1)
                    pe.matmul(ms[i // KC][:], ones[:], sq[i % 2][:], start=(i % KC == 0), stop=(i % KC == KC - 1)).then_inc(s["summed"], 1)

            @block.vector
            def _(dve):
                dve.wait_ge(s["set_in"], 16)
                for sl in range(2):
                    t = CTX + 512 * sl
                    dve.wait_ge(s["rooted"], sl + 1)
                    dve.reciprocal(inv[sl][:], root[:]).then_inc(s["inverted"], 1)
                    dve.wait_ge(s["inverted"], sl + 1)
                    for k in range(KC):
                        dve.scalar_tensor_tensor(y[:, k, sl * 512:sl * 512 + 512], x[:, k, t:t + 512], nw[:, k:k + 1], inv[sl][:],
                                                 ALU.mult, ALU.mult).then_inc(s["done"], 1)


def begin(nc, loads, zeros, fills):
    with Stage(nc, "begin") as st:
        zero = st.sb("zero", [P, G_Z - S_V])
        loaded, zeroed, filled, stored = (st.sem(n) for n in ("loaded", "zeroed", "filled", "stored"))
        with nc.Block() as block:
            @block.sync
            def _(sp):
                for dst, src in loads:
                    sp.dma_start(dst, src).then_inc(loaded, 16)
                sp.wait_ge(zeroed, 1)
                for dst in zeros:
                    sp.dma_start(dst, zero[0:dst.shape[0], 0:dst.shape[1]]).then_inc(stored, 16)
                sp.wait_ge(stored, 16 * len(zeros))
                sp.wait_ge(loaded, 16 * len(loads))

            @block.vector
            def _(dve):
                dve.memset(zero[:], 0.0).then_inc(zeroed, 1)
                for dst, value in fills:
                    dve.memset(dst, value).then_inc(filled, 1)
                dve.wait_ge(filled, len(fills))


def program(nc, x_in, cs, ada_w, ada_b, norm_mix, norm_ffn, w_in, small, sinks, conv_w, mix_norm, w_out, w_ffn,
            final_norm, mats_in, tri_in, ksteps_in, qsteps_in, rope, win, out):
    scratch = lambda name, shape: nc.dram_tensor(name, shape, F32, kind="Internal").ap()
    proj = scratch("proj", (ROWS, IN_W))
    pack = scratch("pack", (TILES, P, T_W))
    feat = scratch("feat", (TILES, P, F_N, P))
    diag = scratch("diag", (2, 4 * TILES, GH, 32, 32))
    inv = scratch("inv", (4 * TILES, GH, 4, 32, 32))
    tot = scratch("tot", (TILES, P, 16))
    swq = scratch("swq", (TILES, P, 4, P))
    swk = scratch("swk", (P, TOK + 2 * P))
    us = scratch("us", (TILES, P, 512))
    with ExitStack() as mem:
        def sb(name, shape):
            return mem.enter_context(nc.sbuf_tensor(name, shape, F32))

        x = sb("x", [P, KC, TOK])
        mats, tri, ksteps, qsteps = sb("mats", [P, 8, P]), sb("tri", [P, 2, HD]), sb("ksteps", [P, 2]), sb("qsteps", [P, 2, P])
        ones, eps = sb("ones", [P, P]), sb("eps", [P, 1])
        mods = [(sb(f"mod{l}", [P, NMOD * KC, 2]), sb(f"amix{l}", [P, KC, 2]), sb(f"affn{l}", [P, KC, 2])) for l in range(DEPTH)]
        pads = [(0, P), (P, P + 1), (R0 + 1 + CTX, R0 + 2 + CTX), (ROWS - P - 1, ROWS - 1), (ROWS - 1, ROWS)]
        begin(nc, [(x[:], x_in), (mats[:], mats_in), (tri[:], tri_in), (ksteps[:], ksteps_in), (qsteps[:], qsteps_in)],
              [proj[a:b, S_V:G_Z] for a, b in pads] + [swk[:, 0:P], swk[:, TOK + P:TOK + 2 * P]],
              [(ones[:], 1.0 / DM), (eps[:], EPS)])
        for layer in range(DEPTH):
            lo = 0 if layer < DEPTH - 1 else CTX
            t0 = lo // P
            mod, amix, affn = mods[layer]
            if layer == 0:
                modulation(nc, [mix_part(0)], cs, ada_w, ada_b, (norm_mix, norm_ffn), mats[:, C_ID, :], mods)
            project(nc, layer, x, w_in, proj, mod, amix, ones, eps)
            prepare(nc, layer, proj, rope, conv_w, small, mats, tri, ksteps, qsteps, pack, feat, diag, tot, swq, swk)
            parts = [rest_part(layer)] + ([mix_part(layer + 1)] if layer + 1 < DEPTH else [])
            solve(nc, layer, diag, inv, lambda st: modulating(nc, st, parts, cs, ada_w, ada_b, (norm_mix, norm_ffn), mats[:, C_ID, :], mods))
            join(nc, layer, pack, inv, feat, us)
            with Stage(nc, f"o{layer}") as so:
                o_ret, o_gdn = so.sb("o_ret", [P, 2, 2, TOK]), so.sb("o_gdn", [P, 2, 2, TOK])
                scan(nc, layer, pack, feat, tot, us, small, mats, o_ret, o_gdn)
                y_hi, y_lo = so.sb("y_hi", [P, KC, TOK], F32R), so.sb("y_lo", [P, KC, TOK], F32R)
                gated(nc, layer, t0, proj, mix_norm, mats, o_ret, o_gdn, y_hi, y_lo, eps)
                window(nc, layer, t0, proj, swq, swk, win, sinks, mats, y_hi, y_lo)
                mixed(nc, layer, lo, x, w_out[layer], mod, y_hi, y_lo)
            ffn(nc, layer, x, lo, w_ffn[layer], mod, affn, ones, eps)
        final(nc, x, final_norm, out, ones, eps)


def ffn_units(w1, w2):
    units = []
    for j0 in range(0, FC, 4):
        js = min(4, FC - j0)
        for j in range(j0, j0 + js):
            for half in range(2):
                c = w1[:, half * DFF + j * P:half * DFF + (j + 1) * P]
                units.append(c.reshape(KC, P, P).transpose(1, 0, 2).reshape(P, DM))
        wide = DM // js
        rows = w2[j0 * P:(j0 + js) * P].reshape(js, P, DM)
        for m in range(0, DM, wide):
            units.append(rows[:, :, m:m + wide].transpose(1, 0, 2).reshape(P, DM))
    return np.stack(units)


def kernel(**inputs):
    import concourse.bacc as bacc
    from concourse.bass_utils import run_bass_kernel_spmd

    a = {k: np.asarray(v) for k, v in inputs.items()}
    feature = lambda v: np.ascontiguousarray(v.reshape(-1, P).T)
    spread = lambda v: np.broadcast_to(v.reshape(1, -1), (P, v.size))
    mats, tri, ksteps, qsteps, rope, win = constants()
    tokens = np.concatenate([a["ctx"][0], a["x"][0]], 0)
    arrays = {
        "x_in": tokens.T.reshape(KC, P, TOK).transpose(1, 0, 2),
        "cs": np.stack([feature(a["c"][0]), feature(a["c_ctx"])], -1),
        "ada_w": a["ada_w"],
        "ada_b": np.stack([feature(v) for v in a["ada_b"]]),
        "norm_mix": np.stack([feature(v) for v in a["norm_mix_w"]]),
        "norm_ffn": np.stack([feature(v) for v in a["norm_ffn_w"]]),
        "w_in": a["w_in"],
        "small": np.stack([np.stack([spread(a[n][l]) for n in ("gdn_a_log", "gdn_dt_bias", "ret_rate")], 1) for l in range(DEPTH)]),
        "sinks": np.stack([spread(v) for v in a["swa_sinks"]]),
        "conv_w": np.broadcast_to(a["gdn_conv_w"][:, None], (DEPTH, P, 3, 768)),
        "mix_norm": np.stack([np.concatenate([feature(a["ret_norm_w"][l]), feature(np.tile(a["gdn_norm_w"][l], 4))], 1) for l in range(DEPTH)]),
        "w_out": a["w_out"].reshape(DEPTH, KC, P, KC, P).transpose(0, 3, 2, 1, 4).reshape(DEPTH, KC, P, DM),
        "w_ffn": np.stack([ffn_units(a["w_ffn_in"][l], a["w_ffn_out"][l]) for l in range(DEPTH)]),
        "final_norm": feature(a["final_norm_w"]),
        "mats_in": mats, "tri_in": tri, "ksteps_in": ksteps, "qsteps_in": qsteps, "rope": rope, "win": win,
    }
    arrays = {k: np.ascontiguousarray(v) for k, v in arrays.items()}
    nc = bacc.Bacc("TRN2", target_bir_lowering=False, num_devices=1)
    args = [nc.dram_tensor(k, v.shape, mybir.dt.from_np(v.dtype), kind="ExternalInput").ap() for k, v in arrays.items()]
    args.append(nc.dram_tensor("out", (P, KC, LAT), F32, kind="ExternalOutput").ap())
    program(nc, *args)
    r = run_bass_kernel_spmd(nc, [arrays], core_ids=[0])
    out = r.results[0]["out"]
    return np.ascontiguousarray(out.transpose(1, 0, 2).reshape(DM, LAT).T)[None]
```
